# Optimizing a Trainium2 kernel written in Bass

```python
import math
import jax, jax.numpy as jnp
from jax import lax
import numpy as np

D_MODEL = 1024
BATCH = 1
SEQ = 512
DEPTH = 2

HEAD_DIM = 64
N_HEADS = D_MODEL // HEAD_DIM
N_KV = 4
HPG = N_HEADS // N_KV
Q_WIDTH = N_HEADS * HEAD_DIM
KV_WIDTH = N_KV * HEAD_DIM
CMP_LEN = 32
CMP_STRIDE = 16
CMP_HIDDEN = 256
SLC_LEN = 64
N_SELECT = 16
NSA_WINDOW = 512
NSA_QBLK = 64
NSA_IN = Q_WIDTH + 6 * KV_WIDTH + 3 * N_HEADS
NSA_SPLITS = (Q_WIDTH, Q_WIDTH + KV_WIDTH, Q_WIDTH + 2 * KV_WIDTH, Q_WIDTH + 3 * KV_WIDTH,
              Q_WIDTH + 4 * KV_WIDTH, Q_WIDTH + 5 * KV_WIDTH, Q_WIDTH + 6 * KV_WIDTH)
SWA_WINDOW = 128
SWA_QBLK = 128
N_BUCKETS = 32
MAX_DISTANCE = 128
N_EXPERTS = 16
N_GROUPS = 4
EXPERTS_PER_GROUP = N_EXPERTS // N_GROUPS
TOP_K = 2
D_EXPERT = 256
N_A_LAYERS = max(1, DEPTH // 2)
N_B_LAYERS = DEPTH - N_A_LAYERS
ALPHA = (2.0 * DEPTH) ** 0.25
BETA = (8.0 * DEPTH) ** -0.25
LN_EPS = 1e-5
NEG = -1e30
ATTN_SCALE = HEAD_DIM ** -0.5

kernel_name = 'nsa_swa_sink_yoco_grouped_moe'

def layer_norm(x, g, b):
    xf = x.astype(jnp.float32)
    mu = xf.mean(-1, keepdims=True)
    var = jnp.mean(jnp.square(xf - mu), -1, keepdims=True)
    return ((xf - mu) * lax.rsqrt(var + LN_EPS) * g.astype(jnp.float32)
            + b.astype(jnp.float32)).astype(x.dtype)

def modulate(x, shift, scale):
    return x * (1.0 + scale[:, None, :]) + shift[:, None, :]

def rel_bucket(dist):
    max_exact = N_BUCKETS // 2
    d = jnp.maximum(dist, 0)
    large = max_exact + (jnp.log(jnp.maximum(d, 1).astype(jnp.float32) / max_exact)
                         / math.log(MAX_DISTANCE / max_exact)
                         * (N_BUCKETS - max_exact)).astype(jnp.int32)
    large = jnp.minimum(large, N_BUCKETS - 1)
    return jnp.where(d < max_exact, d, large)

def masked_softmax(logits, valid):
    p = jax.nn.softmax(jnp.where(valid, logits, NEG), axis=-1)
    return jnp.where(valid, p, 0.0)

def compress_blocks(k, pos, w1, w2):
    B, G, S, dk = k.shape
    chunks = k.reshape(B, G, S // CMP_STRIDE, CMP_STRIDE, dk)
    blocks = jnp.concatenate([chunks[:, :, :-1], chunks[:, :, 1:]], axis=3) + pos
    blocks = blocks.reshape(B, G, S // CMP_STRIDE - 1, CMP_LEN * dk)
    return jax.nn.gelu(blocks @ w1) @ w2

def band_bias(rel_table, qblk, window):
    n_k = qblk + window
    dist = jnp.arange(qblk)[:, None] + window - jnp.arange(n_k)[None, :]
    band = (dist >= 0) & (dist < window)
    bias = rel_table[rel_bucket(dist)].astype(jnp.float32)
    bias = bias.reshape(qblk, n_k, N_KV, HPG).transpose(2, 3, 0, 1)
    return dist, band, bias

def nsa_mixer(h, w_in, k_w1, k_w2, v_w1, v_w2, k_pos, v_pos, w_out, rel_table):
    B, S, _ = h.shape
    G, J, dk = N_KV, HPG, HEAD_DIM
    proj = h @ w_in
    q, kc, vc, ksl, vsl, kw, vw, gl = jnp.split(proj, NSA_SPLITS, axis=-1)
    q = q.reshape(B, S, G, J, dk).transpose(0, 2, 3, 1, 4)
    to_kv = lambda t: t.reshape(B, S, G, dk).transpose(0, 2, 1, 3)
    kc, vc, ksl, vsl, kw, vw = [to_kv(t) for t in (kc, vc, ksl, vsl, kw, vw)]
    gates = jax.nn.sigmoid(gl.astype(jnp.float32)).reshape(B, S, 3, G, J).transpose(0, 3, 4, 1, 2)

    k_cmp = compress_blocks(kc, k_pos, k_w1, k_w2)
    v_cmp = compress_blocks(vc, v_pos, v_w1, v_w2)
    n_cmp = k_cmp.shape[2]
    cmp_end = jnp.arange(n_cmp) * CMP_STRIDE + CMP_LEN - 1
    n_slc = S // SLC_LEN
    n_sel = min(N_SELECT, n_slc)
    c_start = jnp.arange(n_cmp)[:, None] * CMP_STRIDE
    s_start = jnp.arange(n_slc)[None, :] * SLC_LEN
    overlap = ((c_start < s_start + SLC_LEN) & (c_start + CMP_LEN > s_start)).astype(jnp.float32)
    k_blk = ksl.reshape(B, G, n_slc, SLC_LEN, dk)
    v_blk = vsl.reshape(B, G, n_slc, SLC_LEN, dk)
    blk_off = jnp.arange(SLC_LEN)
    b_idx = jnp.arange(B)[:, None, None, None]
    g_idx = jnp.arange(G)[None, :, None, None]
    table_g = rel_table.astype(jnp.float32).reshape(N_BUCKETS, G, J).transpose(1, 0, 2)
    jblk = jnp.arange(n_slc)
    kw_pad = jnp.pad(kw, ((0, 0), (0, 0), (NSA_WINDOW, 0), (0, 0)))
    vw_pad = jnp.pad(vw, ((0, 0), (0, 0), (NSA_WINDOW, 0), (0, 0)))
    _, win_band, win_bias = band_bias(rel_table, NSA_QBLK, NSA_WINDOW)
    n_kw = NSA_QBLK + NSA_WINDOW

    def q_block(qb):
        s0 = qb * NSA_QBLK
        tq = s0 + jnp.arange(NSA_QBLK)
        qblk = lax.dynamic_slice_in_dim(q, s0, NSA_QBLK, axis=3)

        dist_c = tq[:, None] - cmp_end[None, :]
        bias_c = rel_table[rel_bucket(dist_c)].astype(jnp.float32)
        bias_c = bias_c.reshape(NSA_QBLK, n_cmp, G, J).transpose(2, 3, 0, 1)
        lg_c = jnp.einsum('bghqd,bgnd->bghqn', qblk, k_cmp).astype(jnp.float32) * ATTN_SCALE + bias_c
        p_c = masked_softmax(lg_c, dist_c >= 0)
        o_c = jnp.einsum('bghqn,bgnd->bghqd', p_c.astype(v_cmp.dtype), v_cmp)

        imp = jnp.einsum('bghqn,nj->bgqj', p_c, overlap)
        cur = (tq // SLC_LEN)[:, None]
        forced = (jblk[None, :] == 0) | (jblk[None, :] == cur) | (jblk[None, :] == cur - 1)
        future = jblk[None, :] > cur
        imp = jnp.where(forced, 1e9, jnp.where(future, -1e9, imp))
        _, idx = lax.top_k(imp, n_sel)
        n_ks = n_sel * SLC_LEN
        k_sel = k_blk[b_idx, g_idx, idx].reshape(B, G, NSA_QBLK, n_ks, dk)
        v_sel = v_blk[b_idx, g_idx, idx].reshape(B, G, NSA_QBLK, n_ks, dk)
        kpos_s = (idx[..., None] * SLC_LEN + blk_off).reshape(B, G, NSA_QBLK, n_ks)
        dist_s = tq[None, None, :, None] - kpos_s
        bias_s = table_g[g_idx, rel_bucket(dist_s)].transpose(0, 1, 4, 2, 3)
        lg_s = jnp.einsum('bghqd,bgqkd->bghqk', qblk, k_sel).astype(jnp.float32) * ATTN_SCALE + bias_s
        p_s = masked_softmax(lg_s, (dist_s >= 0)[:, :, None])
        o_s = jnp.einsum('bghqk,bgqkd->bghqd', p_s.astype(v_sel.dtype), v_sel)

        kb = lax.dynamic_slice_in_dim(kw_pad, s0, n_kw, axis=2)
        vb = lax.dynamic_slice_in_dim(vw_pad, s0, n_kw, axis=2)
        kpos_w = s0 - NSA_WINDOW + jnp.arange(n_kw)
        valid_w = win_band & (kpos_w >= 0)[None, :]
        lg_w = jnp.einsum('bghqd,bgkd->bghqk', qblk, kb).astype(jnp.float32) * ATTN_SCALE + win_bias
        p_w = masked_softmax(lg_w, valid_w)
        o_w = jnp.einsum('bghqk,bgkd->bghqd', p_w.astype(vb.dtype), vb)

        g = lax.dynamic_slice_in_dim(gates, s0, NSA_QBLK, axis=3).astype(o_c.dtype)
        return g[..., 0:1] * o_c + g[..., 1:2] * o_s + g[..., 2:3] * o_w

    o = lax.map(q_block, jnp.arange(S // NSA_QBLK))
    o = o.transpose(1, 0, 4, 2, 3, 5).reshape(B, S, Q_WIDTH)
    return o @ w_out

def swa_sink_mixer(h, w_q, k_sh, v_sh, sinks, w_out, rel_table):
    B, S, _ = h.shape
    G, J, dk = N_KV, HPG, HEAD_DIM
    q = (h @ w_q).reshape(B, S, G, J, dk).transpose(0, 2, 3, 1, 4)
    k_pad = jnp.pad(k_sh, ((0, 0), (0, 0), (SWA_WINDOW, 0), (0, 0)))
    v_pad = jnp.pad(v_sh, ((0, 0), (0, 0), (SWA_WINDOW, 0), (0, 0)))
    _, band, bias = band_bias(rel_table, SWA_QBLK, SWA_WINDOW)
    n_k = SWA_QBLK + SWA_WINDOW
    sink = jnp.broadcast_to(sinks.astype(jnp.float32).reshape(1, G, J, 1, 1), (B, G, J, SWA_QBLK, 1))

    def q_block(qb):
        s0 = qb * SWA_QBLK
        qblk = lax.dynamic_slice_in_dim(q, s0, SWA_QBLK, axis=3)
        kb = lax.dynamic_slice_in_dim(k_pad, s0, n_k, axis=2)
        vb = lax.dynamic_slice_in_dim(v_pad, s0, n_k, axis=2)
        kpos = s0 - SWA_WINDOW + jnp.arange(n_k)
        valid = band & (kpos >= 0)[None, :]
        lg = jnp.einsum('bghqd,bgkd->bghqk', qblk, kb).astype(jnp.float32) * ATTN_SCALE + bias
        lg = jnp.where(valid, lg, NEG)
        p = jax.nn.softmax(jnp.concatenate([lg, sink], axis=-1), axis=-1)[..., :-1]
        return jnp.einsum('bghqk,bgkd->bghqd', p.astype(vb.dtype), vb)

    o = lax.map(q_block, jnp.arange(S // SWA_QBLK))
    o = o.transpose(1, 0, 4, 2, 3, 5).reshape(B, S, Q_WIDTH)
    return o @ w_out

def grouped_moe(h, router_w, router_b, w_gate, w_up, w_down):
    B, S, D = h.shape
    T = B * S
    t = h.reshape(T, D)
    s = jax.nn.sigmoid((t @ router_w).astype(jnp.float32))
    sb = s + router_b.astype(jnp.float32)
    grp_score = lax.top_k(sb.reshape(T, N_GROUPS, EXPERTS_PER_GROUP), TOP_K)[0].sum(-1)
    grp = jnp.argmax(grp_score, axis=-1)
    in_grp = (jnp.arange(N_EXPERTS) // EXPERTS_PER_GROUP)[None, :] == grp[:, None]
    _, e_idx = lax.top_k(jnp.where(in_grp, sb, -jnp.inf), TOP_K)
    s_sel = jnp.take_along_axis(s, e_idx, axis=-1)
    w = s_sel / s_sel.sum(-1, keepdims=True)
    gates = jnp.einsum('tk,tke->te', w, jax.nn.one_hot(e_idx, N_EXPERTS, dtype=jnp.float32)).astype(t.dtype)
    out = jnp.zeros_like(t)
    for e in range(N_EXPERTS):
        he = jax.nn.silu(t @ w_gate[e]) * (t @ w_up[e])
        out = out + gates[:, e:e + 1] * (he @ w_down[e])
    return out.reshape(B, S, D)

def setup_inputs(seed: int = 0) -> dict:
    key = jax.random.key(seed)
    ks = jax.random.split(key, 24)
    D = D_MODEL
    nrm = lambda k, shape, s: jax.random.normal(k, shape, jnp.float32) * s
    return {
        'x': nrm(ks[0], (BATCH, SEQ, D), 1.0),
        'c': nrm(ks[1], (BATCH, D), 1.0),
        'nsa_w_in': nrm(ks[2], (N_A_LAYERS, D, NSA_IN), D ** -0.5),
        'cmp_k_w1': nrm(ks[3], (N_A_LAYERS, CMP_LEN * HEAD_DIM, CMP_HIDDEN), (CMP_LEN * HEAD_DIM) ** -0.5),
        'cmp_k_w2': nrm(ks[4], (N_A_LAYERS, CMP_HIDDEN, HEAD_DIM), CMP_HIDDEN ** -0.5),
        'cmp_v_w1': nrm(ks[5], (N_A_LAYERS, CMP_LEN * HEAD_DIM, CMP_HIDDEN), (CMP_LEN * HEAD_DIM) ** -0.5),
        'cmp_v_w2': nrm(ks[6], (N_A_LAYERS, CMP_HIDDEN, HEAD_DIM), CMP_HIDDEN ** -0.5),
        'cmp_k_pos': nrm(ks[7], (N_A_LAYERS, CMP_LEN, HEAD_DIM), 0.1),
        'cmp_v_pos': nrm(ks[8], (N_A_LAYERS, CMP_LEN, HEAD_DIM), 0.1),
        'nsa_w_out': nrm(ks[9], (N_A_LAYERS, Q_WIDTH, D), Q_WIDTH ** -0.5 * BETA),
        'swa_w_q': nrm(ks[10], (N_B_LAYERS, D, Q_WIDTH), D ** -0.5),
        'swa_sinks': nrm(ks[11], (N_B_LAYERS, N_HEADS), 0.5),
        'swa_w_out': nrm(ks[12], (N_B_LAYERS, Q_WIDTH, D), Q_WIDTH ** -0.5 * BETA),
        'shared_w_kv': nrm(ks[13], (D, 2 * KV_WIDTH), D ** -0.5),
        'rel_bias': nrm(ks[14], (N_BUCKETS, N_HEADS), 0.5),
        'router_w': nrm(ks[15], (D, N_EXPERTS), D ** -0.5),
        'router_b': nrm(ks[16], (N_EXPERTS,), 0.01),
        'moe_w_gate': nrm(ks[17], (DEPTH, N_EXPERTS, D, D_EXPERT), D ** -0.5),
        'moe_w_up': nrm(ks[18], (DEPTH, N_EXPERTS, D, D_EXPERT), D ** -0.5),
        'moe_w_down': nrm(ks[19], (DEPTH, N_EXPERTS, D_EXPERT, D), D_EXPERT ** -0.5 * BETA),
        'ada_w': nrm(ks[20], (DEPTH, D, 6 * D), 0.1 * D ** -0.5),
        'ada_b': nrm(ks[21], (DEPTH, 6 * D), 0.02),
        'ln_g': 1.0 + nrm(ks[22], (DEPTH, 2, D), 0.02),
        'ln_b': nrm(ks[23], (DEPTH, 2, D), 0.02),
    }

def reference(x, c, nsa_w_in, cmp_k_w1, cmp_k_w2, cmp_v_w1, cmp_v_w2, cmp_k_pos, cmp_v_pos,
              nsa_w_out, swa_w_q, swa_sinks, swa_w_out, shared_w_kv, rel_bias, router_w, router_b,
              moe_w_gate, moe_w_up, moe_w_down, ada_w, ada_b, ln_g, ln_b):
    B, S, _ = x.shape
    cond = jax.nn.silu(c)
    k_sh = None
    v_sh = None
    for layer in range(DEPTH):
        ada = cond @ ada_w[layer] + ada_b[layer]
        sh_a, sc_a, g_a, sh_f, sc_f, g_f = jnp.split(ada, 6, axis=-1)
        h = modulate(x, sh_a, sc_a)
        if layer < N_A_LAYERS:
            mix = nsa_mixer(h, nsa_w_in[layer], cmp_k_w1[layer], cmp_k_w2[layer], cmp_v_w1[layer],
                            cmp_v_w2[layer], cmp_k_pos[layer], cmp_v_pos[layer], nsa_w_out[layer], rel_bias)
        else:
            if layer == N_A_LAYERS:
                kv = (x @ shared_w_kv).reshape(B, S, 2, N_KV, HEAD_DIM).transpose(2, 0, 3, 1, 4)
                k_sh, v_sh = kv[0], kv[1]
            lb = layer - N_A_LAYERS
            mix = swa_sink_mixer(h, swa_w_q[lb], k_sh, v_sh, swa_sinks[lb], swa_w_out[lb], rel_bias)
        x = layer_norm(ALPHA * x + (1.0 + g_a)[:, None, :] * mix, ln_g[layer, 0], ln_b[layer, 0])
        h = modulate(x, sh_f, sc_f)
        ffn = grouped_moe(h, router_w, router_b, moe_w_gate[layer], moe_w_up[layer], moe_w_down[layer])
        x = layer_norm(ALPHA * x + (1.0 + g_f)[:, None, :] * ffn, ln_g[layer, 1], ln_b[layer, 1])
    return x


_drawn_inputs = setup_inputs


def setup_inputs(seed=0):
    import zlib

    import numpy as np

    out = dict(_drawn_inputs(seed))
    spreads = {}
    factors = {'cmp_k_pos': 14.961, 'swa_sinks': 8.0}
    for name, (base, spread) in spreads.items():
        noise = np.random.default_rng([zlib.crc32(name.encode()), seed]).standard_normal(out[name].shape)
        drawn = base * np.exp(spread * noise) if base else spread * noise
        out[name] = __import__('jax').numpy.asarray(drawn.astype(out[name].dtype))
    for name, factor in factors.items():
        out[name] = (out[name] * factor).astype(out[name].dtype)
    return out
```

```python
from contextlib import ExitStack

import concourse.bass as bass
import numpy as np
from concourse import mybir

F32 = mybir.dt.float32
U32 = mybir.dt.uint32
ALU = mybir.AluOpType
ACT = mybir.ActivationFunctionType
AX = mybir.AxisListType

P = 128
D = 1024
T = 512
KD = D // P
NT = T // P
NH, NG, HD = 16, 4, 64
HPG = NH // NG
QW, KVW = NH * HD, NG * HD
NSA_IN = QW + 6 * KVW + 3 * NH
CMP_LEN, CMP_STRIDE, CMP_HIDDEN = 32, 16, 256
NC = T // CMP_STRIDE - 1
NCP = NC + 1
CK = CMP_LEN * HD // P
N_EXP, D_EXP = 16, 256
EPG = 4
NE_GRP = N_EXP // EPG
BUCKETS, MAX_DIST = 32, 128
WINDOW = 128
ALPHA = 4.0 ** 0.25
LN_EPS = 1e-5
SCALE = HD ** -0.5
MASKED = 1e30
NOWHERE = 65536.0
PART = 2048
SLOT = 6144
RING = 3


def bucket_rows():
    def one_hot(dist, valid):
        d = np.maximum(dist, 0)
        half = BUCKETS // 2
        large = half + (np.log(np.maximum(d, 1).astype(np.float32) / np.float32(half))
                        / np.float32(np.log(MAX_DIST / half)) * np.float32(half)).astype(np.int32)
        b = np.where(d < half, d, np.minimum(large, BUCKETS - 1))
        b = np.where(valid, b, BUCKETS)
        return (np.arange(BUCKETS + 1)[:, None] == b[None, :]).astype(np.float32)

    back = T - 1 - np.arange(640)
    near = 2 * WINDOW - 1 - np.arange(384)
    ahead = np.arange(1024) - T
    return np.concatenate([one_hot(back, back >= 0), one_hot(near, (near >= 0) & (near < WINDOW)),
                           one_hot(ahead, ahead >= 0)], axis=1)


BACK, NEAR, AHEAD = 0, 640, 1024


class Steps:

    def __init__(self, eng, sem):
        self.eng, self.sem, self.n, self.extra = eng, sem, 0, None

    def mark(self, ins):
        ins.then_inc(self.sem, 1)
        self.n += 1

    def wait(self):
        self.eng.wait_ge(self.sem, self.n if self.extra is None else self.extra + self.n)

    def link(self, ins):
        self.mark(ins)
        self.wait()

    def enter(self, it, per):
        self.extra, self.n0, self.per = it * per, self.n, per

    def leave(self, rounds):
        assert self.n - self.n0 == self.per, (self.n - self.n0, self.per)
        self.extra, self.n = None, self.n0 + rounds * self.per


def build(nc, t):
    with ExitStack() as ctx:
        def sb(name, shape):
            return ctx.enter_context(nc.sbuf_tensor(name, shape, F32))

        def sem(name):
            return ctx.enter_context(nc.semaphore(name))

        X = sb("X", [P, NT, D])
        XT = sb("XT", [P, KD * T])
        HT = sb("HT", [P, KD, T])
        O = sb("O", [P, NT, D])
        ring = sb("ring", [P, RING, SLOT])
        KTV = sb("KTV", [P, SLOT])
        G = sb("G", [P, 2, 2, D])
        WORK = sb("WORK", [P, 6144])
        ident = sb("ident", [P, P])
        ones = sb("ones", [P, P])
        cond = sb("cond", [P, KD])
        adaC = sb("adaC", [P, 2, 4, KD])
        GT = sb("GT", [P, NT, 3 * NH])
        routw = sb("routw", [P, KD, N_EXP])
        routb = sb("routb", [P, N_EXP])
        KC = sb("KC", [HD, NG, NC])
        VC = sb("VC", [NCP, KVW])
        maskc = sb("maskc", [P, NT, NC])
        nsink = sb("nsink", [P, NH])
        sums = sb("sums", [P, 2, 8])
        mins = sb("mins", [P, 2, 8])
        small = sb("small", [P, 64])
        moeg = sb("moeg", [P, NT, N_EXP])
        stats = sb("stats", [P, NT, 2, 6])
        mv = sb("mv", [P, NT, 4])
        nhalf = sb("nhalf", [P, 1])
        relb = sb("relb", [BUCKETS + 1, NH])
        upper = sb("upper", [P, P])
        row = sb("row", [P, P])
        tcol = sb("tcol", [P, NT])
        slot_rows = ctx.enter_context(nc.sbuf_tensor("slot_rows", [P, 2, N_EXP], U32))
        many = ctx.enter_context(nc.sbuf_tensor("many", [P, 2], U32))
        more = small[:, 20:28]
        more_rows = ctx.enter_context(nc.sbuf_tensor("more_rows", [P, 2], U32))
        w2 = sb("w2", [P, 2, 2, HD])

        BC = XT[:, 0:NT * NC * NH].rearrange("p (i n h) -> p i n h", i=NT, n=NC)
        acc = XT[:, PART:2 * PART]
        PcT = XT[0:NCP, PART:PART + T]
        Pc = XT[:, PART + T:PART + T + P].rearrange("p (i n) -> p i n", i=NT)
        osc = XT[:, PART + 2 * T:PART + 3 * T].rearrange("p (u d) -> p u d", d=HD)
        XTk = XT[:, :].rearrange("p (k t) -> p k t", k=KD)
        OH = O[0:BUCKETS + 1, 0:2, :].rearrange("p a n -> p (a n)")
        KC2 = O[:, 2, :].rearrange("p (g u) -> p g u", g=NG)
        VC2 = O[:, 3, :].rearrange("p (g u) -> p g u", g=NG)
        KT = KTV[0:HD, 0:2 * NG * T].rearrange("p (b g t) -> p b g t", b=2, g=NG)
        V = KTV[:, 2 * NG * T:].rearrange("p (b i n) -> p b i n", b=2, i=NT)
        adab = WORK[0:1, 0:PART]
        logits = WORK[:, 0:1024].rearrange("p (b n) -> p b n", b=2)
        probs = WORK[:, 1024:2048].rearrange("p (b n) -> p b n", b=2)
        probsT = WORK[:, 2048:3072].rearrange("p (b n) -> p b n", b=2)
        QT = WORK[0:HD, 3072:5120].rearrange("p (h t) -> p h t", h=HPG)
        B = WORK[:, 5120:6144].rearrange("p (b n) -> p b n", b=2)
        glw = WORK[:, 3072:3072 + KD * 3 * NH].rearrange("p (k n) -> p k n", k=KD)
        posT = WORK[:, 3584:3584 + 2 * CK].rearrange("p (b k) -> p b k", b=2)
        posb = WORK[:, 3648:3648 + 4].rearrange("p (b m) -> p b m", b=2)
        hid = WORK[:, 4096:4096 + 4 * P].rearrange("p (b m n) -> p b m n", b=2, m=2)
        c8 = WORK[0:KD, 4608:4608 + P]
        pos16 = WORK[0:CK, 4736:4736 + 2 * P].rearrange("p (b n) -> p b n", b=2)
        biasrow = WORK[0:NH, 5120:6144]
        sink_now = small[:, 62:64]
        sink_diff = small[:, 0:8].rearrange("p (b i) -> p b i", b=2)
        sink_exp = small[:, 8:16].rearrange("p (b i) -> p b i", b=2)
        lng, lnb = XT[:, 0:D], XT[:, D:2 * D]
        lnx = XT[:, 2 * D:4 * D].rearrange("p (b n) -> p b n", b=2)
        Xg = WORK[:, 0:2 * D].rearrange("p (b n) -> p b n", b=2)
        XgT = HT[:, 0:4, :].rearrange("p a n -> p (a n)").rearrange("p (b k s) -> p b k s", b=2, k=KD)
        hmidT = HT[:, 4, :].rearrange("p (b m s) -> p b m s", b=2, m=2)
        routes = HT[:, 5, 0:NT * N_EXP * 4].rearrange("p (i e c) -> p i e c", i=NT, e=N_EXP)
        place = HT[:, 5, 256:256 + NT * N_EXP].rearrange("p (i e) -> p i e", i=NT)
        by_slot = HT[:, 5, 320:320 + 4 * N_EXP].rearrange("p (e c) -> p e c", c=4)
        Y = WORK[:, 2 * D:4 * D].rearrange("p (b n) -> p b n", b=2)
        silu = WORK[:, 5120:5632].rearrange("p (b n) -> p b n", b=2)
        hmid = WORK[:, 5632:6144].rearrange("p (b n) -> p b n", b=2)
        Y1 = HT[:, :, :].rearrange("p k t -> p (k t)").rearrange("p (i n) -> p i n", i=NT)
        onehot = O[:, :, :].rearrange("p i n -> p (i n)").rearrange("p (q e i s) -> p q e i s", q=2, e=EPG, i=NT)
        rt = WORK[:, 4096:4096 + 1024].rearrange("p (s i e) -> p s i e", s=16, i=NT)
        sel = rt[:, 4, :, :]

        ps = [ctx.enter_context(nc.psum_tensor(f"ps{i}", [P, 512], F32)) for i in range(8)]
        JB = 4

        scratch_back = nc.dram_tensor("scratch_back", [NH, 640], F32, kind="Internal").ap()
        scratch_near = nc.dram_tensor("scratch_near", [NH, 384], F32, kind="Internal").ap()
        bias_back = nc.dram_tensor("bias_back", [NH, P, T], F32, kind="Internal").ap()
        bias_near = nc.dram_tensor("bias_near", [NH, P, 2 * WINDOW], F32, kind="Internal").ap()
        tokens = [nc.dram_tensor(f"tokens{n}", [T, D], F32, kind="Internal").ap() for n in range(2)]
        answers = [nc.dram_tensor(f"answers{n}", [2 * T, D], F32, kind="Internal").ap() for n in range(2)]

        jobs, stage = [], {}

        def plan(name, engines):
            stage[name] = range(len(jobs), len(jobs) + len(engines))
            jobs.extend(engines)

        plan("cond", "A")
        plan("bias", "DDD")
        plan("biasc", "ADAD")
        plan("pos", "AD")
        for layer in range(2):
            if layer == 0:
                plan("ada0.0", "D")
                plan("hT0", "ADADADAD")
                plan("kcvc", "ADAD")
                plan("ada0.1", "DAA")
                plan("ksvs", "ADADAD")
                plan("kwvw", "ADADAD")
                plan("gl", "A")
                plan("ada0.2", "DAA")
                plan("posb", "DD")
                plan("hid", "AAAA")
                plan("cmp", "DD")
                plan("ada1.0", "D")
                plan("ada1.1", "DAA")
                plan("ada1.2", "DAA")
            else:
                plan("xT1", "AAAAAAAA")
                plan("kv", "ADADAD")
            plan(f"oT{layer}", "ADADADAD")
            plan(f"wo{layer}", "D" * 8)
            plan(f"hf{layer}", "ADADADAD")
            plan(f"rout{layer}", "A")
            plan(f"place{layer}", "D")
            plan(f"slots{layer}", "DDDD")
        product = sem("product")
        evac = {"A": sem("evac_act"), "D": sem("evac_dve")}
        nth = [jobs[:j + 1].count(jobs[j]) for j in range(len(jobs))]

        def bank(j):
            return ps[j % JB]

        def wait_bank(eng, j):
            if j >= JB:
                eng.wait_ge(evac[jobs[j - JB]], nth[j - JB])

        def wait_evacuated(eng, name, last=None):
            js = list(stage[name])[:last]
            for e in "AD":
                own = [nth[j] for j in js if jobs[j] == e]
                if own:
                    eng.wait_ge(evac[e], own[-1])

        loaded = [0] * (RING + 1)
        items = {}

        def item(name, slot, rounds=1):
            items[name] = (slot, loaded[slot])
            loaded[slot] += 16 * rounds

        first_items = [f"ada0.0.{q}" for q in range(3)] + ["kcvc"] + [f"ada0.1.{q}" for q in range(3)] \
            + ["ksvs", "kwvw"] + [f"ada0.2.{q}" for q in range(3)] + ["w1k", "w1v"]
        for n, name in enumerate(first_items):
            item(name, n % RING)
        item("wq0", 2, NG)
        next_items = [f"ada1.{c}.{q}" for c in range(3) for q in range(3)] + ["wo0.0", "wo0.1"]
        for n, name in enumerate(next_items):
            item(name, n % RING)
        SLOTS = RING + 1
        ROUNDS = N_EXP // SLOTS
        before_experts = {0: list(loaded)}
        for n in range(SLOTS):
            loaded[n] += 48 * ROUNDS
        item("wkv", 0)
        item("wq1", 1, NG)
        item("wo1.0", 2)
        item("wo1.1", 0)
        before_experts[1] = list(loaded)

        landed = [sem(f"landed{s}") for s in range(RING + 1)]

        def slot(name):
            s = items[name][0]
            return ring[:, s, :]

        def wait_item(eng, name):
            s, before = items[name]
            eng.wait_ge(landed[s], before + 16)

        x_in, c_in, small_in, oh_in, adab_in, gl_in, ln_in = map(sem, (
            "x_in", "c_in", "small_in", "oh_in", "adab_in", "gl_in", "ln_in"))
        consts, rel_ready, vrow_ready, vrow_out, toeplitz = map(sem, (
            "consts", "rel_ready", "vrow_ready", "vrow_out", "toeplitz"))
        ada_sum = sem("ada_sum")
        dve_step, act_step, pool_step = sem("dve_step"), sem("act_step"), sem("pool_step")
        names = ("qproj qt bias_even bias_odd score logit expo turn pte_act pte_dve pv cscore cshift cexp cprob cturn "
                 "cpt cpv comb heads").split()
        A = [{n: sem(f"{n}{layer}") for n in names} for layer in range(2)]
        mnames = "xturn xact xdve gu silu hmid hturn hmt down yact ydve yfree".split()
        M = [{n: sem(f"m_{n}{layer}") for n in mnames} for layer in range(2)]
        PRIMED = 1
        ln_var, ln_rstd, ln_nb, ln_norm, ln_gain, ln_done = (
            sem(f"ln_{n}") for n in ("var", "rstd", "nb", "norm", "gain", "done"))
        routed = [sem(f"routed{n}") for n in range(2)]
        onehot_ready = [sem(f"onehot{n}") for n in range(2)]
        slots_ready = [sem(f"slots_ready{n}") for n in range(2)]
        tokens_out = [sem(f"tokens_out{n}") for n in range(2)]
        gathered = [[sem(f"gathered{n}{b}") for b in range(2)] for n in range(2)]
        scattered = [[sem(f"scattered{n}{b}") for b in range(2)] for n in range(2)]
        answers_in = [sem(f"answers_in{n}") for n in range(2)]
        rnames = "w onehot rows slots gather xturn xact gu silu hmid hturn hmt down y scatter free".split()
        R_ = [{n: sem(f"r_{n}{layer}") for n in rnames} for layer in range(2)]
        more_step = [sem(f"more_step{n}") for n in range(2)]
        WS = [3, 2, 0, 1]
        stored = sem("stored")
        hT1_ready = sem("hT1_ready")

        def expert_slot(n):
            s = WS[n % SLOTS]
            return ring[:, s, :] if s < RING else KTV[:, :]

        def gate_up(w):
            return w[:, 0:4096].rearrange("p (b k n) -> p k b n", b=2, k=KD)

        def down(w):
            return w[:, 4096:6144].rearrange("p (k n) -> p k n", k=2)

        def apart(eng):
            eng.nop(nofuse=True)

        CHUNK = [3, 3, 2]

        U = [2 * NT, NT]
        units = [[(i, b, 0, P * (i + 1)) for i in range(NT) for b in range(2)],
                 [(i, 0, P * max(i - 1, 0), P * min(i + 1, 2)) for i in range(NT)]]
        LAG = 3

        block = ctx.enter_context(nc.Block())

        @block.sync
        def _(sp):
            def load(name, dst, src, after=None):
                if after is not None:
                    for s, v in after:
                        sp.wait_ge(s, v)
                sp.dma_start(dst, src).then_inc(landed[items[name][0]], 16)

            def ada_item(layer, c, q, after):
                k0, n = sum(CHUNK[:q]), CHUNK[q]
                name = f"ada{layer}.{c}.{q}"
                load(name, slot(name)[:, 0:n * PART].rearrange("p (k n) -> p k n", k=n),
                     t["ada_w"][layer, k0 * P:(k0 + n) * P, c * PART:(c + 1) * PART].rearrange("(k p) n -> p k n", p=P),
                     after)

            def matrix(name, src, after):
                k, n = src.shape[0] // P, src.shape[1]
                load(name, slot(name)[:, 0:k * n].rearrange("p (k n) -> p k n", k=k),
                     src.rearrange("(k p) n -> p k n", p=P), after)

            def used(names):
                out = []
                for n in names:
                    if isinstance(n, tuple):
                        out.append(n)
                    else:
                        out.append((product, stage[n][-1] + 1))
                return out

            for sems in A + M + R_:
                for n, primed in sems.items():
                    if n not in ("bias_even", "bias_odd", "w", "gather", "scatter"):
                        sp.sem_inc(primed, PRIMED)
            sp.dma_start(c8, t["c"].rearrange("o (k p) -> (o k) p", p=P)).then_inc(c_in, 16)
            sp.dma_start(adab, t["ada_b"][0:1, 0:PART]).then_inc(adab_in, 16)
            done_ada = {}
            n = 0
            for layer in range(2):
                for c in range(3):
                    for q in range(3):
                        n += 1
                        done_ada[f"ada{layer}.{c}.{q}"] = (ada_sum, n)
            win = t["nsa_w_in"][0]
            c0 = QW
            release = {f"ada{a}.{c}.{q}": [done_ada[f"ada{a}.{c}.{q}"]] for a in range(2) for c in range(3) for q in range(3)}
            release |= {"kcvc": used(["kcvc"]), "ksvs": used(["ksvs"]), "kwvw": used(["kwvw"]), "w1k": used(["hid"]),
                        "w1v": used(["hid"]), "wo0.0": used(["wo0"]), "wo0.1": used(["wo0"])}
            for n, name in enumerate(first_items):
                after_ = release[first_items[n - RING]] if n >= RING else None
                if name.startswith("ada"):
                    ada_item(0, int(name[5]), int(name[7]), after_)
                elif name in ("kcvc", "ksvs", "kwvw"):
                    b = {"kcvc": 0, "ksvs": 1, "kwvw": 2}[name]
                    matrix(name, win[:, c0 + 2 * b * KVW:c0 + 2 * (b + 1) * KVW], after_)
                else:
                    matrix(name, t["cmp_k_w1" if name == "w1k" else "cmp_v_w1"][0], after_)
                if name == "ada0.0.2":
                    sp.dma_start(X[:, :, :], t["x"].rearrange("o (i p) n -> p (o i) n", p=P)).then_inc(x_in, 16)
                if name in ("kcvc", "kwvw"):
                    c = 1 if name == "kcvc" else 2
                    sp.wait_ge(product, stage[f"ada0.{c - 1}"][-1] + 1)
                    sp.dma_start(adab, t["ada_b"][0:1, c * PART:(c + 1) * PART]).then_inc(adab_in, 16)

            def attention_loads(layer):
                S = A[layer]
                wq = win[:, 0:QW] if layer == 0 else t["swa_w_q"][0]
                name = f"wq{layer}"
                dst = slot(name)[:, 0:KD * KVW].rearrange("p (k n) -> p k n", k=KD)
                width = units[layer][-1][3]
                table = bias_back if layer == 0 else bias_near
                with sp.Fori(0, NG) as g:
                    sp.wait_ge(S["qproj"], PRIMED + g * 2)
                    sp.dma_start(dst, wq[:, bass.ds(g * KVW, KVW)].rearrange("(k p) n -> p k n", p=P))\
                        .then_inc(landed[items[name][0]], 16)
                    for hh in range(HPG):
                        if hh >= 2:
                            sp.wait_ge(S["logit"], PRIMED + g * (HPG * U[layer]) + (hh - 1) * U[layer])
                        else:
                            sp.wait_ge(S["logit"], PRIMED + g * (HPG * U[layer]))
                        sp.dma_start(B[:, hh % 2, 0:width],
                                     table[bass.ds(g * HPG + hh, 1)].rearrange("o p n -> p (o n)"))\
                            .then_inc(S["bias_odd" if hh % 2 else "bias_even"], 16)

            for s, v in release[[n for n in first_items if items[n][0] == 2][-1]]:
                sp.wait_ge(s, v)
            sp.wait_ge(toeplitz, 32)
            sp.wait_ge(product, stage["cmp"][-1] + 1)
            for e in "AD":
                sp.wait_ge(evac[e], max(nth[j] for j in range(stage["cmp"][-1] + 1) if jobs[j] == e))
            attention_loads(0)

            for n, name in enumerate(next_items):
                s = items[name][0]
                if n >= RING:
                    after_ = release[next_items[n - RING]]
                elif s == 2:
                    after_ = [(A[0]["qproj"], PRIMED + 2 * NG)]
                else:
                    after_ = release[[m for m in first_items if items[m][0] == s][-1]]
                if name.startswith("ada"):
                    c, q = int(name[5]), int(name[7])
                    if q == 0:
                        sp.wait_ge(A[0]["heads"], PRIMED + NH)
                        if c:
                            sp.wait_ge(product, stage[f"ada1.{c - 1}"][-1] + 1)
                        sp.dma_start(adab, t["ada_b"][1:2, c * PART:(c + 1) * PART]).then_inc(adab_in, 16)
                    ada_item(1, c, q, after_)
                else:
                    b = int(name[-1])
                    matrix(name, t["nsa_w_out"][0][:, b * 512:(b + 1) * 512], after_)

            def norm_params(n):
                layer, sub = n // 2, n % 2
                sp.dma_start(lng, t["ln_g"][layer, sub:sub + 1, :].to_broadcast([P, D])).then_inc(ln_in, 16)
                sp.dma_start(lnb, t["ln_b"][layer, sub:sub + 1, :].to_broadcast([P, D])).then_inc(ln_in, 16)

            def expert_load(layer, dst, e, done):
                for j, w in enumerate(("moe_w_gate", "moe_w_up")):
                    sp.dma_start(dst[:, j * 2048:(j + 1) * 2048].rearrange("p (k n) -> p k n", k=KD),
                                 t[w][layer][bass.ds(e, 1)].rearrange("o (k p) n -> p (o k) n", p=P)).then_inc(done, 16)
                sp.dma_start(down(dst), t["moe_w_down"][layer][bass.ds(e, 1)].rearrange("o (k p) n -> p (o k) n", p=P))\
                    .then_inc(done, 16)

            def expert_loads(layer):
                with sp.Fori(1, ROUNDS) as r:
                    for n in range(SLOTS):
                        sp.wait_ge(M[layer]["down"], PRIMED + r * SLOTS + (n + 1 - SLOTS))
                        expert_load(layer, expert_slot(n), r * SLOTS + n, landed[WS[n]])

            def more_loads(layer):
                with sp.Fori(0, N_EXP) as e:
                    sp.wait_ge(R_[layer]["down"], PRIMED + e * 3)
                    expert_load(layer, ring[:, 0, :], e, R_[layer]["w"])

            def answers_back(layer):
                for b in range(2):
                    sp.wait_ge(scattered[layer][b], 16 * N_EXP // 2)
                src = answers[layer].rearrange("(i p r) n -> p i r n", p=P, r=2)
                for i in range(NT):
                    sp.dma_start(O[:, i, :], src[:, i, 0, :]).then_inc(answers_in[layer], 16)
                    sp.dma_start(Y1[:, i, :], src[:, i, 1, :]).then_inc(answers_in[layer], 16)

            def general(layer):
                sp.wait_ge(M[layer]["down"], PRIMED + N_EXP)
                sp.wait_ge(slots_ready[layer], 4)
                flag = sp.value_load(many[0:1, layer:layer + 1], min_val=0, max_val=1)
                with sp.If(flag == 1):
                    more_loads(layer)
                    sp.wait_ge(R_[layer]["scatter"], 16 * 3 * N_EXP)

            norm_params(0)
            expert_load(0, expert_slot(0), 0, landed[WS[0]])
            sp.wait_ge(product, stage["ada1.2"][-1] + 1)
            expert_load(0, expert_slot(1), 1, landed[WS[1]])
            for i in range(NT):
                sp.wait_ge(ln_done, 0 * NT + i + 1)
                sp.dma_start(tokens[0][i * P:(i + 1) * P, :], X[:, i, :]).then_inc(tokens_out[0], 16)
            for n in (2, 3):
                expert_load(0, expert_slot(n), n, landed[WS[n]])
            norm_params(1)
            expert_loads(0)
            general(0)
            answers_back(0)
            matrix("wkv", t["shared_w_kv"], None)
            attention_loads(1)
            matrix("wo1.0", t["swa_w_out"][0][:, 0:512], None)
            matrix("wo1.1", t["swa_w_out"][0][:, 512:1024], [(product, stage["kv"][-1] + 1)])
            sp.wait_ge(A[1]["heads"], PRIMED + NH)
            sp.wait_ge(A[1]["pv"], PRIMED + NH * U[1])
            norm_params(2)
            expert_load(1, expert_slot(0), 0, landed[WS[0]])
            for i in range(NT):
                sp.wait_ge(ln_done, 2 * NT + i + 1)
                sp.dma_start(tokens[1][i * P:(i + 1) * P, :], X[:, i, :]).then_inc(tokens_out[1], 16)
            for n in (1, 2, 3):
                expert_load(1, expert_slot(n), n, landed[WS[n]])
            norm_params(3)
            expert_loads(1)
            general(1)
            answers_back(1)
            for i in range(NT):
                sp.wait_ge(ln_done, 3 * NT + i + 1)
                sp.dma_start(t["out"][0, i * P:(i + 1) * P, :], X[:, i, :]).then_inc(stored, 16)
            sp.wait_ge(stored, 16 * NT)

        @block.gpsimd
        def _(pool):
            steps = Steps(pool, pool_step)
            nc.gpsimd.memset(ones[:, :], 1.0).then_inc(consts, 1)
            nc.gpsimd.memset(nhalf[:, :], -0.5).then_inc(consts, 1)
            steps.link(nc.gpsimd.memset(ident[:, :], 0.0))
            nc.gpsimd.affine_select(out=ident[:, :], in_=ident[:, :], compare_op=ALU.not_equal, fill=1.0, base=0,
                                    pattern=[[-1, P]], channel_multiplier=1).then_inc(consts, 1)
            steps.link(nc.gpsimd.memset(maskc[:, :, :], 1.0))
            nc.gpsimd.affine_select(out=maskc[:, :, :], in_=maskc[:, :, :], compare_op=ALU.is_ge, fill=0.0,
                                    base=1 - CMP_LEN, pattern=[[P, NT], [-CMP_STRIDE, NC]],
                                    channel_multiplier=1).then_inc(consts, 1)
            steps.link(nc.gpsimd.memset(relb[:, :], MASKED * -1.0))
            steps.link(nc.gpsimd.memset(upper[:, :], 1.0))
            nc.gpsimd.affine_select(out=upper[:, :], in_=upper[:, :], compare_op=ALU.is_gt, fill=0.0, base=0,
                                    pattern=[[1, P]], channel_multiplier=-1).then_inc(consts, 1)
            nc.gpsimd.iota(row[:, :], pattern=[[1, P]], base=0, channel_multiplier=0,
                           allow_small_or_imprecise_dtypes=True).then_inc(consts, 1)
            nc.gpsimd.iota(tcol[:, :], pattern=[[P, NT]], base=0, channel_multiplier=1,
                           allow_small_or_imprecise_dtypes=True).then_inc(consts, 1)
            pool.dma_start(relb[0:BUCKETS, :], t["rel_bias"]).then_inc(rel_ready, 16)
            pool.dma_start(OH, t["buckets"]).then_inc(oh_in, 16)
            pool.dma_start(pos16[:, 0, :], t["cmp_k_pos"].rearrange("o (k l) d -> (o k) (l d)", l=2)).then_inc(small_in, 16)
            pool.dma_start(pos16[:, 1, :], t["cmp_v_pos"].rearrange("o (k l) d -> (o k) (l d)", l=2)).then_inc(small_in, 16)
            pool.dma_start(glw, win_gates(t)).then_inc(gl_in, 16)
            pool.dma_start(w2[:, 0], t["cmp_k_w2"][0].rearrange("(m p) n -> p m n", p=P)).then_inc(small_in, 16)
            pool.dma_start(w2[:, 1], t["cmp_v_w2"][0].rearrange("(m p) n -> p m n", p=P)).then_inc(small_in, 16)
            pool.dma_start(routw[:, :, :], t["router_w"].rearrange("(k p) n -> p k n", p=P)).then_inc(small_in, 16)
            pool.dma_start(routb[:, :], t["router_b"].rearrange("(o n) -> o n", o=1).to_broadcast([P, N_EXP])).then_inc(small_in, 16)
            pool.dma_start(nsink[:, :], t["swa_sinks"].to_broadcast([P, NH])).then_inc(small_in, 16)
            wait_evacuated(pool, "bias")
            pool.dma_start(scratch_back, biasrow[:, 0:640]).then_inc(vrow_out, 16)
            pool.dma_start(scratch_near, biasrow[:, 640:1024]).then_inc(vrow_out, 16)
            pool.wait_ge(vrow_out, 32)
            for src, dst, n, width in ((scratch_back, bias_back, T, 640), (scratch_near, bias_near, 2 * WINDOW, 384)):
                shifted = bass.AP(tensor=src.tensor, offset=P - 1, ap=[[width, NH], [-1, P], [1, n]])
                pool.dma_start(dst, shifted).then_inc(toeplitz, 16)

            def heads(layer):
                S = A[layer]
                with pool.Fori(0, NG) as g:
                    for hh in range(HPG):
                        pool.wait_ge(S["comb"], PRIMED + g * HPG + hh + 1)
                        o = O[:, :, bass.ds((g * HPG + hh) * HD, HD)]
                        if layer == 0:
                            v = osc.rearrange("p (i b) d -> p i b d", b=2)
                            nc.gpsimd.tensor_tensor(o, v[:, :, 0, :], v[:, :, 1, :], ALU.add).then_inc(S["heads"], 1)
                        else:
                            nc.gpsimd.tensor_copy(o, osc[:, 0:NT, :]).then_inc(S["heads"], 1)

            def norm(n):
                for i in range(NT):
                    pool.wait_ge(ln_var, NT * n + i + 1)
                    nc.gpsimd.tensor_tensor(mv[:, i, 2:3], mv[:, i, 1:2], nhalf[:, :], ALU.pow).then_inc(ln_rstd, 1)
                pool.wait_ge(ln_in, 32 * (n + 1))
                for i in range(NT):
                    pool.wait_ge(ln_gain, NT * n + i + 1)
                    nc.gpsimd.tensor_tensor(X[:, i, :], X[:, i, :], lnb, ALU.add).then_inc(ln_done, 1)

            def gather(dst, rows, layer):
                return nc.gpsimd.indirect_dma_start(dst, None, tokens[layer], bass.IndirectOffsetOnAxis(ap=rows, axis=0),
                                                    bounds_check=T - 1, oob_is_err=False)

            def scatter(src, rows, layer):
                return nc.gpsimd.indirect_dma_start(answers[layer], bass.IndirectOffsetOnAxis(ap=rows, axis=0), src, None,
                                                    bounds_check=2 * T - 1, oob_is_err=False)

            def experts(layer):
                S = M[layer]

                def fetch(e):
                    pool.wait_ge(slots_ready[layer], e // EPG + 1)
                    if e >= 2:
                        pool.wait_ge(S["xturn"], PRIMED + e - 1)
                    gather(Xg[:, e % 2, :], slot_rows[:, 0, e:e + 1], layer).then_inc(gathered[layer][e % 2], 16)

                pool.wait_ge(routed[layer], 1)
                steps.link(nc.gpsimd.memset(Xg[:, :, :], 0.0))
                pool.wait_ge(tokens_out[layer], 16 * NT)
                fetch(0)
                fetch(1)
                pool.sem_inc(S["yfree"], 1)
                for e in range(N_EXP):
                    if e + 2 < N_EXP:
                        fetch(e + 2)
                    if e:
                        pool.wait_ge(scattered[layer][(e - 1) % 2], 16 * ((e - 1) // 2 + 1))
                        pool.sem_inc(S["yfree"], 1)
                    pool.wait_ge(S["yact"], PRIMED + e + 1)
                    pool.wait_ge(S["ydve"], PRIMED + e + 1)
                    scatter(Y[:, e % 2, :], slot_rows[:, 1, e:e + 1], layer).then_inc(scattered[layer][e % 2], 16)
                for b in range(2):
                    pool.wait_ge(scattered[layer][b], 16 * N_EXP // 2)
                flag = pool.value_load(many[0:1, layer:layer + 1], min_val=0, max_val=1)
                with pool.If(flag == 1):
                    more_tokens(layer)

            def more_tokens(layer):
                S = R_[layer]
                with pool.Fori(0, N_EXP) as e:
                    for b in range(3):
                        pool.wait_ge(S["rows"], PRIMED + e * 3 + (b + 1))
                        apart(pool)
                        gather(Xg[:, 0, :], more_rows[:, 0:1], layer).then_inc(S["gather"], 16)
                        pool.wait_ge(S["y"], PRIMED + e * 3 + (b + 1))
                        apart(pool)
                        scatter(Y[:, 0, :], more_rows[:, 1:2], layer).then_inc(S["scatter"], 16)
                        pool.wait_ge(S["scatter"], e * 48 + 16 * (b + 1))
                        pool.sem_inc(S["free"], 1)

            pool.wait_ge(product, stage["cmp"][-1] + 1)
            heads(0)
            norm(0)
            experts(0)
            norm(1)
            heads(1)
            norm(2)
            experts(1)
            norm(3)

        @block.tensor
        def _(pe):
            def mm(out, lhsT, rhs, start, stop):
                return nc.tensor.matmul(out, lhsT, rhs, start=start, stop=stop)

            def ada(layer, c):
                js = iter(stage[f"ada{layer}.{c}"])
                pe.wait_ge(ada_sum, 9 * layer + 3 * (c + 1))
                pe.wait_ge(adab_in, 16 * (3 * layer + c + 1))
                cols = {0: range(16), 1: range(8, 16), 2: range(8)}[c]
                j = next(js)
                wait_bank(pe, j)
                for n, q in enumerate(cols):
                    mm(bank(j)[:, n:n + 1], acc[:, q * P:(q + 1) * P], ones[:, 0:1], True, False)
                    last = mm(bank(j)[:, n:n + 1], adab[:, q * P:(q + 1) * P], ones[0:1, 0:1], False, True)
                last.then_inc(product, 1)
                if c:
                    for q in range(2):
                        j = next(js)
                        o = (0 if c == 1 else D) + q * 512
                        wait_bank(pe, j)
                        mm(bank(j)[:, :], ones[:, :], acc[:, o:o + 512], True, False)
                        mm(bank(j)[:, :], ones[0:1, :], adab[:, o:o + 512], False, True).then_inc(product, 1)

            def turn(name, rows):
                for k, j in enumerate(stage[name]):
                    wait_bank(pe, j)
                    for i in range(NT):
                        last = nc.tensor.transpose(bank(j)[:, i * P:(i + 1) * P], rows[:, i, k * P:(k + 1) * P], ident[:, :])
                    last.then_inc(product, 1)

            def by_columns(js, w, cols, src):
                for j, c in zip(js, cols):
                    wait_bank(pe, j)
                    for k in range(KD):
                        last = mm(bank(j)[:, :], w[:, k, c:c + P], src[:, k, :], k == 0, k == KD - 1)
                    last.then_inc(product, 1)

            def by_tokens(js, w, c, n, src):
                for i, j in enumerate(js):
                    wait_bank(pe, j)
                    for k in range(KD):
                        last = mm(bank(j)[:, 0:n], src[:, k, i * P:(i + 1) * P], w[:, k, c:c + n], k == 0, k == KD - 1)
                    last.then_inc(product, 1)

            def as_matrix(name, n=512, k=KD):
                return slot(name)[:, 0:k * n].rearrange("p (k n) -> p k n", k=k)

            pe.wait_ge(consts, 3)
            pe.wait_ge(c_in, 16)
            j, = stage["cond"]
            nc.tensor.transpose(bank(j)[:, 0:KD], c8, ident[0:KD, 0:KD]).then_inc(product, 1)
            pe.wait_ge(rel_ready, 16)
            pe.wait_ge(oh_in, 16)
            pe.wait_ge(pool_step, 3)
            for j, (o, n) in zip(stage["bias"], ((BACK, 512), (BACK + 512, 128), (NEAR, 384))):
                mm(bank(j)[0:NH, 0:n], relb[:, :], OH[:, o:o + n], True, True).then_inc(product, 1)
            for i, j in enumerate(stage["biasc"]):
                wait_bank(pe, j)
                for n in range(NC):
                    o = AHEAD + T + i * P - n * CMP_STRIDE - (CMP_LEN - 1)
                    last = mm(bank(j)[:, n * NH:(n + 1) * NH], OH[:, o:o + P], relb[:, :], True, True)
                last.then_inc(product, 1)
            pe.wait_ge(small_in, 16 * 7)
            for b, j in enumerate(stage["pos"]):
                wait_bank(pe, j)
                nc.tensor.transpose(bank(j)[:, 0:CK], pos16[:, b, :], ident[0:CK, 0:CK]).then_inc(product, 1)
            ada(0, 0)
            pe.wait_ge(x_in, 16)
            turn("hT0", X)
            wait_evacuated(pe, "hT0")
            wait_item(pe, "kcvc")
            by_columns(stage["kcvc"], as_matrix("kcvc"), (0, P, 2 * P, 3 * P), HT)
            ada(0, 1)
            for name in ("ksvs", "kwvw"):
                wait_item(pe, name)
                by_columns(stage[name][0:2], as_matrix(name), (0, P), HT)
                by_tokens(stage[name][2:], as_matrix(name), KVW, KVW, HT)
            pe.wait_ge(gl_in, 16)
            j, = stage["gl"]
            wait_bank(pe, j)
            for i in range(NT):
                for k in range(KD):
                    last = mm(bank(j)[:, i * 3 * NH:(i + 1) * 3 * NH], HT[:, k, i * P:(i + 1) * P], glw[:, k, :],
                              k == 0, k == KD - 1)
            last.then_inc(product, 1)
            ada(0, 2)
            wait_evacuated(pe, "pos")
            wait_evacuated(pe, "kcvc")
            for b, (j, name) in enumerate(zip(stage["posb"], ("w1k", "w1v"))):
                wait_item(pe, name)
                wait_bank(pe, j)
                for m in range(2):
                    for k in range(CK):
                        last = mm(bank(j)[:, m:m + 1], as_matrix(name, 256, CK)[:, k, m * P:(m + 1) * P],
                                  posT[:, b, k:k + 1], k == 0, k == CK - 1)
                last.then_inc(product, 1)
            js = iter(stage["hid"])
            for name, src in (("w1k", KC2), ("w1v", VC2)):
                for m in range(2):
                    j = next(js)
                    wait_bank(pe, j)
                    for k in range(CK):
                        last = mm(bank(j)[:, 0:NG * NC], as_matrix(name, 256, CK)[:, k, m * P:(m + 1) * P],
                                  src[:, :, k:k + 8 * (NC - 1) + 1:8], k == 0, k == CK - 1)
                    last.then_inc(product, 1)
            wait_evacuated(pe, "hid")
            j, jv = stage["cmp"]
            wait_bank(pe, j)
            for m in range(2):
                last = mm(bank(j)[0:HD, 0:NG * NC], w2[:, 0, m, :], hid[:, 0, m, 0:NG * NC], m == 0, m == 1)
            last.then_inc(product, 1)
            wait_bank(pe, jv)
            for g in range(NG):
                for m in range(2):
                    last = mm(bank(jv)[0:NC, g * HD:(g + 1) * HD], hid[:, 1, m, g * NC:(g + 1) * NC], w2[:, 1, m, :],
                              m == 0, m == 1)
            last.then_inc(product, 1)

            def attention(layer):
                S = A[layer]
                n_units = HPG * U[layer]
                w = slot(f"wq{layer}")[:, 0:KD * KVW].rearrange("p (k n) -> p k n", k=KD)
                s, before = items[f"wq{layer}"]
                with pe.Fori(0, NG) as g:
                    def scores(u):
                        i, b, k0, ext = units[layer][u % U[layer]]
                        if u >= 2:
                            pe.wait_ge(S["logit"], PRIMED + g * n_units + u - 1)
                        apart(pe)
                        mm(ps[4 + u % 2][:, 0:ext], QT[:, u // U[layer], i * P:(i + 1) * P],
                           KT[:, b, bass.ds(g, 1), k0:k0 + ext].rearrange("p o t -> p (o t)"), True, True)\
                            .then_inc(S["score"], 1)

                    def turns(u):
                        ext = units[layer][u % U[layer]][3]
                        pe.wait_ge(S["expo"], PRIMED + g * n_units + u + 1)
                        if u >= 2:
                            pe.wait_ge(S["pte_act" if u % 2 == 0 else "pte_dve"], PRIMED + g * (n_units // 2) + u // 2)
                        for k in range(ext // P):
                            last = nc.tensor.transpose(ps[6 + u % 2][:, k * P:(k + 1) * P],
                                                       probs[:, u % 2, k * P:(k + 1) * P], ident[:, :])
                        last.then_inc(S["turn"], 1)

                    def values(u):
                        i, b, k0, ext = units[layer][u % U[layer]]
                        hh, n = divmod(u, U[layer])
                        pe.wait_ge(S["pte_act" if u % 2 == 0 else "pte_dve"], PRIMED + g * (n_units // 2) + u // 2 + 1)
                        if n == 0:
                            pe.wait_ge(S["comb"], PRIMED + g * HPG + hh)
                        apart(pe)
                        for k in range(ext // P):
                            last = mm(ps[3][:, n * HD:(n + 1) * HD], probsT[:, u % 2, k * P:(k + 1) * P],
                                      V[:, b, k0 // P + k, bass.ds(g * HD, HD)], k == 0, k == ext // P - 1)
                        last.then_inc(S["pv"], 1)

                    pe.wait_ge(landed[s], g * 16 + (before + 16))
                    if layer == 0:
                        pe.wait_ge(S["cpt"], PRIMED + g * HPG)
                    for m in range(2):
                        for k in range(KD):
                            last = mm(ps[1 + m][:, :], w[:, k, m * P:(m + 1) * P], HT[:, k, :], k == 0, k == KD - 1)
                        last.then_inc(S["qproj"], 1)
                    pe.wait_ge(S["qt"], PRIMED + g * 2 + 2)
                    for u in range(n_units + LAG):
                        hh, n = divmod(u, U[layer])
                        if u < n_units:
                            if layer == 0 and n == 0:
                                if hh:
                                    pe.wait_ge(S["cshift"], PRIMED + g * HPG + hh)
                                apart(pe)
                                for i in range(NT):
                                    last = mm(ps[1][:, i * NCP:i * NCP + NC], QT[:, hh, i * P:(i + 1) * P],
                                              KC[:, bass.ds(g, 1), :].rearrange("p o n -> p (o n)"), True, True)
                                last.then_inc(S["cscore"], 1)
                            scores(u)
                        if 0 <= u - LAG + 1 < n_units:
                            turns(u - LAG + 1)
                        if layer == 0 and n == 5 and u < n_units:
                            pe.wait_ge(S["cprob"], PRIMED + g * HPG + hh + 1)
                            if hh:
                                pe.wait_ge(S["cpt"], PRIMED + g * HPG + hh)
                            for i in range(NT):
                                last = nc.tensor.transpose(ps[2][0:NC, i * P:(i + 1) * P], Pc[:, i, 0:NC], ident[:, :])
                            last.then_inc(S["cturn"], 1)
                        if layer == 0 and n == 7 and u < n_units:
                            pe.wait_ge(S["cpt"], PRIMED + g * HPG + hh + 1)
                            pe.wait_ge(S["comb"], PRIMED + g * HPG + hh)
                            apart(pe)
                            for i in range(NT):
                                last = mm(ps[0][:, i * HD:(i + 1) * HD], PcT[0:NC, i * P:(i + 1) * P],
                                          VC[0:NC, bass.ds(g * HD, HD)], True, True)
                            last.then_inc(S["cpv"], 1)
                        if u >= LAG:
                            values(u - LAG)
                    pe.wait_ge(S["comb"], PRIMED + g * HPG + HPG)

            def output(layer):
                turn_name = f"oT{layer}"
                pe.wait_ge(A[layer]["heads"], PRIMED + NH)
                turn(turn_name, O)
                wait_evacuated(pe, turn_name)
                js = iter(stage[f"wo{layer}"])
                for i in range(NT):
                    for b in range(2):
                        name = f"wo{layer}.{b}"
                        wait_item(pe, name)
                        j = next(js)
                        wait_bank(pe, j)
                        for k in range(KD):
                            last = mm(bank(j)[:, :], HT[:, k, i * P:(i + 1) * P], as_matrix(name)[:, k, :],
                                      k == 0, k == KD - 1)
                        last.then_inc(product, 1)

            def route(layer):
                pe.wait_ge(ln_done, NT * (2 * layer) + NT)
                turn(f"hf{layer}", X)
                wait_evacuated(pe, f"hf{layer}")
                j, = stage[f"rout{layer}"]
                wait_bank(pe, j)
                for i in range(NT):
                    for k in range(KD):
                        last = mm(bank(j)[:, i * N_EXP:(i + 1) * N_EXP], HT[:, k, i * P:(i + 1) * P], routw[:, k, :],
                                  k == 0, k == KD - 1)
                last.then_inc(product, 1)

            def find_slots(layer):
                j, = stage[f"place{layer}"]
                wait_bank(pe, j)
                pe.wait_ge(routed[layer], 1)
                for i in range(NT):
                    for n in range(i):
                        mm(bank(j)[:, i * N_EXP:(i + 1) * N_EXP], ones[:, :], sel[:, n, :], n == 0, False)
                    mm(bank(j)[:, i * N_EXP:(i + 1) * N_EXP], upper[:, :], sel[:, i, :], i == 0, True)
                for n in range(NT):
                    last = mm(bank(j)[:, NT * N_EXP:(NT + 1) * N_EXP], ones[:, :], sel[:, n, :], n == 0, n == NT - 1)
                last.then_inc(product, 1)
                for q, j in enumerate(stage[f"slots{layer}"]):
                    wait_bank(pe, j)
                    pe.wait_ge(onehot_ready[layer], q + 1)
                    for e in range(EPG):
                        for i in range(NT):
                            last = mm(bank(j)[:, e * 4:e * 4 + 4], onehot[:, q % 2, e, i, :],
                                      routes[:, i, q * EPG + e, :], i == 0, i == NT - 1)
                    last.then_inc(product, 1)

            def turn_tokens(src, banks):
                for k in range(KD):
                    last = nc.tensor.transpose(ps[banks[k // 4]][:, (k % 4) * P:(k % 4 + 1) * P],
                                               src[:, k * P:(k + 1) * P], ident[:, :])
                return last

            def experts(layer):
                S = M[layer]

                def tokens_in(r, n):
                    v = r * SLOTS + n
                    pe.wait_ge(gathered[layer][n % 2], r * 32 + 16 * (n // 2 + 1))
                    pe.wait_ge(S["xact"], PRIMED + v)
                    pe.wait_ge(S["xdve"], PRIMED + v)
                    turn_tokens(Xg[:, n % 2, :], (0, 1)).then_inc(S["xturn"], 1)

                def hidden(r, n):
                    v = r * SLOTS + n
                    pe.wait_ge(landed[WS[n % SLOTS]], r * 48 + (before_experts[layer][WS[n % SLOTS]] + 48 * (n // SLOTS + 1)))
                    pe.wait_ge(S["xact"], PRIMED + v + 1)
                    pe.wait_ge(S["xdve"], PRIMED + v + 1)
                    if not isinstance(v, int) or v >= 2:
                        pe.wait_ge(S["hmid"], PRIMED + v - 1)
                    w = gate_up(expert_slot(n))
                    for k in range(KD):
                        last = mm(ps[2 + n % 2][:, :], XgT[:, n % 2, k, :], w[:, k, :, :], k == 0, k == KD - 1)
                    last.then_inc(S["gu"], 1)

                def step(r, n):
                    v = r * SLOTS + n
                    if not isinstance(r, int) or v + 1 < N_EXP:
                        hidden(r, n + 1)
                    pe.wait_ge(S["hmid"], PRIMED + v + 1)
                    for m in range(2):
                        last = nc.tensor.transpose(ps[4 + n % 2][:, m * P:(m + 1) * P], hmid[:, n % 2, m * P:(m + 1) * P],
                                                   ident[:, :])
                    last.then_inc(S["hturn"], 1)
                    if not isinstance(r, int) or v + 2 < N_EXP:
                        tokens_in(r, n + 2)
                    pe.wait_ge(S["hmt"], PRIMED + v + 1)
                    pe.wait_ge(S["yact"], PRIMED + v)
                    pe.wait_ge(S["ydve"], PRIMED + v)
                    w = down(expert_slot(n))
                    for b in range(2):
                        for k in range(2):
                            last = mm(ps[6 + b][:, :], hmidT[:, n % 2, k, :], w[:, k, b * 512:(b + 1) * 512], k == 0, k == 1)
                    last.then_inc(S["down"], 1)

                wait_all(f"slots{layer}")
                tokens_in(0, 0)
                hidden(0, 0)
                tokens_in(0, 1)
                with pe.Fori(0, ROUNDS - 1) as r:
                    for n in range(SLOTS):
                        step(r, n)
                for n in range(SLOTS):
                    step(ROUNDS - 1, n)
                flag = pe.value_load(many[0:1, layer:layer + 1], min_val=0, max_val=1)
                with pe.If(flag == 1):
                    more_tokens(layer)

            def more_tokens(layer):
                S = R_[layer]
                pe.wait_ge(M[layer]["yact"], PRIMED + N_EXP)
                pe.wait_ge(M[layer]["ydve"], PRIMED + N_EXP)
                with pe.Fori(0, N_EXP) as e:
                    for b in range(3):
                        v = PRIMED + e * 3 + b
                        pe.wait_ge(S["onehot"], v + 1)
                        apart(pe)
                        for i in range(NT):
                            last = mm(ps[5][:, 0:4], onehot[:, 0, 0, i, :],
                                      routes[:, i, bass.ds(e, 1), :].rearrange("p o c -> p (o c)"), i == 0, i == NT - 1)
                        last.then_inc(S["slots"], 1)
                        pe.wait_ge(S["gather"], e * 48 + 16 * (b + 1))
                        turn_tokens(Xg[:, 0, :], (0, 1)).then_inc(S["xturn"], 1)
                        pe.wait_ge(S["w"], e * 48 + 48)
                        pe.wait_ge(S["xact"], v + 1)
                        for k in range(KD):
                            last = mm(ps[2][:, :], XgT[:, 0, k, :], gate_up(ring[:, 0, :])[:, k, :, :], k == 0, k == KD - 1)
                        last.then_inc(S["gu"], 1)
                        pe.wait_ge(S["hmid"], v + 1)
                        for m in range(2):
                            last = nc.tensor.transpose(ps[4][:, m * P:(m + 1) * P], hmid[:, 0, m * P:(m + 1) * P], ident[:, :])
                        last.then_inc(S["hturn"], 1)
                        pe.wait_ge(S["hmt"], v + 1)
                        for h in range(2):
                            for k in range(2):
                                last = mm(ps[6 + h][:, :], hmidT[:, 0, k, :], down(ring[:, 0, :])[:, k, h * 512:(h + 1) * 512],
                                          k == 0, k == 1)
                        last.then_inc(S["down"], 1)

            def wait_all(last):
                for e in "AD":
                    pe.wait_ge(evac[e], max(nth[j] for j in range(stage[last][-1] + 1) if jobs[j] == e))

            wait_all("cmp")
            attention(0)
            pe.wait_ge(A[0]["heads"], PRIMED + NH)
            for c in range(3):
                ada(1, c)
            output(0)
            route(0)
            find_slots(0)
            experts(0)
            pe.wait_ge(ln_done, NT * 2)
            turn("xT1", X)
            wait_evacuated(pe, "xT1")
            wait_item(pe, "wkv")
            by_columns(stage["kv"][0:2], as_matrix("wkv"), (0, P), XTk)
            by_tokens(stage["kv"][2:], as_matrix("wkv"), KVW, KVW, XTk)
            pe.wait_ge(hT1_ready, KD)
            wait_all("kv")
            attention(1)
            output(1)
            route(1)
            find_slots(1)
            experts(1)

        @block.scalar
        def _(act):
            steps = Steps(act, act_step)

            def arrived(j):
                act.wait_ge(product, j + 1)

            def copy(out, j, src, scale=1.0):
                arrived(j)
                nc.scalar.activation(out, src, ACT.Copy, scale=scale).then_inc(evac["A"], 1)

            def mine(name):
                return [(n, j) for n, j in enumerate(stage[name]) if jobs[j] == "A"]

            (_, j), = mine("cond")
            arrived(j)
            nc.scalar.activation(cond[:, :], bank(j)[:, 0:KD], ACT.Silu).then_inc(evac["A"], 1)
            for i, j in mine("biasc"):
                copy(BC[:, i, :, :].rearrange("p n h -> p (n h)"), j, bank(j)[:, 0:NC * NH], -1.0)
            for b, j in mine("pos"):
                copy(posT[:, b, :], j, bank(j)[:, 0:CK])

            def modulated(name, layer, sub):
                for k, j in mine(name):
                    arrived(j)
                    nc.scalar.activation(HT[:, k, :], bank(j)[:, :], ACT.Identity,
                                         bias=adaC[:, layer, 2 * sub, k:k + 1],
                                         scale=adaC[:, layer, 2 * sub + 1, k:k + 1]).then_inc(evac["A"], 1)

            def ada_rows(layer, c):
                for n, j in mine(f"ada{layer}.{c}"):
                    arrived(j)
                    q = n - 1
                    nc.scalar.activation(G[:, layer, c - 1, q * 512:(q + 1) * 512], bank(j)[:, :], ACT.Identity,
                                         bias=ones[:, 0:1]).then_inc(evac["A"], 1)

            wait_evacuated(act, "ada0.0")
            modulated("hT0", 0, 0)
            for n, j in mine("kcvc"):
                arrived(j)
                split_halves(lambda o, i: nc.scalar.activation(o, i, ACT.Copy), KC2 if n < 2 else VC2, n % 2, bank(j)).then_inc(evac["A"], 1)
            act.wait_ge(consts, 3)
            ada_rows(0, 1)

            def keys_values(name, b):
                for n, j in mine(name):
                    arrived(j)
                    if n < 2:
                        for half in range(2):
                            last = nc.scalar.activation(KT[:, b, 2 * n + half, :], bank(j)[half * HD:(half + 1) * HD, :], ACT.Copy)
                    else:
                        last = nc.scalar.activation(V[:, b, n - 2, :], bank(j)[:, 0:KVW], ACT.Copy)
                    last.then_inc(evac["A"], 1)

            keys_values("ksvs", 0)
            keys_values("kwvw", 1)
            (_, j), = mine("gl")
            arrived(j)
            nc.scalar.activation(GT[:, :, :].rearrange("p i n -> p (i n)"), bank(j)[:, 0:NT * 3 * NH],
                                 ACT.Sigmoid).then_inc(evac["A"], 1)
            ada_rows(0, 2)
            wait_evacuated(act, "posb")
            for n, j in mine("hid"):
                arrived(j)
                nc.scalar.activation(hid[:, n // 2, n % 2, 0:NG * NC], bank(j)[:, 0:NG * NC], ACT.Gelu_apprx_tanh,
                                     bias=posb[:, n // 2, n % 2:n % 2 + 1]).then_inc(evac["A"], 1)

            def attention(layer):
                S = A[layer]
                n_units = HPG * U[layer]
                with act.Fori(0, NG) as g:
                    for m in range(2):
                        act.wait_ge(S["qproj"], PRIMED + g * 2 + m + 1)
                        for half in range(2):
                            last = nc.scalar.activation(QT[:, 2 * m + half, :], ps[1 + m][half * HD:(half + 1) * HD, :],
                                                        ACT.Copy, scale=-SCALE)
                        last.then_inc(S["qt"], 1)
                    for u in range(n_units + LAG - 1):
                        hh, n = divmod(u, U[layer])
                        if u < n_units:
                            i, b, k0, ext = units[layer][n]
                            if layer == 0 and n == 1:
                                act.wait_ge(S["cshift"], PRIMED + g * HPG + hh + 1)
                                nc.scalar.activation(Pc[:, :, 0:NC], Pc[:, :, 0:NC], ACT.Exp, scale=-1.0).then_inc(S["cexp"], 1)
                            act.wait_ge(S["logit"], PRIMED + g * n_units + u + 1)
                            if u >= 2:
                                act.wait_ge(S["turn"], PRIMED + g * n_units + u - 1)
                            nc.scalar.activation(probs[:, u % 2, 0:ext], logits[:, u % 2, 0:ext], ACT.Exp, scale=-1.0,
                                                 bias=mins[:, hh % 2, n:n + 1],
                                                 accum_out=sums[:, hh % 2, n:n + 1]).then_inc(S["expo"], 1)
                            if layer == 1 and n == NT - 1:
                                act.wait_ge(S["cprob"], PRIMED + g * HPG + hh + 1)
                                nc.scalar.activation(sink_exp[:, hh % 2, :], sink_diff[:, hh % 2, :], ACT.Exp).then_inc(S["cexp"], 1)
                            if layer == 0 and n == 6:
                                act.wait_ge(S["cturn"], PRIMED + g * HPG + hh + 1)
                                nc.scalar.activation(PcT[0:NC, :], ps[2][0:NC, :], ACT.Copy).then_inc(S["cpt"], 1)
                        v = u - LAG + 1
                        if v >= 0 and v % 2 == 0:
                            act.wait_ge(S["turn"], PRIMED + g * n_units + v + 1)
                            if v >= 2:
                                act.wait_ge(S["pv"], PRIMED + g * n_units + v - 1)
                            ext = units[layer][v % U[layer]][3]
                            nc.scalar.activation(probsT[:, 0, 0:ext], ps[6][:, 0:ext], ACT.Copy).then_inc(S["pte_act"], 1)

            def norm(n):
                for i in range(NT):
                    act.wait_ge(ln_nb, NT * n + i + 1)
                    if i >= 2:
                        act.wait_ge(ln_gain, NT * n + i - 1)
                    nc.scalar.activation(lnx[:, i % 2, :], X[:, i, :], ACT.Identity, scale=mv[:, i, 2:3],
                                         bias=mv[:, i, 3:4]).then_inc(ln_norm, 1)

            def output(layer):
                for k, j in mine(f"oT{layer}"):
                    copy(HT[:, k, :], j, bank(j)[:, :])
                norm(2 * layer)

            def route(layer):
                wait_evacuated_ada(act, layer)
                modulated(f"hf{layer}", layer, 1)
                (_, j), = mine(f"rout{layer}")
                arrived(j)
                nc.scalar.activation(rt[:, 0, :, :].rearrange("p i e -> p (i e)"), bank(j)[:, 0:NT * N_EXP],
                                     ACT.Sigmoid).then_inc(evac["A"], 1)

            def wait_evacuated_ada(eng, layer):
                wait_evacuated(eng, f"ada{layer}.2")
                wait_evacuated(eng, f"ada{layer}.1")

            def tokens_modulated(src, dst, layer, k0):
                for k in range(4):
                    last = nc.scalar.activation(dst[:, k0 + k, :], src[:, k * P:(k + 1) * P], ACT.Identity,
                                                bias=adaC[:, layer, 2, k0 + k:k0 + k + 1],
                                                scale=adaC[:, layer, 3, k0 + k:k0 + k + 1])
                return last

            def experts(layer):
                S = M[layer]

                def tokens_in(r, n):
                    act.wait_ge(S["xturn"], PRIMED + r * SLOTS + n + 1)
                    tokens_modulated(ps[0], XgT[:, n % 2], layer, 0).then_inc(S["xact"], 1)

                def hidden(r, n):
                    v = r * SLOTS + n
                    act.wait_ge(S["gu"], PRIMED + v + 1)
                    if not isinstance(v, int) or v >= 2:
                        act.wait_ge(S["hmid"], PRIMED + v - 1)
                    nc.scalar.activation(silu[:, n % 2, :], ps[2 + n % 2][:, 0:D_EXP], ACT.Silu).then_inc(S["silu"], 1)

                def step(r, n):
                    v = r * SLOTS + n
                    if not isinstance(r, int) or v + 1 < N_EXP:
                        hidden(r, n + 1)
                    act.wait_ge(S["hturn"], PRIMED + v + 1)
                    nc.scalar.activation(hmidT[:, n % 2, :, :].rearrange("p m n -> p (m n)"), ps[4 + n % 2][:, 0:2 * P],
                                         ACT.Copy).then_inc(S["hmt"], 1)
                    if not isinstance(r, int) or v + 2 < N_EXP:
                        tokens_in(r, n + 2)
                    act.wait_ge(S["down"], PRIMED + v + 1)
                    act.wait_ge(S["yfree"], PRIMED + v)
                    apart(act)
                    nc.scalar.activation(Y[:, n % 2, 0:512], ps[6][:, :], ACT.Copy,
                                         scale=by_slot[:, bass.ds(v, 1), 3:4].rearrange("p o c -> p (o c)")
                                         ).then_inc(S["yact"], 1)

                act.wait_ge(slots_ready[layer], 4)
                tokens_in(0, 0)
                hidden(0, 0)
                tokens_in(0, 1)
                with act.Fori(0, ROUNDS - 1) as r:
                    for n in range(SLOTS):
                        step(r, n)
                for n in range(SLOTS):
                    step(ROUNDS - 1, n)
                flag = act.value_load(many[0:1, layer:layer + 1], min_val=0, max_val=1)
                with act.If(flag == 1):
                    S = R_[layer]
                    with act.Fori(0, N_EXP) as e:
                        for b in range(3):
                            v = PRIMED + e * 3 + b
                            act.wait_ge(S["xturn"], v + 1)
                            tokens_modulated(ps[0], XgT[:, 0], layer, 0)
                            tokens_modulated(ps[1], XgT[:, 0], layer, 4).then_inc(S["xact"], 1)
                            act.wait_ge(S["gu"], v + 1)
                            nc.scalar.activation(silu[:, 0, :], ps[2][:, 0:D_EXP], ACT.Silu).then_inc(S["silu"], 1)
                            act.wait_ge(S["hturn"], v + 1)
                            nc.scalar.activation(hmidT[:, 0, :, :].rearrange("p m n -> p (m n)"), ps[4][:, 0:2 * P],
                                                 ACT.Copy).then_inc(S["hmt"], 1)

            attention(0)
            for c in (1, 2):
                ada_rows(1, c)
            output(0)
            route(0)
            experts(0)
            norm(1)
            for k, j in mine("xT1"):
                copy(XTk[:, k, :], j, bank(j)[:, :])
            keys_values("kv", 0)
            attention(1)
            output(1)
            route(1)
            experts(1)
            norm(3)

        @block.vector
        def _(dve):
            steps = Steps(dve, dve_step)
            link = steps.link

            def arrived(j):
                dve.wait_ge(product, j + 1)

            def mine(name):
                return [(n, j) for n, j in enumerate(stage[name]) if jobs[j] == "D"]

            def ada_sums(layer, c):
                if layer or c:
                    prev = f"ada{layer}.{c - 1}" if c else "ada0.2"
                    dve.wait_ge(product, stage[prev][-1] + 1)
                k = 0
                for q in range(3):
                    name = f"ada{layer}.{c}.{q}"
                    wait_item(dve, name)
                    w = slot(name)[:, 0:CHUNK[q] * PART].rearrange("p (k n) -> p k n", k=CHUNK[q])
                    for kk in range(CHUNK[q]):
                        if k == 0:
                            ins = nc.vector.tensor_scalar(acc, w[:, kk, :], cond[:, k:k + 1], None, ALU.mult)
                        else:
                            ins = nc.vector.scalar_tensor_tensor(acc, w[:, kk, :], cond[:, k:k + 1], acc, ALU.mult, ALU.add)
                        k += 1
                        if kk == CHUNK[q] - 1:
                            ins.then_inc(ada_sum, 1)
                            dve.wait_ge(ada_sum, 9 * layer + 3 * c + q + 1)
                        else:
                            link(ins)

            def ada_columns(layer, c):
                (_, j), = mine(f"ada{layer}.{c}")
                arrived(j)
                if c == 0:
                    nc.vector.tensor_copy(adaC[:, layer, 0, :], bank(j)[:, 0:KD])
                    ins = nc.vector.tensor_scalar(adaC[:, layer, 1, :], bank(j)[:, KD:2 * KD], 1.0, None, ALU.add)
                elif c == 1:
                    ins = nc.vector.tensor_copy(adaC[:, layer, 2, :], bank(j)[:, 0:KD])
                else:
                    ins = nc.vector.tensor_scalar(adaC[:, layer, 3, :], bank(j)[:, 0:KD], 1.0, None, ALU.add)
                ins.then_inc(evac["D"], 1)

            for (n, j), (o, w) in zip(mine("bias"), ((0, 512), (512, 128), (640, 384))):
                arrived(j)
                nc.vector.tensor_scalar(biasrow[:, o:o + w], bank(j)[0:NH, 0:w], -1.0, None, ALU.mult).then_inc(evac["D"], 1)
            for i, j in mine("biasc"):
                arrived(j)
                nc.vector.tensor_scalar(BC[:, i, :, :].rearrange("p n h -> p (n h)"), bank(j)[:, 0:NC * NH], -1.0, None,
                                        ALU.mult).then_inc(evac["D"], 1)
            for b, j in mine("pos"):
                arrived(j)
                nc.vector.tensor_copy(posT[:, b, :], bank(j)[:, 0:CK]).then_inc(evac["D"], 1)
            dve.wait_ge(small_in, 16 * 7)
            link(nc.vector.tensor_scalar(nsink[:, :], nsink[:, :], -1.0, None, ALU.mult))
            wait_evacuated(dve, "cond")
            ada_sums(0, 0)
            ada_columns(0, 0)

            def modulated(name, layer, sub):
                for k, j in mine(name):
                    arrived(j)
                    nc.vector.tensor_scalar(HT[:, k, :], bank(j)[:, :], adaC[:, layer, 2 * sub + 1, k:k + 1],
                                            adaC[:, layer, 2 * sub, k:k + 1], ALU.mult, ALU.add).then_inc(evac["D"], 1)

            def keys_values(name, b):
                for n, j in mine(name):
                    arrived(j)
                    if n < 2:
                        for half in range(2):
                            last = nc.vector.tensor_copy(KT[:, b, 2 * n + half, :], bank(j)[half * HD:(half + 1) * HD, :])
                    else:
                        last = nc.vector.tensor_copy(V[:, b, n - 2, :], bank(j)[:, 0:KVW])
                    last.then_inc(evac["D"], 1)

            wait_evacuated(dve, "ada0.0")
            modulated("hT0", 0, 0)
            for n, j in mine("kcvc"):
                arrived(j)
                split_halves(nc.vector.tensor_copy, KC2 if n < 2 else VC2, n % 2, bank(j)).then_inc(evac["D"], 1)
            ada_sums(0, 1)
            ada_columns(0, 1)
            keys_values("ksvs", 0)
            keys_values("kwvw", 1)
            ada_sums(0, 2)
            ada_columns(0, 2)
            for b, j in mine("posb"):
                arrived(j)
                nc.vector.tensor_copy(posb[:, b, :], bank(j)[:, 0:2]).then_inc(evac["D"], 1)
            (_, j), (_, jv) = mine("cmp")
            arrived(j)
            nc.vector.tensor_copy(KC[:, :, :].rearrange("p g n -> p (g n)"), bank(j)[0:HD, 0:NG * NC]).then_inc(evac["D"], 1)
            arrived(jv)
            nc.vector.tensor_copy(VC[0:NC, :], bank(jv)[0:NC, 0:KVW]).then_inc(evac["D"], 1)

            def attention(layer):
                S = A[layer]
                n_units = HPG * U[layer]
                nu = U[layer]
                per = HPG * (10 if layer == 0 else 3)
                with dve.Fori(0, NG) as g:
                    steps.enter(g, per)

                    def combine(hh):
                        h = g * HPG + hh
                        dve.wait_ge(S["pv"], PRIMED + g * n_units + (hh + 1) * nu)
                        dve.wait_ge(S["heads"], PRIMED + g * HPG + hh)
                        if layer == 1:
                            dve.wait_ge(S["cexp"], PRIMED + g * HPG + hh + 1)
                            link(nc.vector.tensor_tensor(small[:, 16:16 + nu], sums[:, hh % 2, 0:nu], sink_exp[:, hh % 2, :],
                                                         ALU.add))
                            link(nc.vector.reciprocal(small[:, 32:32 + nu], small[:, 16:16 + nu]))
                            nc.vector.tensor_tensor(osc[:, 0:nu, :],
                                                    ps[3][:, 0:nu * HD].rearrange("p (u d) -> p u d", d=HD),
                                                    small[:, 32:32 + nu].unsqueeze(2).to_broadcast([P, nu, HD]),
                                                    ALU.mult).then_inc(S["comb"], 1)
                            return
                        gates = GT[:, :, :].rearrange("p i (b h) -> p i b h", b=3)
                        rs = small[:, 0:nu].rearrange("p (i b) -> p i b", b=2)
                        link(nc.vector.reciprocal(small[:, 0:nu], sums[:, hh % 2, :]))
                        link(nc.vector.tensor_tensor(rs, rs, gates[:, :, 1:3, bass.ds(h, 1)].rearrange("p i b o -> p i (b o)"),
                                                     ALU.mult))
                        link(nc.vector.tensor_tensor(osc[:, :, :], ps[3][:, :].rearrange("p (u d) -> p u d", d=HD),
                                                     small[:, 0:nu].unsqueeze(2).to_broadcast([P, nu, HD]), ALU.mult))
                        dve.wait_ge(S["cpv"], PRIMED + g * HPG + hh + 1)
                        v = osc.rearrange("p (i b) d -> p i b d", b=2)[:, :, 0, :]
                        nc.vector.tensor_tensor(v, v, ps[0][:, 0:NT * HD].rearrange("p (i d) -> p i d", d=HD),
                                                ALU.add).then_inc(S["comb"], 1)

                    for u in range(n_units + LAG + 1):
                        hh, n = divmod(u, nu)
                        if u >= nu + LAG - 0 and (u - LAG) % nu == 0:
                            combine((u - LAG) // nu - 1)
                        if u < n_units:
                            i, b, k0, ext = units[layer][n]
                            if layer == 0 and n == 1:
                                dve.wait_ge(S["cscore"], PRIMED + g * HPG + hh + 1)
                                dve.wait_ge(S["cturn"], PRIMED + g * HPG + hh)
                                link(nc.vector.tensor_tensor(
                                    Pc[:, :, 0:NC], ps[1][:, 0:NT * NCP].rearrange("p (i n) -> p i n", i=NT)[:, :, 0:NC],
                                    BC[:, :, :, bass.ds(g * HPG + hh, 1)].rearrange("p i n o -> p i (n o)"), ALU.add))
                                link(nc.vector.tensor_reduce(small[:, 40:44], Pc[:, :, 0:NC], AX.X, ALU.min))
                                nc.vector.tensor_tensor(Pc[:, :, 0:NC], Pc[:, :, 0:NC],
                                                        small[:, 40:44].unsqueeze(2).to_broadcast([P, NT, NC]),
                                                        ALU.subtract).then_inc(S["cshift"], 1)
                            if layer == 0 and n == 3:
                                dve.wait_ge(S["cexp"], PRIMED + g * HPG + hh + 1)
                                link(nc.vector.tensor_tensor(Pc[:, :, 0:NC], Pc[:, :, 0:NC], maskc[:, :, :], ALU.mult))
                                link(nc.vector.tensor_reduce(small[:, 44:48], Pc[:, :, 0:NC], AX.X, ALU.add))
                                link(nc.vector.tensor_scalar(small[:, 48:52], small[:, 44:48], 1e-30, None, ALU.max))
                                link(nc.vector.reciprocal(small[:, 52:56], small[:, 48:52]))
                                gates = GT[:, :, :].rearrange("p i (b h) -> p i b h", b=3)
                                link(nc.vector.tensor_tensor(small[:, 56:60], small[:, 52:56],
                                                             gates[:, :, 0, bass.ds(g * HPG + hh, 1)].rearrange("p i o -> p (i o)"),
                                                             ALU.mult))
                                nc.vector.tensor_tensor(Pc[:, :, 0:NC], Pc[:, :, 0:NC],
                                                        small[:, 56:60].unsqueeze(2).to_broadcast([P, NT, NC]),
                                                        ALU.mult).then_inc(S["cprob"], 1)
                            if layer == 1 and n == 0:
                                link(nc.vector.tensor_copy(sink_now[:, hh % 2:hh % 2 + 1], nsink[:, bass.ds(g * HPG + hh, 1)]))
                            dve.wait_ge(S["score"], PRIMED + g * n_units + u + 1)
                            dve.wait_ge(S["bias_odd" if hh % 2 else "bias_even"], g * (8 * HPG) + 16 * (hh // 2 + 1))
                            if u >= 2:
                                dve.wait_ge(S["expo"], PRIMED + g * n_units + u - 1)
                            apart(dve)
                            full = units[layer][-1][3]
                            start = sink_now[:, hh % 2:hh % 2 + 1] if layer == 1 else 3.0e38
                            nc.vector.tensor_tensor_reduce(logits[:, u % 2, 0:ext], ps[4 + u % 2][:, 0:ext],
                                                           B[:, hh % 2, full - ext:full], 1.0, start, ALU.add, ALU.min,
                                                           mins[:, hh % 2, n:n + 1]).then_inc(S["logit"], 1)
                            if layer == 1 and n == NT - 1:
                                dve.wait_ge(S["logit"], PRIMED + g * n_units + u + 1)
                                nc.vector.tensor_scalar(sink_diff[:, hh % 2, :], mins[:, hh % 2, 0:NT],
                                                        sink_now[:, hh % 2:hh % 2 + 1], None,
                                                        ALU.subtract).then_inc(S["cprob"], 1)
                        v = u - LAG + 1
                        if 0 <= v < n_units and v % 2 == 1:
                            dve.wait_ge(S["turn"], PRIMED + g * n_units + v + 1)
                            if v >= 2:
                                dve.wait_ge(S["pv"], PRIMED + g * n_units + v - 1)
                            ext = units[layer][v % nu][3]
                            nc.vector.tensor_copy(probsT[:, 1, 0:ext], ps[7][:, 0:ext]).then_inc(S["pte_dve"], 1)
                steps.leave(NG)

            def residual(n, i, b, branch, src_psum):
                x = X[:, i, b * 512:(b + 1) * 512]
                y = O[:, i, b * 512:(b + 1) * 512]
                ins = nc.vector.tensor_tensor(y, branch, G[:, n // 2, n % 2, b * 512:(b + 1) * 512], ALU.mult)
                if src_psum:
                    ins.then_inc(evac["D"], 1)
                    dve.wait_ge(evac["D"], src_psum)
                else:
                    link(ins)
                link(nc.vector.scalar_tensor_tensor(x, x, ALPHA, y, ALU.mult, ALU.add))
                link(nc.vector.bn_stats(stats[:, i, b, :], x))

            def norm_stats(n, i):
                link(nc.vector.bn_aggr(mv[:, i, 0:2], stats[:, i, :, :].rearrange("p b s -> p (b s)")))
                nc.vector.tensor_scalar(mv[:, i, 1:2], mv[:, i, 1:2], LN_EPS, None, ALU.add).then_inc(ln_var, 1)

            def norm_apply(n):
                for i in range(NT):
                    dve.wait_ge(ln_rstd, NT * n + i + 1)
                    nc.vector.scalar_tensor_tensor(mv[:, i, 3:4], mv[:, i, 0:1], -1.0, mv[:, i, 2:3], ALU.mult,
                                                   ALU.mult).then_inc(ln_nb, 1)
                dve.wait_ge(ln_in, 32 * (n + 1))
                for i in range(NT):
                    dve.wait_ge(ln_norm, NT * n + i + 1)
                    nc.vector.tensor_tensor(X[:, i, :], lnx[:, i % 2, :], lng, ALU.mult).then_inc(ln_gain, 1)

            def output(layer):
                for k, j in mine(f"oT{layer}"):
                    arrived(j)
                    nc.vector.tensor_copy(HT[:, k, :], bank(j)[:, :]).then_inc(evac["D"], 1)
                wait_evacuated(dve, f"ada{layer}.1")
                js = iter(stage[f"wo{layer}"])
                for i in range(NT):
                    for b in range(2):
                        j = next(js)
                        arrived(j)
                        residual(2 * layer, i, b, bank(j)[:, :], nth[j])
                    norm_stats(2 * layer, i)
                norm_apply(2 * layer)

            def route(layer):
                wait_evacuated(dve, f"ada{layer}.1")
                modulated(f"hf{layer}", layer, 1)
                wait_evacuated(dve, f"rout{layer}")
                s, sbias, rank, tmp = (rt[:, n, :, :] for n in range(4))
                score = rt[:, 5, :, 0:NE_GRP]
                best = rt[:, 6, :, 0:1]
                free = rt[:, 7, :, 0:1]
                hit = rt[:, 8, :, 0:NE_GRP]
                pair = rt[:, 9, :, 0:NE_GRP]
                tt = nc.vector.tensor_tensor

                def member(x, a):
                    return x.rearrange("p i (g e) -> p i g e", e=EPG)[:, :, :, a]

                link(tt(sbias, s, routb[:, :].unsqueeze(1).to_broadcast([P, NT, N_EXP]), ALU.add))
                link(nc.vector.memset(rank, 0.0))
                first = True
                for a in range(EPG):
                    for b in range(a + 1, EPG):
                        if first:
                            link(tt(score, member(sbias, a), member(sbias, b), ALU.add))
                            first = False
                        else:
                            link(tt(pair, member(sbias, a), member(sbias, b), ALU.add))
                            link(tt(score, score, pair, ALU.max))
                        link(tt(pair, member(sbias, b), member(sbias, a), ALU.is_gt))
                        link(tt(member(rank, a), member(rank, a), pair, ALU.add))
                        link(nc.vector.tensor_scalar(pair, pair, -1.0, 1.0, ALU.mult, ALU.add))
                        link(tt(member(rank, b), member(rank, b), pair, ALU.add))
                link(nc.vector.tensor_reduce(best.rearrange("p i o -> p (i o)"), score, AX.X, ALU.max))
                link(nc.vector.memset(free, 1.0))
                for a in range(NE_GRP):
                    link(tt(hit[:, :, a:a + 1], score[:, :, a:a + 1], best, ALU.is_ge))
                    link(tt(hit[:, :, a:a + 1], hit[:, :, a:a + 1], free, ALU.mult))
                    link(tt(free, free, hit[:, :, a:a + 1], ALU.subtract))
                link(nc.vector.tensor_scalar(sel, rank, 2.0, None, ALU.is_lt))
                for a in range(EPG):
                    link(tt(member(sel, a), member(sel, a), hit, ALU.mult))
                link(tt(tmp, sel, s, ALU.mult))
                link(nc.vector.tensor_reduce(best.rearrange("p i o -> p (i o)"), tmp, AX.X, ALU.add))
                link(nc.vector.reciprocal(free, best))
                link(tt(moeg[:, :, :], tmp, free.to_broadcast([P, NT, N_EXP]), ALU.mult))
                dve.wait_ge(consts, 7)
                number = tcol[:, :].unsqueeze(2).to_broadcast([P, NT, N_EXP])
                link(nc.vector.memset(rank, 0.0))
                for a in range(1, EPG):
                    link(tt(member(rank, a), member(rank, a - 1), member(sel, a - 1), ALU.add))
                tt(tmp, number, number, ALU.add).then_inc(routed[layer], 1)
                dve.wait_ge(routed[layer], 1)
                link(tt(routes[:, :, :, 1], tmp, rank, ALU.add))
                link(nc.vector.tensor_copy(routes[:, :, :, 0], number))
                link(nc.vector.memset(routes[:, :, :, 2], 1.0))
                link(nc.vector.tensor_copy(routes[:, :, :, 3], moeg[:, :, :]))
                j, = stage[f"place{layer}"]
                arrived(j)
                link(nc.vector.tensor_reduce(more[:, 0:1], bank(j)[:, NT * N_EXP:(NT + 1) * N_EXP], AX.X, ALU.max))
                nc.vector.scalar_tensor_tensor(place[:, :, :], bank(j)[:, 0:NT * N_EXP].rearrange("p (i e) -> p i e", i=NT),
                                               1.0, sel, ALU.add, ALU.mult).then_inc(evac["D"], 1)
                dve.wait_ge(evac["D"], nth[j])
                link(nc.vector.tensor_scalar(place[:, :, :], place[:, :, :], -1.0, None, ALU.add))
                link(nc.vector.tensor_scalar(many[:, layer:layer + 1], more[:, 0:1], float(P), None, ALU.is_gt))

                def collect(q):
                    j = stage[f"slots{layer}"][q]
                    arrived(j)
                    es = slice(q * EPG, (q + 1) * EPG)
                    nc.vector.tensor_copy(by_slot[:, es, :], bank(j)[:, 0:4 * EPG].rearrange("p (e c) -> p e c", c=4)
                                          ).then_inc(evac["D"], 1)
                    dve.wait_ge(evac["D"], nth[j])
                    link(nc.vector.tensor_scalar(more[:, 0:EPG], by_slot[:, es, 2], -NOWHERE, NOWHERE, ALU.mult, ALU.add))
                    link(tt(slot_rows[:, 0, es], by_slot[:, es, 0], more[:, 0:EPG], ALU.add))
                    tt(slot_rows[:, 1, es], by_slot[:, es, 1], more[:, 0:EPG], ALU.add).then_inc(slots_ready[layer], 1)
                    dve.wait_ge(slots_ready[layer], q + 1)

                for q in range(NE_GRP):
                    if q >= 2:
                        arrived(stage[f"slots{layer}"][q - 2])
                    for e in range(EPG):
                        last = tt(onehot[:, q % 2, e, :, :], row[:, :].unsqueeze(1).to_broadcast([P, NT, P]),
                                  place[:, :, q * EPG + e].unsqueeze(2).to_broadcast([P, NT, P]), ALU.is_equal)
                    last.then_inc(onehot_ready[layer], 1)
                    if q:
                        collect(q - 1)
                collect(NE_GRP - 1)

            def experts(layer):
                S = M[layer]

                def tokens_in(r, n):
                    dve.wait_ge(S["xturn"], PRIMED + r * SLOTS + n + 1)
                    for k in range(4, KD):
                        last = nc.vector.tensor_scalar(XgT[:, n % 2, k, :], ps[1][:, (k - 4) * P:(k - 3) * P],
                                                       adaC[:, layer, 3, k:k + 1], adaC[:, layer, 2, k:k + 1],
                                                       ALU.mult, ALU.add)
                    last.then_inc(S["xdve"], 1)

                def hidden(r, n):
                    v = r * SLOTS + n
                    dve.wait_ge(S["silu"], PRIMED + v + 1)
                    if not isinstance(v, int) or v >= 2:
                        dve.wait_ge(S["hturn"], PRIMED + v - 1)
                    nc.vector.tensor_tensor(hmid[:, n % 2, :], silu[:, n % 2, :], ps[2 + n % 2][:, D_EXP:2 * D_EXP],
                                            ALU.mult).then_inc(S["hmid"], 1)

                def step(r, n):
                    v = r * SLOTS + n
                    if not isinstance(r, int) or v + 1 < N_EXP:
                        hidden(r, n + 1)
                    if not isinstance(r, int) or v + 2 < N_EXP:
                        tokens_in(r, n + 2)
                    dve.wait_ge(S["down"], PRIMED + v + 1)
                    dve.wait_ge(S["yfree"], PRIMED + v)
                    nc.vector.tensor_scalar(Y[:, n % 2, 512:1024], ps[7][:, :],
                                            by_slot[:, bass.ds(v, 1), 3:4].rearrange("p o c -> p (o c)"), None,
                                            ALU.mult).then_inc(S["ydve"], 1)

                tokens_in(0, 0)
                hidden(0, 0)
                tokens_in(0, 1)
                with dve.Fori(0, ROUNDS - 1) as r:
                    for n in range(SLOTS):
                        step(r, n)
                for n in range(SLOTS):
                    step(ROUNDS - 1, n)
                flag = dve.value_load(many[0:1, layer:layer + 1], min_val=0, max_val=1)
                with dve.If(flag == 1):
                    more_tokens(layer)
                n = 2 * layer + 1
                for i in range(NT):
                    dve.wait_ge(answers_in[layer], 32 * NT)
                    link(nc.vector.tensor_tensor(O[:, i, :], O[:, i, :], Y1[:, i, :], ALU.add))
                    for b in range(2):
                        residual(n, i, b, O[:, i, b * 512:(b + 1) * 512], 0)
                    norm_stats(n, i)
                norm_apply(n)

            def more_tokens(layer):
                S = R_[layer]
                step_of_mine = more_step[layer]
                with dve.Fori(0, N_EXP) as e:
                    for b in range(3):
                        v = PRIMED + e * 3 + b
                        m = e * 9 + 3 * b
                        dve.wait_ge(S["free"], v)
                        nc.vector.tensor_scalar(more[:, 0:NT], place[:, :, bass.ds(e, 1)].rearrange("p i o -> p (i o)"),
                                                float(-P * (b + 1)), None, ALU.add).then_inc(step_of_mine, 1)
                        dve.wait_ge(step_of_mine, m + 1)
                        nc.vector.tensor_tensor(onehot[:, 0, 0, :, :], row[:, :].unsqueeze(1).to_broadcast([P, NT, P]),
                                                more[:, 0:NT].unsqueeze(2).to_broadcast([P, NT, P]),
                                                ALU.is_equal).then_inc(S["onehot"], 1)
                        dve.wait_ge(S["slots"], v + 1)
                        nc.vector.tensor_copy(more[:, 0:4], ps[5][:, 0:4]).then_inc(step_of_mine, 1)
                        dve.wait_ge(step_of_mine, m + 2)
                        nc.vector.tensor_scalar(more[:, 4:5], more[:, 2:3], -NOWHERE, NOWHERE, ALU.mult, ALU.add).then_inc(step_of_mine, 1)
                        dve.wait_ge(step_of_mine, m + 3)
                        nc.vector.tensor_tensor(more_rows[:, :], more[:, 0:2], more[:, 4:5].to_broadcast([P, 2]), ALU.add)\
                            .then_inc(S["rows"], 1)
                        dve.wait_ge(S["silu"], v + 1)
                        nc.vector.tensor_tensor(hmid[:, 0, :], silu[:, 0, :], ps[2][:, D_EXP:2 * D_EXP], ALU.mult)\
                            .then_inc(S["hmid"], 1)
                        dve.wait_ge(S["down"], v + 1)
                        for h in range(2):
                            last = nc.vector.tensor_scalar(Y[:, 0, h * 512:(h + 1) * 512], ps[6 + h][:, :], more[:, 3:4], None,
                                                           ALU.mult)
                        last.then_inc(S["y"], 1)
                dve.wait_ge(S["scatter"], 16 * 3 * N_EXP)

            dve.wait_ge(consts, 4)
            attention(0)
            dve.wait_ge(A[0]["heads"], PRIMED + NH)
            for c in range(3):
                ada_sums(1, c)
                ada_columns(1, c)
            output(0)
            route(0)
            experts(0)
            for k, (n, j) in enumerate([(n, j) for n, j in enumerate(stage["xT1"])]):
                dve.wait_ge(evac["A"], nth[j])
                nc.vector.tensor_scalar(HT[:, k, :], XTk[:, k, :], adaC[:, 1, 1, k:k + 1], adaC[:, 1, 0, k:k + 1],
                                        ALU.mult, ALU.add).then_inc(hT1_ready, 1)
            keys_values("kv", 0)
            attention(1)
            output(1)
            route(1)
            experts(1)


def win_gates(t):
    return t["nsa_w_in"][0][:, QW + 6 * KVW:NSA_IN].rearrange("(k p) n -> p k n", p=P)


def split_halves(copy, dst, m, src):
    for half in range(2):
        for odd in range(2):
            last = copy(dst[odd * HD:(odd + 1) * HD, 2 * m + half, :], src[half * HD:(half + 1) * HD, odd::2])
    return last


_INS = ["x", "c", "nsa_w_in", "cmp_k_w1", "cmp_k_w2", "cmp_v_w1", "cmp_v_w2", "cmp_k_pos", "cmp_v_pos", "nsa_w_out",
        "swa_w_q", "swa_sinks", "swa_w_out", "shared_w_kv", "rel_bias", "router_w", "router_b", "moe_w_gate",
        "moe_w_up", "moe_w_down", "ada_w", "ada_b", "ln_g", "ln_b"]


def kernel(**inputs):
    import concourse.bacc as bacc
    from concourse.bass_utils import run_bass_kernel_spmd

    nc = bacc.Bacc("TRN2", target_bir_lowering=False, num_devices=1)
    arrays, tensors = {}, {}
    for name, a in [(n, np.ascontiguousarray(inputs[n])) for n in _INS] + [("buckets", bucket_rows())]:
        arrays[f"in_{name}"] = a
        tensors[name] = nc.dram_tensor(f"in_{name}", a.shape, F32, kind="ExternalInput").ap()
    tensors["out"] = nc.dram_tensor("out", (1, T, D), F32, kind="ExternalOutput").ap()
    build(nc, tensors)
    r = run_bass_kernel_spmd(nc, [arrays], core_ids=[0])
    return r.results[0]["out"]
```

```python
from contextlib import ExitStack

import concourse.bass as bass
import numpy as np
from concourse import mybir

F32 = mybir.dt.float32
U32 = mybir.dt.uint32
ALU = mybir.AluOpType
ACT = mybir.ActivationFunctionType
AX = mybir.AxisListType

P = 128
D = 1024
T = 512
KD = D // P
NT = T // P
NH, NG, HD = 16, 4, 64
HPG = NH // NG
QW, KVW = NH * HD, NG * HD
NSA_IN = QW + 6 * KVW + 3 * NH
CMP_LEN, CMP_STRIDE, CMP_HIDDEN = 32, 16, 256
NC = T // CMP_STRIDE - 1
NCP = NC + 1
CK = CMP_LEN * HD // P
N_EXP, D_EXP = 16, 256
EPG = 4
NE_GRP = N_EXP // EPG
BUCKETS, MAX_DIST = 32, 128
WINDOW = 128
ALPHA = 4.0 ** 0.25
LN_EPS = 1e-5
SCALE = HD ** -0.5
MASKED = 1e30
NOWHERE = 65536.0
PART = 2048
SLOT = 6144
RING = 3


def bucket_rows():
    def one_hot(dist, valid):
        d = np.maximum(dist, 0)
        half = BUCKETS // 2
        large = half + (np.log(np.maximum(d, 1).astype(np.float32) / np.float32(half))
                        / np.float32(np.log(MAX_DIST / half)) * np.float32(half)).astype(np.int32)
        b = np.where(d < half, d, np.minimum(large, BUCKETS - 1))
        b = np.where(valid, b, BUCKETS)
        return (np.arange(BUCKETS + 1)[:, None] == b[None, :]).astype(np.float32)

    back = T - 1 - np.arange(640)
    near = 2 * WINDOW - 1 - np.arange(384)
    ahead = np.arange(1024) - T
    return np.concatenate([one_hot(back, back >= 0), one_hot(near, (near >= 0) & (near < WINDOW)),
                           one_hot(ahead, ahead >= 0)], axis=1)


BACK, NEAR, AHEAD = 0, 640, 1024


class Steps:

    def __init__(self, eng, sem):
        self.eng, self.sem, self.n, self.extra = eng, sem, 0, None

    def mark(self, ins):
        ins.then_inc(self.sem, 1)
        self.n += 1

    def wait(self):
        self.eng.wait_ge(self.sem, self.n if self.extra is None else self.extra + self.n)

    def link(self, ins):
        self.mark(ins)
        self.wait()

    def enter(self, it, per):
        self.extra, self.n0, self.per = it * per, self.n, per

    def leave(self, rounds):
        assert self.n - self.n0 == self.per, (self.n - self.n0, self.per)
        self.extra, self.n = None, self.n0 + rounds * self.per


def build(nc, t):
    with ExitStack() as ctx:
        def sb(name, shape):
            return ctx.enter_context(nc.sbuf_tensor(name, shape, F32))

        def sem(name):
            return ctx.enter_context(nc.semaphore(name))

        X = sb("X", [P, NT, D])
        XT = sb("XT", [P, KD * T])
        HT = sb("HT", [P, KD, T])
        O = sb("O", [P, NT, D])
        ring = sb("ring", [P, RING, SLOT])
        KTV = sb("KTV", [P, SLOT])
        G = sb("G", [P, 2, 2, D])
        WORK = sb("WORK", [P, 6144])
        ident = sb("ident", [P, P])
        ones = sb("ones", [P, P])
        cond = sb("cond", [P, KD])
        adaC = sb("adaC", [P, 2, 4, KD])
        GT = sb("GT", [P, NT, 3 * NH])
        routw = sb("routw", [P, KD, N_EXP])
        routb = sb("routb", [P, N_EXP])
        KC = sb("KC", [HD, NG, NC])
        VC = sb("VC", [NCP, KVW])
        maskc = sb("maskc", [P, NT, NC])
        nsink = sb("nsink", [P, NH])
        sums = sb("sums", [P, 2, 8])
        mins = sb("mins", [P, 2, 8])
        small = sb("small", [P, 64])
        moeg = sb("moeg", [P, NT, N_EXP])
        stats = sb("stats", [P, NT, 2, 6])
        mv = sb("mv", [P, NT, 4])
        nhalf = sb("nhalf", [P, 1])
        relb = sb("relb", [BUCKETS + 1, NH])
        upper = sb("upper", [P, P])
        row = sb("row", [P, P])
        tcol = sb("tcol", [P, NT])
        slot_rows = ctx.enter_context(nc.sbuf_tensor("slot_rows", [P, 2, N_EXP], U32))
        many = ctx.enter_context(nc.sbuf_tensor("many", [P, 2], U32))
        more = small[:, 20:28]
        more_rows = ctx.enter_context(nc.sbuf_tensor("more_rows", [P, 2], U32))
        w2 = sb("w2", [P, 2, 2, HD])

        BC = XT[:, 0:NT * NC * NH].rearrange("p (i n h) -> p i n h", i=NT, n=NC)
        acc = XT[:, PART:2 * PART]
        acc_rest = ring[:, 2, PART:SLOT]
        acc_next = ring[:, 0, :]
        PcT = XT[0:NCP, PART:PART + T]
        Pc = XT[:, PART + T:PART + T + P].rearrange("p (i n) -> p i n", i=NT)
        osc = XT[:, PART + 2 * T:PART + 3 * T].rearrange("p (u d) -> p u d", d=HD)
        XTk = XT[:, :].rearrange("p (k t) -> p k t", k=KD)
        OH = O[0:BUCKETS + 1, 0:2, :].rearrange("p a n -> p (a n)")
        KC2 = O[:, 2, :].rearrange("p (g u) -> p g u", g=NG)
        VC2 = O[:, 3, :].rearrange("p (g u) -> p g u", g=NG)
        KT = KTV[0:HD, 0:2 * NG * T].rearrange("p (b g t) -> p b g t", b=2, g=NG)
        V = KTV[:, 2 * NG * T:].rearrange("p (b i n) -> p b i n", b=2, i=NT)
        logits = WORK[:, 0:1024].rearrange("p (b n) -> p b n", b=2)
        probs = WORK[:, 1024:2048].rearrange("p (b n) -> p b n", b=2)
        probsT = WORK[:, 2048:3072].rearrange("p (b n) -> p b n", b=2)
        QT = WORK[0:HD, 3072:5120].rearrange("p (h t) -> p h t", h=HPG)
        B = WORK[:, 5120:6144].rearrange("p (b n) -> p b n", b=2)
        glw = WORK[:, 3072:3072 + KD * 3 * NH].rearrange("p (k n) -> p k n", k=KD)
        posT = WORK[:, 3584:3584 + 2 * CK].rearrange("p (b k) -> p b k", b=2)
        posb = WORK[:, 3648:3648 + 4].rearrange("p (b m) -> p b m", b=2)
        hid = WORK[:, 4096:4096 + 4 * P].rearrange("p (b m n) -> p b m n", b=2, m=2)
        c8 = WORK[0:KD, 4608:4608 + P]
        pos16 = WORK[0:CK, 4736:4736 + 2 * P].rearrange("p (b n) -> p b n", b=2)
        biasrow = WORK[0:NH, 5120:6144]
        sink_now = small[:, 62:64]
        sink_diff = small[:, 0:8].rearrange("p (b i) -> p b i", b=2)
        sink_exp = small[:, 8:16].rearrange("p (b i) -> p b i", b=2)
        lng, lnb = XT[:, 0:D], XT[:, D:2 * D]
        lnx = XT[:, 2 * D:4 * D].rearrange("p (b n) -> p b n", b=2)
        Xg = WORK[:, 0:2 * D].rearrange("p (b n) -> p b n", b=2)
        XgT = HT[:, 0:4, :].rearrange("p a n -> p (a n)").rearrange("p (b k s) -> p b k s", b=2, k=KD)
        hmidT = HT[:, 4, :].rearrange("p (b m s) -> p b m s", b=2, m=2)
        routes = HT[:, 5, 0:NT * N_EXP * 4].rearrange("p (i e c) -> p i e c", i=NT, e=N_EXP)
        place = HT[:, 5, 256:256 + NT * N_EXP].rearrange("p (i e) -> p i e", i=NT)
        by_slot = HT[:, 5, 320:320 + 4 * N_EXP].rearrange("p (e c) -> p e c", c=4)
        Y = WORK[:, 2 * D:4 * D].rearrange("p (b n) -> p b n", b=2)
        silu = WORK[:, 5120:5632].rearrange("p (b n) -> p b n", b=2)
        hmid = WORK[:, 5632:6144].rearrange("p (b n) -> p b n", b=2)
        Y1 = HT[:, :, :].rearrange("p k t -> p (k t)").rearrange("p (i n) -> p i n", i=NT)
        onehot = O[:, :, :].rearrange("p i n -> p (i n)").rearrange("p (q e i s) -> p q e i s", q=2, e=EPG, i=NT)
        rt = WORK[:, 4096:4096 + 1024].rearrange("p (s i e) -> p s i e", s=16, i=NT)
        sel = rt[:, 4, :, :]

        ps = [ctx.enter_context(nc.psum_tensor(f"ps{i}", [P, 512], F32)) for i in range(8)]
        JB = 4

        scratch_back = nc.dram_tensor("scratch_back", [NH, 640], F32, kind="Internal").ap()
        scratch_near = nc.dram_tensor("scratch_near", [NH, 384], F32, kind="Internal").ap()
        bias_back = nc.dram_tensor("bias_back", [NH, P, T], F32, kind="Internal").ap()
        bias_near = nc.dram_tensor("bias_near", [NH, P, 2 * WINDOW], F32, kind="Internal").ap()
        tokens = [nc.dram_tensor(f"tokens{n}", [T, D], F32, kind="Internal").ap() for n in range(2)]
        answers = [nc.dram_tensor(f"answers{n}", [2 * T, D], F32, kind="Internal").ap() for n in range(2)]

        jobs, stage = [], {}

        def plan(name, engines):
            stage[name] = range(len(jobs), len(jobs) + len(engines))
            jobs.extend(engines)

        plan("cond", "A")
        plan("bias", "DDD")
        plan("biasc", "ADAD")
        plan("pos", "AD")
        for layer in range(2):
            if layer == 0:
                plan("ada0", "D")
                plan("hT0", "ADADADAD")
                plan("kcvc", "ADAD")
                plan("ksvs", "ADADAD")
                plan("kwvw", "ADADAD")
                plan("gl", "A")
                plan("posb", "DD")
                plan("hid", "AAAA")
                plan("cmp", "DD")
                plan("rest", "DAAAA")
            else:
                plan("xT1", "AAAAAAAA")
                plan("kv", "ADADAD")
            plan(f"oT{layer}", "ADADADAD")
            plan(f"wo{layer}", "D" * 8)
            if layer == 0:
                plan("next", "DAAAA")
            plan(f"hf{layer}", "ADADADAD")
            plan(f"rout{layer}", "A")
            plan(f"place{layer}", "D")
            plan(f"slots{layer}", "DDDD")
        product = sem("product")
        evac = {"A": sem("evac_act"), "D": sem("evac_dve")}
        nth = [jobs[:j + 1].count(jobs[j]) for j in range(len(jobs))]

        def bank(j):
            return ps[j % JB]

        def wait_bank(eng, j):
            if j >= JB:
                eng.wait_ge(evac[jobs[j - JB]], nth[j - JB])

        def wait_evacuated(eng, name, last=None):
            js = list(stage[name])[:last]
            for e in "AD":
                own = [nth[j] for j in js if jobs[j] == e]
                if own:
                    eng.wait_ge(evac[e], own[-1])

        loaded = [0] * (RING + 1)
        items = {}

        def item(name, slot, rounds=1):
            items[name] = (slot, loaded[slot])
            loaded[slot] += 16 * rounds

        first_items = [f"ada{q}" for q in range(3)] + ["kcvc", "ksvs", "kwvw", "w1k", "w1v"]
        for n, name in enumerate(first_items):
            item(name, n % RING)
        item("wq0", 2, NG)
        item("late", 1, NH)
        item("wo0.0", 3)
        item("wo0.1", 1)
        SLOTS = RING + 1
        ROUNDS = N_EXP // SLOTS
        before_experts = {0: list(loaded)}
        for n in range(SLOTS):
            loaded[n] += 48 * ROUNDS
        item("wkv", 0)
        item("wq1", 1, NG)
        item("wo1.0", 2)
        item("wo1.1", 0)
        before_experts[1] = list(loaded)

        landed = [sem(f"landed{s}") for s in range(RING + 1)]

        def slot(name):
            s = items[name][0]
            return ring[:, s, :] if s < RING else KTV[:, :]

        def wait_item(eng, name):
            s, before = items[name]
            eng.wait_ge(landed[s], before + 16)

        x_in, c_in, small_in, oh_in, acc_zero, acc_bias, gl_in, ln_in = map(sem, (
            "x_in", "c_in", "small_in", "oh_in", "acc_zero", "acc_bias", "gl_in", "ln_in"))
        consts, rel_ready, vrow_ready, vrow_out, toeplitz = map(sem, (
            "consts", "rel_ready", "vrow_ready", "vrow_out", "toeplitz"))
        ada_sum = sem("ada_sum")
        late_sum = sem("late_sum")
        dve_step, act_step, pool_step = sem("dve_step"), sem("act_step"), sem("pool_step")
        names = ("qproj qt bias_even bias_odd score logit expo turn pte_act pte_dve pv cscore cshift cexp cprob cturn "
                 "cpt cpv comb heads").split()
        A = [{n: sem(f"{n}{layer}") for n in names} for layer in range(2)]
        mnames = "xturn xact xdve gu silu hmid hturn hmt down yact ydve yfree".split()
        M = [{n: sem(f"m_{n}{layer}") for n in mnames} for layer in range(2)]
        PRIMED = 1
        ln_var, ln_rstd, ln_nb, ln_norm, ln_gain, ln_done = (
            sem(f"ln_{n}") for n in ("var", "rstd", "nb", "norm", "gain", "done"))
        routed = [sem(f"routed{n}") for n in range(2)]
        onehot_ready = [sem(f"onehot{n}") for n in range(2)]
        slots_ready = [sem(f"slots_ready{n}") for n in range(2)]
        tokens_out = [sem(f"tokens_out{n}") for n in range(2)]
        gathered = [[sem(f"gathered{n}{b}") for b in range(2)] for n in range(2)]
        scattered = [[sem(f"scattered{n}{b}") for b in range(2)] for n in range(2)]
        answers_in = [sem(f"answers_in{n}") for n in range(2)]
        rnames = "w onehot rows slots gather xturn xact gu silu hmid hturn hmt down y scatter free".split()
        R_ = [{n: sem(f"r_{n}{layer}") for n in rnames} for layer in range(2)]
        more_step = [sem(f"more_step{n}") for n in range(2)]
        WS = [[2, 0, 1, 3], [3, 1, 2, 0]]
        stored = sem("stored")
        hT1_ready = sem("hT1_ready")

        def expert_slot(layer, n):
            s = WS[layer][n % SLOTS]
            return ring[:, s, :] if s < RING else KTV[:, :]

        def gate_up(w):
            return w[:, 0:4096].rearrange("p (b k n) -> p k b n", b=2, k=KD)

        def down(w):
            return w[:, 4096:6144].rearrange("p (k n) -> p k n", k=2)

        def apart(eng):
            eng.nop(nofuse=True)

        CHUNK = [3, 3, 2]

        U = [2 * NT, NT]
        ORDER = (3, 0, 2, 1)
        units = [[(i, b, 0, P * (i + 1)) for b in range(2) for i in ORDER],
                 [(i, 0, P * max(i - 1, 0), P * min(i + 1, 2)) for i in range(NT)]]
        BRANCHES = [2, 1]
        WIDEST = [T, 2 * WINDOW]
        LAG = 3

        block = ctx.enter_context(nc.Block())

        @block.sync
        def _(sp):
            def load(name, dst, src, after=None):
                if after is not None:
                    for s, v in after:
                        sp.wait_ge(s, v)
                sp.dma_start(dst, src).then_inc(landed[items[name][0]], 16)

            def ada_item(q, after):
                k0, n = sum(CHUNK[:q]), CHUNK[q]
                name = f"ada{q}"
                load(name, slot(name)[:, 0:n * PART].rearrange("p (k n) -> p k n", k=n),
                     t["ada_w"][0, k0 * P:(k0 + n) * P, 0:PART].rearrange("(k p) n -> p k n", p=P), after)

            def matrix(name, src, after):
                k, n = src.shape[0] // P, src.shape[1]
                load(name, slot(name)[:, 0:k * n].rearrange("p (k n) -> p k n", k=k),
                     src.rearrange("(k p) n -> p k n", p=P), after)

            def used(names):
                out = []
                for n in names:
                    if isinstance(n, tuple):
                        out.append(n)
                    else:
                        out.append((product, stage[n][-1] + 1))
                return out

            for sems in A + M + R_:
                for n, primed in sems.items():
                    if n not in ("bias_even", "bias_odd", "w", "gather", "scatter"):
                        sp.sem_inc(primed, PRIMED)
            sp.dma_start(c8, t["c"].rearrange("o (k p) -> (o k) p", p=P)).then_inc(c_in, 16)
            sp.sem_inc(late_sum, PRIMED)
            win = t["nsa_w_in"][0]
            c0 = QW
            release = {f"ada{q}": [(ada_sum, q + 1)] for q in range(3)}
            release |= {"kcvc": used(["kcvc"]), "ksvs": used(["ksvs"]), "kwvw": used(["kwvw"])}
            for n, name in enumerate(first_items):
                after_ = release[first_items[n - RING]] if n >= RING else None
                if name.startswith("ada"):
                    ada_item(int(name[3]), after_)
                elif name in ("kcvc", "ksvs", "kwvw"):
                    b = {"kcvc": 0, "ksvs": 1, "kwvw": 2}[name]
                    matrix(name, win[:, c0 + 2 * b * KVW:c0 + 2 * (b + 1) * KVW], after_)
                else:
                    matrix(name, t["cmp_k_w1" if name == "w1k" else "cmp_v_w1"][0], after_)
                if name == "ada0":
                    sp.wait_ge(acc_zero, 1)
                    sp.dma_start(acc[0:1, :], t["ada_b"][0:1, 0:PART]).then_inc(acc_bias, 16)
                if name == "ada2":
                    sp.dma_start(X[:, :, :], t["x"].rearrange("o (i p) n -> p (o i) n", p=P)).then_inc(x_in, 16)

            def attention_loads(layer, first=0, last=NG, late=None):
                S = A[layer]
                wq = win[:, 0:QW] if layer == 0 else t["swa_w_q"][0]
                name = f"wq{layer}"
                dst = slot(name)[:, 0:KD * KVW].rearrange("p (k n) -> p k n", k=KD)
                width = WIDEST[layer]
                table = bias_back if layer == 0 else bias_near
                with sp.Fori(first, last) as g:
                    sp.wait_ge(S["qproj"], PRIMED + g * 2)
                    sp.dma_start(dst, wq[:, bass.ds(g * KVW, KVW)].rearrange("(k p) n -> p k n", p=P))\
                        .then_inc(landed[items[name][0]], 16)
                    for hh in range(HPG):
                        if hh >= 2:
                            sp.wait_ge(S["logit"], PRIMED + g * (HPG * U[layer]) + (hh - 1) * U[layer])
                        else:
                            sp.wait_ge(S["logit"], PRIMED + g * (HPG * U[layer]))
                        sp.dma_start(B[:, hh % 2, 0:width],
                                     table[bass.ds(g * HPG + hh, 1)].rearrange("o p n -> p (o n)"))\
                            .then_inc(S["bias_odd" if hh % 2 else "bias_even"], 16)
                        if late is not None:
                            sp.wait_ge(late_sum, PRIMED + g * HPG + hh)
                            k = g * HPG + (hh - first * HPG)
                            w = t["ada_w"][late].rearrange("(k p) n -> p k n", p=P)
                            o = PART if late == 0 else 0
                            sp.dma_start(slot("late")[:, o:], w[:, bass.ds(k, 1), o:].rearrange("p o n -> p (o n)"))\
                                .then_inc(landed[items["late"][0]], 16)

            sp.wait_ge(toeplitz, 32)
            sp.wait_ge(product, stage["cmp"][-1] + 1)
            for e in "AD":
                sp.wait_ge(evac[e], max(nth[j] for j in range(stage["cmp"][-1] + 1) if jobs[j] == e))
            for dst, layer, o, n in ((acc_rest, 0, PART, 2), (acc_next, 1, 0, 3)):
                sp.wait_ge(acc_zero, n)
                sp.dma_start(dst[0:1, :], t["ada_b"][layer:layer + 1, o:]).then_inc(acc_bias, 16)
            attention_loads(0, 0, NG // 2, late=0)
            attention_loads(0, NG // 2, NG, late=1)
            sp.wait_ge(late_sum, PRIMED + NH)
            matrix("wo0.1", t["nsa_w_out"][0][:, 512:1024], None)
            sp.wait_ge(A[0]["heads"], PRIMED + NH)
            matrix("wo0.0", t["nsa_w_out"][0][:, 0:512], None)

            def norm_params(n):
                layer, sub = n // 2, n % 2
                sp.dma_start(lng, t["ln_g"][layer, sub:sub + 1, :].to_broadcast([P, D])).then_inc(ln_in, 16)
                sp.dma_start(lnb, t["ln_b"][layer, sub:sub + 1, :].to_broadcast([P, D])).then_inc(ln_in, 16)

            def expert_load(layer, dst, e, done):
                for j, w in enumerate(("moe_w_gate", "moe_w_up")):
                    sp.dma_start(dst[:, j * 2048:(j + 1) * 2048].rearrange("p (k n) -> p k n", k=KD),
                                 t[w][layer][bass.ds(e, 1)].rearrange("o (k p) n -> p (o k) n", p=P)).then_inc(done, 16)
                sp.dma_start(down(dst), t["moe_w_down"][layer][bass.ds(e, 1)].rearrange("o (k p) n -> p (o k) n", p=P))\
                    .then_inc(done, 16)

            def expert_loads(layer):
                with sp.Fori(1, ROUNDS) as r:
                    for n in range(SLOTS):
                        sp.wait_ge(M[layer]["down"], PRIMED + r * SLOTS + (n + 1 - SLOTS))
                        expert_load(layer, expert_slot(layer, n), r * SLOTS + n, landed[WS[layer][n]])

            def more_loads(layer):
                with sp.Fori(0, N_EXP) as e:
                    sp.wait_ge(R_[layer]["down"], PRIMED + e * 3)
                    expert_load(layer, ring[:, 0, :], e, R_[layer]["w"])

            def answers_back(layer):
                for b in range(2):
                    sp.wait_ge(scattered[layer][b], 16 * N_EXP // 2)
                src = answers[layer].rearrange("(i p r) n -> p i r n", p=P, r=2)
                for i in range(NT):
                    sp.dma_start(O[:, i, :], src[:, i, 0, :]).then_inc(answers_in[layer], 16)
                    sp.dma_start(Y1[:, i, :], src[:, i, 1, :]).then_inc(answers_in[layer], 16)

            def general(layer):
                sp.wait_ge(M[layer]["down"], PRIMED + N_EXP)
                sp.wait_ge(slots_ready[layer], 4)
                flag = sp.value_load(many[0:1, layer:layer + 1], min_val=0, max_val=1)
                with sp.If(flag == 1):
                    more_loads(layer)
                    sp.wait_ge(R_[layer]["scatter"], 16 * 3 * N_EXP)

            def first_expert(layer, n):
                expert_load(layer, expert_slot(layer, n), n, landed[WS[layer][n]])

            norm_params(0)
            sp.wait_ge(product, stage["rest"][-1] + 1)
            first_expert(0, 0)
            sp.wait_ge(product, stage["next"][-1] + 1)
            first_expert(0, 1)
            for n in (2, 3):
                first_expert(0, n)
            for i in range(NT):
                sp.wait_ge(ln_done, 0 * NT + i + 1)
                sp.dma_start(tokens[0][i * P:(i + 1) * P, :], X[:, i, :]).then_inc(tokens_out[0], 16)
            norm_params(1)
            expert_loads(0)
            general(0)
            answers_back(0)
            matrix("wkv", t["shared_w_kv"], None)
            attention_loads(1)
            matrix("wo1.0", t["swa_w_out"][0][:, 0:512], None)
            matrix("wo1.1", t["swa_w_out"][0][:, 512:1024], [(product, stage["kv"][-1] + 1)])
            sp.wait_ge(A[1]["heads"], PRIMED + NH)
            sp.wait_ge(A[1]["pv"], PRIMED + NH * U[1])
            norm_params(2)
            first_expert(1, 0)
            first_expert(1, 1)
            sp.wait_ge(product, stage["wo1"][-1] + 1)
            for n in (2, 3):
                first_expert(1, n)
            for i in range(NT):
                sp.wait_ge(ln_done, 2 * NT + i + 1)
                sp.dma_start(tokens[1][i * P:(i + 1) * P, :], X[:, i, :]).then_inc(tokens_out[1], 16)
            norm_params(3)
            expert_loads(1)
            general(1)
            answers_back(1)
            for i in range(NT):
                sp.wait_ge(ln_done, 3 * NT + i + 1)
                sp.dma_start(t["out"][0, i * P:(i + 1) * P, :], X[:, i, :]).then_inc(stored, 16)
            sp.wait_ge(stored, 16 * NT)

        @block.gpsimd
        def _(pool):
            steps = Steps(pool, pool_step)
            nc.gpsimd.memset(ones[:, :], 1.0).then_inc(consts, 1)
            nc.gpsimd.memset(nhalf[:, :], -0.5).then_inc(consts, 1)
            steps.link(nc.gpsimd.memset(ident[:, :], 0.0))
            nc.gpsimd.affine_select(out=ident[:, :], in_=ident[:, :], compare_op=ALU.not_equal, fill=1.0, base=0,
                                    pattern=[[-1, P]], channel_multiplier=1).then_inc(consts, 1)
            steps.link(nc.gpsimd.memset(maskc[:, :, :], 1.0))
            nc.gpsimd.affine_select(out=maskc[:, :, :], in_=maskc[:, :, :], compare_op=ALU.is_ge, fill=0.0,
                                    base=1 - CMP_LEN, pattern=[[P, NT], [-CMP_STRIDE, NC]],
                                    channel_multiplier=1).then_inc(consts, 1)
            steps.link(nc.gpsimd.memset(relb[:, :], MASKED * -1.0))
            steps.link(nc.gpsimd.memset(upper[:, :], 1.0))
            nc.gpsimd.affine_select(out=upper[:, :], in_=upper[:, :], compare_op=ALU.is_gt, fill=0.0, base=0,
                                    pattern=[[1, P]], channel_multiplier=-1).then_inc(consts, 1)
            nc.gpsimd.iota(row[:, :], pattern=[[1, P]], base=0, channel_multiplier=0,
                           allow_small_or_imprecise_dtypes=True).then_inc(consts, 1)
            nc.gpsimd.iota(tcol[:, :], pattern=[[P, NT]], base=0, channel_multiplier=1,
                           allow_small_or_imprecise_dtypes=True).then_inc(consts, 1)
            pool.dma_start(relb[0:BUCKETS, :], t["rel_bias"]).then_inc(rel_ready, 16)
            pool.dma_start(OH, t["buckets"]).then_inc(oh_in, 16)
            pool.dma_start(pos16[:, 0, :], t["cmp_k_pos"].rearrange("o (k l) d -> (o k) (l d)", l=2)).then_inc(small_in, 16)
            pool.dma_start(pos16[:, 1, :], t["cmp_v_pos"].rearrange("o (k l) d -> (o k) (l d)", l=2)).then_inc(small_in, 16)
            pool.dma_start(glw, win_gates(t)).then_inc(gl_in, 16)
            pool.dma_start(w2[:, 0], t["cmp_k_w2"][0].rearrange("(m p) n -> p m n", p=P)).then_inc(small_in, 16)
            pool.dma_start(w2[:, 1], t["cmp_v_w2"][0].rearrange("(m p) n -> p m n", p=P)).then_inc(small_in, 16)
            pool.dma_start(routw[:, :, :], t["router_w"].rearrange("(k p) n -> p k n", p=P)).then_inc(small_in, 16)
            pool.dma_start(routb[:, :], t["router_b"].rearrange("(o n) -> o n", o=1).to_broadcast([P, N_EXP])).then_inc(small_in, 16)
            pool.dma_start(nsink[:, :], t["swa_sinks"].to_broadcast([P, NH])).then_inc(small_in, 16)
            nc.gpsimd.memset(acc, 0.0).then_inc(acc_zero, 1)
            wait_evacuated(pool, "bias")
            pool.dma_start(scratch_back, biasrow[:, 0:640]).then_inc(vrow_out, 16)
            pool.dma_start(scratch_near, biasrow[:, 640:1024]).then_inc(vrow_out, 16)
            pool.wait_ge(vrow_out, 32)
            for src, dst, n, width in ((scratch_back, bias_back, T, 640), (scratch_near, bias_near, 2 * WINDOW, 384)):
                shifted = bass.AP(tensor=src.tensor, offset=P - 1, ap=[[width, NH], [-1, P], [1, n]])
                pool.dma_start(dst, shifted).then_inc(toeplitz, 16)

            def heads(layer):
                S = A[layer]
                with pool.Fori(0, NG) as g:
                    for hh in range(HPG):
                        pool.wait_ge(S["comb"], PRIMED + g * HPG + hh + 1)
                        o = O[:, :, bass.ds((g * HPG + hh) * HD, HD)]
                        if layer == 0:
                            v = osc.rearrange("p (i b) d -> p i b d", b=2)
                            nc.gpsimd.tensor_tensor(o, v[:, :, 0, :], v[:, :, 1, :], ALU.add).then_inc(S["heads"], 1)
                        else:
                            nc.gpsimd.tensor_copy(o, osc[:, 0:NT, :]).then_inc(S["heads"], 1)

            def norm(n):
                for i in range(NT):
                    pool.wait_ge(ln_var, NT * n + i + 1)
                    nc.gpsimd.tensor_tensor(mv[:, i, 2:3], mv[:, i, 1:2], nhalf[:, :], ALU.pow).then_inc(ln_rstd, 1)
                pool.wait_ge(ln_in, 32 * (n + 1))
                for i in range(NT):
                    pool.wait_ge(ln_gain, NT * n + i + 1)
                    nc.gpsimd.tensor_tensor(X[:, i, :], X[:, i, :], lnb, ALU.add).then_inc(ln_done, 1)

            def gather(dst, rows, layer):
                return nc.gpsimd.indirect_dma_start(dst, None, tokens[layer], bass.IndirectOffsetOnAxis(ap=rows, axis=0),
                                                    bounds_check=T - 1, oob_is_err=False)

            def scatter(src, rows, layer):
                return nc.gpsimd.indirect_dma_start(answers[layer], bass.IndirectOffsetOnAxis(ap=rows, axis=0), src, None,
                                                    bounds_check=2 * T - 1, oob_is_err=False)

            def experts(layer):
                S = M[layer]

                def fetch(e):
                    pool.wait_ge(slots_ready[layer], e // EPG + 1)
                    if e >= 2:
                        pool.wait_ge(S["xturn"], PRIMED + e - 1)
                    gather(Xg[:, e % 2, :], slot_rows[:, 0, e:e + 1], layer).then_inc(gathered[layer][e % 2], 16)

                pool.wait_ge(routed[layer], 1)
                steps.link(nc.gpsimd.memset(Xg[:, :, :], 0.0))
                pool.wait_ge(tokens_out[layer], 16 * NT)
                fetch(0)
                fetch(1)
                fetch(2)
                pool.sem_inc(S["yfree"], 1)
                for e in range(N_EXP):
                    if e + 3 < N_EXP:
                        fetch(e + 3)
                    pool.wait_ge(S["yact"], PRIMED + e + 1)
                    pool.wait_ge(S["ydve"], PRIMED + e + 1)
                    scatter(Y[:, e % 2, :], slot_rows[:, 1, e:e + 1], layer).then_inc(scattered[layer][e % 2], 16)
                    if e:
                        pool.wait_ge(scattered[layer][(e - 1) % 2], 16 * ((e - 1) // 2 + 1))
                        pool.sem_inc(S["yfree"], 1)
                for b in range(2):
                    pool.wait_ge(scattered[layer][b], 16 * N_EXP // 2)
                flag = pool.value_load(many[0:1, layer:layer + 1], min_val=0, max_val=1)
                with pool.If(flag == 1):
                    more_tokens(layer)

            def more_tokens(layer):
                S = R_[layer]
                with pool.Fori(0, N_EXP) as e:
                    for b in range(3):
                        pool.wait_ge(S["rows"], PRIMED + e * 3 + (b + 1))
                        apart(pool)
                        gather(Xg[:, 0, :], more_rows[:, 0:1], layer).then_inc(S["gather"], 16)
                        pool.wait_ge(S["y"], PRIMED + e * 3 + (b + 1))
                        apart(pool)
                        scatter(Y[:, 0, :], more_rows[:, 1:2], layer).then_inc(S["scatter"], 16)
                        pool.wait_ge(S["scatter"], e * 48 + 16 * (b + 1))
                        pool.sem_inc(S["free"], 1)

            pool.wait_ge(product, stage["kwvw"][-1] + 1)
            nc.gpsimd.memset(acc_rest, 0.0).then_inc(acc_zero, 1)
            pool.wait_ge(product, stage["hid"][-1] + 1)
            nc.gpsimd.memset(acc_next, 0.0).then_inc(acc_zero, 1)
            pool.wait_ge(product, stage["cmp"][-1] + 1)
            heads(0)
            norm(0)
            experts(0)
            norm(1)
            heads(1)
            norm(2)
            experts(1)
            norm(3)

        @block.tensor
        def _(pe):
            def mm(out, lhsT, rhs, start, stop):
                return nc.tensor.matmul(out, lhsT, rhs, start=start, stop=stop)

            def ada(name, sums_of, cols, gates):
                js = iter(stage[name])
                j = next(js)
                wait_bank(pe, j)
                for n, q in enumerate(cols):
                    last = mm(bank(j)[:, n:n + 1], sums_of[:, q * P:(q + 1) * P], ones[:, 0:1], True, True)
                last.then_inc(product, 1)
                for o in gates:
                    j = next(js)
                    wait_bank(pe, j)
                    mm(bank(j)[:, :], ones[:, :], sums_of[:, o:o + 512], True, True).then_inc(product, 1)

            def turn(name, rows):
                for k, j in enumerate(stage[name]):
                    wait_bank(pe, j)
                    for i in range(NT):
                        last = nc.tensor.transpose(bank(j)[:, i * P:(i + 1) * P], rows[:, i, k * P:(k + 1) * P], ident[:, :])
                    last.then_inc(product, 1)

            def by_columns(js, w, cols, src):
                for j, c in zip(js, cols):
                    wait_bank(pe, j)
                    for k in range(KD):
                        last = mm(bank(j)[:, :], w[:, k, c:c + P], src[:, k, :], k == 0, k == KD - 1)
                    last.then_inc(product, 1)

            def by_tokens(js, w, c, n, src):
                for i, j in enumerate(js):
                    wait_bank(pe, j)
                    for k in range(KD):
                        last = mm(bank(j)[:, 0:n], src[:, k, i * P:(i + 1) * P], w[:, k, c:c + n], k == 0, k == KD - 1)
                    last.then_inc(product, 1)

            def as_matrix(name, n=512, k=KD):
                return slot(name)[:, 0:k * n].rearrange("p (k n) -> p k n", k=k)

            pe.wait_ge(consts, 3)
            pe.wait_ge(c_in, 16)
            j, = stage["cond"]
            nc.tensor.transpose(bank(j)[:, 0:KD], c8, ident[0:KD, 0:KD]).then_inc(product, 1)
            pe.wait_ge(rel_ready, 16)
            pe.wait_ge(oh_in, 16)
            pe.wait_ge(pool_step, 3)
            for j, (o, n) in zip(stage["bias"], ((BACK, 512), (BACK + 512, 128), (NEAR, 384))):
                mm(bank(j)[0:NH, 0:n], relb[:, :], OH[:, o:o + n], True, True).then_inc(product, 1)
            for i, j in enumerate(stage["biasc"]):
                wait_bank(pe, j)
                for n in range(NC):
                    o = AHEAD + T + i * P - n * CMP_STRIDE - (CMP_LEN - 1)
                    last = mm(bank(j)[:, n * NH:(n + 1) * NH], OH[:, o:o + P], relb[:, :], True, True)
                last.then_inc(product, 1)
            pe.wait_ge(small_in, 16 * 7)
            for b, j in enumerate(stage["pos"]):
                wait_bank(pe, j)
                nc.tensor.transpose(bank(j)[:, 0:CK], pos16[:, b, :], ident[0:CK, 0:CK]).then_inc(product, 1)
            pe.wait_ge(ada_sum, 3)
            ada("ada0", acc, range(2 * KD), ())
            pe.wait_ge(x_in, 16)
            turn("hT0", X)
            wait_evacuated(pe, "hT0")
            wait_item(pe, "kcvc")
            by_columns(stage["kcvc"], as_matrix("kcvc"), (0, P, 2 * P, 3 * P), HT)
            for name in ("ksvs", "kwvw"):
                wait_item(pe, name)
                by_columns(stage[name][0:2], as_matrix(name), (0, P), HT)
                by_tokens(stage[name][2:], as_matrix(name), KVW, KVW, HT)
            pe.wait_ge(gl_in, 16)
            j, = stage["gl"]
            wait_bank(pe, j)
            for i in range(NT):
                for k in range(KD):
                    last = mm(bank(j)[:, i * 3 * NH:(i + 1) * 3 * NH], HT[:, k, i * P:(i + 1) * P], glw[:, k, :],
                              k == 0, k == KD - 1)
            last.then_inc(product, 1)
            wait_evacuated(pe, "pos")
            wait_evacuated(pe, "kcvc")
            for b, (j, name) in enumerate(zip(stage["posb"], ("w1k", "w1v"))):
                wait_item(pe, name)
                wait_bank(pe, j)
                for m in range(2):
                    for k in range(CK):
                        last = mm(bank(j)[:, m:m + 1], as_matrix(name, 256, CK)[:, k, m * P:(m + 1) * P],
                                  posT[:, b, k:k + 1], k == 0, k == CK - 1)
                last.then_inc(product, 1)
            js = iter(stage["hid"])
            for name, src in (("w1k", KC2), ("w1v", VC2)):
                for m in range(2):
                    j = next(js)
                    wait_bank(pe, j)
                    for k in range(CK):
                        last = mm(bank(j)[:, 0:NG * NC], as_matrix(name, 256, CK)[:, k, m * P:(m + 1) * P],
                                  src[:, :, k:k + 8 * (NC - 1) + 1:8], k == 0, k == CK - 1)
                    last.then_inc(product, 1)
            wait_evacuated(pe, "hid")
            j, jv = stage["cmp"]
            wait_bank(pe, j)
            for m in range(2):
                last = mm(bank(j)[0:HD, 0:NG * NC], w2[:, 0, m, :], hid[:, 0, m, 0:NG * NC], m == 0, m == 1)
            last.then_inc(product, 1)
            wait_bank(pe, jv)
            for g in range(NG):
                for m in range(2):
                    last = mm(bank(jv)[0:NC, g * HD:(g + 1) * HD], hid[:, 1, m, g * NC:(g + 1) * NC], w2[:, 1, m, :],
                              m == 0, m == 1)
            last.then_inc(product, 1)

            def attention(layer):
                S = A[layer]
                n_units = HPG * U[layer]
                w = slot(f"wq{layer}")[:, 0:KD * KVW].rearrange("p (k n) -> p k n", k=KD)
                s, before = items[f"wq{layer}"]
                with pe.Fori(0, NG) as g:
                    def scores(u):
                        i, b, k0, ext = units[layer][u % U[layer]]
                        if u >= 2:
                            pe.wait_ge(S["logit"], PRIMED + g * n_units + u - 1)
                        apart(pe)
                        mm(ps[4 + u % 2][:, 0:ext], QT[:, u // U[layer], i * P:(i + 1) * P],
                           KT[:, b, bass.ds(g, 1), k0:k0 + ext].rearrange("p o t -> p (o t)"), True, True)\
                            .then_inc(S["score"], 1)

                    def turns(u):
                        ext = units[layer][u % U[layer]][3]
                        pe.wait_ge(S["expo"], PRIMED + g * n_units + u + 1)
                        if u >= 2:
                            pe.wait_ge(S["pte_act" if u % 2 == 0 else "pte_dve"], PRIMED + g * (n_units // 2) + u // 2)
                        for k in range(ext // P):
                            last = nc.tensor.transpose(ps[6 + u % 2][:, k * P:(k + 1) * P],
                                                       probs[:, u % 2, k * P:(k + 1) * P], ident[:, :])
                        last.then_inc(S["turn"], 1)

                    def values(u):
                        i, b, k0, ext = units[layer][u % U[layer]]
                        hh, n = divmod(u, U[layer])
                        col = i * BRANCHES[layer] + b
                        pe.wait_ge(S["pte_act" if u % 2 == 0 else "pte_dve"], PRIMED + g * (n_units // 2) + u // 2 + 1)
                        if n == 0:
                            pe.wait_ge(S["comb"], PRIMED + g * HPG + hh)
                        apart(pe)
                        for k in range(ext // P):
                            last = mm(ps[3][:, col * HD:(col + 1) * HD], probsT[:, u % 2, k * P:(k + 1) * P],
                                      V[:, b, k0 // P + k, bass.ds(g * HD, HD)], k == 0, k == ext // P - 1)
                        last.then_inc(S["pv"], 1)

                    pe.wait_ge(landed[s], g * 16 + (before + 16))
                    if layer == 0:
                        pe.wait_ge(S["cpt"], PRIMED + g * HPG)
                    for m in range(2):
                        for k in range(KD):
                            last = mm(ps[1 + m][:, :], w[:, k, m * P:(m + 1) * P], HT[:, k, :], k == 0, k == KD - 1)
                        last.then_inc(S["qproj"], 1)
                    pe.wait_ge(S["qt"], PRIMED + g * 2 + 2)
                    for u in range(n_units + LAG):
                        hh, n = divmod(u, U[layer])
                        if u < n_units:
                            if layer == 0 and n == 0:
                                if hh:
                                    pe.wait_ge(S["cshift"], PRIMED + g * HPG + hh)
                                apart(pe)
                                for i in range(NT):
                                    last = mm(ps[1][:, i * NCP:i * NCP + NC], QT[:, hh, i * P:(i + 1) * P],
                                              KC[:, bass.ds(g, 1), :].rearrange("p o n -> p (o n)"), True, True)
                                last.then_inc(S["cscore"], 1)
                            scores(u)
                        if 0 <= u - LAG + 1 < n_units:
                            turns(u - LAG + 1)
                        if layer == 0 and n == 5 and u < n_units:
                            pe.wait_ge(S["cprob"], PRIMED + g * HPG + hh + 1)
                            if hh:
                                pe.wait_ge(S["cpt"], PRIMED + g * HPG + hh)
                            for i in range(NT):
                                last = nc.tensor.transpose(ps[2][0:NC, i * P:(i + 1) * P], Pc[:, i, 0:NC], ident[:, :])
                            last.then_inc(S["cturn"], 1)
                        if layer == 0 and n == 7 and u < n_units:
                            pe.wait_ge(S["cpt"], PRIMED + g * HPG + hh + 1)
                            pe.wait_ge(S["comb"], PRIMED + g * HPG + hh)
                            apart(pe)
                            for i in range(NT):
                                last = mm(ps[0][:, i * HD:(i + 1) * HD], PcT[0:NC, i * P:(i + 1) * P],
                                          VC[0:NC, bass.ds(g * HD, HD)], True, True)
                            last.then_inc(S["cpv"], 1)
                        if u >= LAG:
                            values(u - LAG)
                    pe.wait_ge(S["comb"], PRIMED + g * HPG + HPG)

            def output(layer):
                turn_name = f"oT{layer}"
                pe.wait_ge(A[layer]["heads"], PRIMED + NH)
                turn(turn_name, O)
                wait_evacuated(pe, turn_name)
                js = iter(stage[f"wo{layer}"])
                for i in range(NT):
                    for b in range(2):
                        name = f"wo{layer}.{b}"
                        wait_item(pe, name)
                        j = next(js)
                        wait_bank(pe, j)
                        for k in range(KD):
                            last = mm(bank(j)[:, :], HT[:, k, i * P:(i + 1) * P], as_matrix(name)[:, k, :],
                                      k == 0, k == KD - 1)
                        last.then_inc(product, 1)

            def route(layer):
                pe.wait_ge(ln_done, NT * (2 * layer) + NT)
                turn(f"hf{layer}", X)
                wait_evacuated(pe, f"hf{layer}")
                j, = stage[f"rout{layer}"]
                wait_bank(pe, j)
                for i in range(NT):
                    for k in range(KD):
                        last = mm(bank(j)[:, i * N_EXP:(i + 1) * N_EXP], HT[:, k, i * P:(i + 1) * P], routw[:, k, :],
                                  k == 0, k == KD - 1)
                last.then_inc(product, 1)

            def find_slots(layer):
                j, = stage[f"place{layer}"]
                wait_bank(pe, j)
                pe.wait_ge(routed[layer], 1)
                for i in range(NT):
                    for n in range(i):
                        mm(bank(j)[:, i * N_EXP:(i + 1) * N_EXP], ones[:, :], sel[:, n, :], n == 0, False)
                    mm(bank(j)[:, i * N_EXP:(i + 1) * N_EXP], upper[:, :], sel[:, i, :], i == 0, True)
                for n in range(NT):
                    last = mm(bank(j)[:, NT * N_EXP:(NT + 1) * N_EXP], ones[:, :], sel[:, n, :], n == 0, n == NT - 1)
                last.then_inc(product, 1)
                for q, j in enumerate(stage[f"slots{layer}"]):
                    wait_bank(pe, j)
                    pe.wait_ge(onehot_ready[layer], q + 1)
                    for e in range(EPG):
                        for i in range(NT):
                            last = mm(bank(j)[:, e * 4:e * 4 + 4], onehot[:, q % 2, e, i, :],
                                      routes[:, i, q * EPG + e, :], i == 0, i == NT - 1)
                    last.then_inc(product, 1)

            def turn_tokens(src, banks):
                for k in range(KD):
                    last = nc.tensor.transpose(ps[banks[k // 4]][:, (k % 4) * P:(k % 4 + 1) * P],
                                               src[:, k * P:(k + 1) * P], ident[:, :])
                return last

            def experts(layer):
                S = M[layer]

                def tokens_in(r, n):
                    v = r * SLOTS + n
                    pe.wait_ge(gathered[layer][n % 2], r * 32 + 16 * (n // 2 + 1))
                    pe.wait_ge(S["xact"], PRIMED + v)
                    pe.wait_ge(S["xdve"], PRIMED + v)
                    turn_tokens(Xg[:, n % 2, :], (0, 1)).then_inc(S["xturn"], 1)

                def hidden(r, n):
                    v = r * SLOTS + n
                    pe.wait_ge(landed[WS[layer][n % SLOTS]], r * 48 + (before_experts[layer][WS[layer][n % SLOTS]] + 48 * (n // SLOTS + 1)))
                    pe.wait_ge(S["xact"], PRIMED + v + 1)
                    pe.wait_ge(S["xdve"], PRIMED + v + 1)
                    if not isinstance(v, int) or v >= 2:
                        pe.wait_ge(S["hmid"], PRIMED + v - 1)
                    w = gate_up(expert_slot(layer, n))
                    for k in range(KD):
                        last = mm(ps[2 + n % 2][:, :], XgT[:, n % 2, k, :], w[:, k, :, :], k == 0, k == KD - 1)
                    last.then_inc(S["gu"], 1)

                def step(r, n):
                    v = r * SLOTS + n
                    if not isinstance(r, int) or v + 1 < N_EXP:
                        hidden(r, n + 1)
                    pe.wait_ge(S["hmid"], PRIMED + v + 1)
                    for m in range(2):
                        last = nc.tensor.transpose(ps[4 + n % 2][:, m * P:(m + 1) * P], hmid[:, n % 2, m * P:(m + 1) * P],
                                                   ident[:, :])
                    last.then_inc(S["hturn"], 1)
                    if not isinstance(r, int) or v + 2 < N_EXP:
                        tokens_in(r, n + 2)
                    pe.wait_ge(S["hmt"], PRIMED + v + 1)
                    pe.wait_ge(S["yact"], PRIMED + v)
                    pe.wait_ge(S["ydve"], PRIMED + v)
                    w = down(expert_slot(layer, n))
                    for b in range(2):
                        for k in range(2):
                            last = mm(ps[6 + b][:, :], hmidT[:, n % 2, k, :], w[:, k, b * 512:(b + 1) * 512], k == 0, k == 1)
                    last.then_inc(S["down"], 1)

                wait_all(f"slots{layer}")
                tokens_in(0, 0)
                hidden(0, 0)
                tokens_in(0, 1)
                with pe.Fori(0, ROUNDS - 1) as r:
                    for n in range(SLOTS):
                        step(r, n)
                for n in range(SLOTS):
                    step(ROUNDS - 1, n)
                flag = pe.value_load(many[0:1, layer:layer + 1], min_val=0, max_val=1)
                with pe.If(flag == 1):
                    more_tokens(layer)

            def more_tokens(layer):
                S = R_[layer]
                pe.wait_ge(M[layer]["yact"], PRIMED + N_EXP)
                pe.wait_ge(M[layer]["ydve"], PRIMED + N_EXP)
                with pe.Fori(0, N_EXP) as e:
                    for b in range(3):
                        v = PRIMED + e * 3 + b
                        pe.wait_ge(S["onehot"], v + 1)
                        apart(pe)
                        for i in range(NT):
                            last = mm(ps[5][:, 0:4], onehot[:, 0, 0, i, :],
                                      routes[:, i, bass.ds(e, 1), :].rearrange("p o c -> p (o c)"), i == 0, i == NT - 1)
                        last.then_inc(S["slots"], 1)
                        pe.wait_ge(S["gather"], e * 48 + 16 * (b + 1))
                        turn_tokens(Xg[:, 0, :], (0, 1)).then_inc(S["xturn"], 1)
                        pe.wait_ge(S["w"], e * 48 + 48)
                        pe.wait_ge(S["xact"], v + 1)
                        for k in range(KD):
                            last = mm(ps[2][:, :], XgT[:, 0, k, :], gate_up(ring[:, 0, :])[:, k, :, :], k == 0, k == KD - 1)
                        last.then_inc(S["gu"], 1)
                        pe.wait_ge(S["hmid"], v + 1)
                        for m in range(2):
                            last = nc.tensor.transpose(ps[4][:, m * P:(m + 1) * P], hmid[:, 0, m * P:(m + 1) * P], ident[:, :])
                        last.then_inc(S["hturn"], 1)
                        pe.wait_ge(S["hmt"], v + 1)
                        for h in range(2):
                            for k in range(2):
                                last = mm(ps[6 + h][:, :], hmidT[:, 0, k, :], down(ring[:, 0, :])[:, k, h * 512:(h + 1) * 512],
                                          k == 0, k == 1)
                        last.then_inc(S["down"], 1)

            def wait_all(last):
                for e in "AD":
                    pe.wait_ge(evac[e], max(nth[j] for j in range(stage[last][-1] + 1) if jobs[j] == e))

            wait_all("cmp")
            attention(0)
            pe.wait_ge(late_sum, PRIMED + NH)
            ada("rest", acc_rest, range(KD, 3 * KD), (0, 512, 3 * D, 3 * D + 512))
            output(0)
            ada("next", acc_next, [*range(2 * KD), *range(3 * KD, 5 * KD)],
                (2 * D, 2 * D + 512, 5 * D, 5 * D + 512))
            route(0)
            find_slots(0)
            experts(0)
            pe.wait_ge(ln_done, NT * 2)
            turn("xT1", X)
            wait_evacuated(pe, "xT1")
            wait_item(pe, "wkv")
            by_columns(stage["kv"][0:2], as_matrix("wkv"), (0, P), XTk)
            by_tokens(stage["kv"][2:], as_matrix("wkv"), KVW, KVW, XTk)
            pe.wait_ge(hT1_ready, KD)
            wait_all("kv")
            attention(1)
            output(1)
            route(1)
            find_slots(1)
            experts(1)

        @block.scalar
        def _(act):
            steps = Steps(act, act_step)

            def arrived(j):
                act.wait_ge(product, j + 1)

            def copy(out, j, src, scale=1.0):
                arrived(j)
                nc.scalar.activation(out, src, ACT.Copy, scale=scale).then_inc(evac["A"], 1)

            def mine(name):
                return [(n, j) for n, j in enumerate(stage[name]) if jobs[j] == "A"]

            (_, j), = mine("cond")
            arrived(j)
            nc.scalar.activation(cond[:, :], bank(j)[:, 0:KD], ACT.Silu).then_inc(evac["A"], 1)
            for i, j in mine("biasc"):
                copy(BC[:, i, :, :].rearrange("p n h -> p (n h)"), j, bank(j)[:, 0:NC * NH], -1.0)
            for b, j in mine("pos"):
                copy(posT[:, b, :], j, bank(j)[:, 0:CK])

            def modulated(name, layer, sub):
                for k, j in mine(name):
                    arrived(j)
                    nc.scalar.activation(HT[:, k, :], bank(j)[:, :], ACT.Identity,
                                         bias=adaC[:, layer, 2 * sub, k:k + 1],
                                         scale=adaC[:, layer, 2 * sub + 1, k:k + 1]).then_inc(evac["A"], 1)

            def ada_rows(name, layer):
                for n, j in mine(name):
                    arrived(j)
                    sub, q = divmod(n - 1, 2)
                    nc.scalar.activation(G[:, layer, sub, q * 512:(q + 1) * 512], bank(j)[:, :], ACT.Identity,
                                         bias=ones[:, 0:1]).then_inc(evac["A"], 1)

            wait_evacuated(act, "ada0")
            modulated("hT0", 0, 0)
            for n, j in mine("kcvc"):
                arrived(j)
                split_halves(lambda o, i: nc.scalar.activation(o, i, ACT.Copy), KC2 if n < 2 else VC2, n % 2, bank(j)).then_inc(evac["A"], 1)

            def keys_values(name, b):
                for n, j in mine(name):
                    arrived(j)
                    if n < 2:
                        for half in range(2):
                            last = nc.scalar.activation(KT[:, b, 2 * n + half, :], bank(j)[half * HD:(half + 1) * HD, :], ACT.Copy)
                    else:
                        last = nc.scalar.activation(V[:, b, n - 2, :], bank(j)[:, 0:KVW], ACT.Copy)
                    last.then_inc(evac["A"], 1)

            keys_values("ksvs", 0)
            keys_values("kwvw", 1)
            (_, j), = mine("gl")
            arrived(j)
            nc.scalar.activation(GT[:, :, :].rearrange("p i n -> p (i n)"), bank(j)[:, 0:NT * 3 * NH],
                                 ACT.Sigmoid).then_inc(evac["A"], 1)
            wait_evacuated(act, "posb")
            for n, j in mine("hid"):
                arrived(j)
                nc.scalar.activation(hid[:, n // 2, n % 2, 0:NG * NC], bank(j)[:, 0:NG * NC], ACT.Gelu_apprx_tanh,
                                     bias=posb[:, n // 2, n % 2:n % 2 + 1]).then_inc(evac["A"], 1)

            def attention(layer):
                S = A[layer]
                n_units = HPG * U[layer]
                with act.Fori(0, NG) as g:
                    for m in range(2):
                        act.wait_ge(S["qproj"], PRIMED + g * 2 + m + 1)
                        for half in range(2):
                            last = nc.scalar.activation(QT[:, 2 * m + half, :], ps[1 + m][half * HD:(half + 1) * HD, :],
                                                        ACT.Copy, scale=-SCALE)
                        last.then_inc(S["qt"], 1)
                    for u in range(n_units + LAG - 1):
                        hh, n = divmod(u, U[layer])
                        if u < n_units:
                            i, b, k0, ext = units[layer][n]
                            col = i * BRANCHES[layer] + b
                            if layer == 0 and n == 1:
                                act.wait_ge(S["cshift"], PRIMED + g * HPG + hh + 1)
                                nc.scalar.activation(Pc[:, :, 0:NC], Pc[:, :, 0:NC], ACT.Exp, scale=-1.0).then_inc(S["cexp"], 1)
                            act.wait_ge(S["logit"], PRIMED + g * n_units + u + 1)
                            if u >= 2:
                                act.wait_ge(S["turn"], PRIMED + g * n_units + u - 1)
                            nc.scalar.activation(probs[:, u % 2, 0:ext], logits[:, u % 2, 0:ext], ACT.Exp, scale=-1.0,
                                                 bias=mins[:, hh % 2, col:col + 1],
                                                 accum_out=sums[:, hh % 2, col:col + 1]).then_inc(S["expo"], 1)
                            if layer == 1 and n == NT - 1:
                                act.wait_ge(S["cprob"], PRIMED + g * HPG + hh + 1)
                                nc.scalar.activation(sink_exp[:, hh % 2, :], sink_diff[:, hh % 2, :], ACT.Exp).then_inc(S["cexp"], 1)
                            if layer == 0 and n == 6:
                                act.wait_ge(S["cturn"], PRIMED + g * HPG + hh + 1)
                                nc.scalar.activation(PcT[0:NC, :], ps[2][0:NC, :], ACT.Copy).then_inc(S["cpt"], 1)
                        v = u - LAG + 1
                        if v >= 0 and v % 2 == 0:
                            act.wait_ge(S["turn"], PRIMED + g * n_units + v + 1)
                            if v >= 2:
                                act.wait_ge(S["pv"], PRIMED + g * n_units + v - 1)
                            ext = units[layer][v % U[layer]][3]
                            nc.scalar.activation(probsT[:, 0, 0:ext], ps[6][:, 0:ext], ACT.Copy).then_inc(S["pte_act"], 1)

            def norm(n):
                for i in range(NT):
                    act.wait_ge(ln_nb, NT * n + i + 1)
                    if i >= 2:
                        act.wait_ge(ln_gain, NT * n + i - 1)
                    nc.scalar.activation(lnx[:, i % 2, :], X[:, i, :], ACT.Identity, scale=mv[:, i, 2:3],
                                         bias=mv[:, i, 3:4]).then_inc(ln_norm, 1)

            def output(layer):
                for k, j in mine(f"oT{layer}"):
                    copy(HT[:, k, :], j, bank(j)[:, :])
                norm(2 * layer)

            def route(layer):
                wait_evacuated(act, "next")
                modulated(f"hf{layer}", layer, 1)
                (_, j), = mine(f"rout{layer}")
                arrived(j)
                nc.scalar.activation(rt[:, 0, :, :].rearrange("p i e -> p (i e)"), bank(j)[:, 0:NT * N_EXP],
                                     ACT.Sigmoid).then_inc(evac["A"], 1)

            def tokens_modulated(src, dst, layer, k0):
                for k in range(4):
                    last = nc.scalar.activation(dst[:, k0 + k, :], src[:, k * P:(k + 1) * P], ACT.Identity,
                                                bias=adaC[:, layer, 2, k0 + k:k0 + k + 1],
                                                scale=adaC[:, layer, 3, k0 + k:k0 + k + 1])
                return last

            def experts(layer):
                S = M[layer]

                def tokens_in(r, n):
                    act.wait_ge(S["xturn"], PRIMED + r * SLOTS + n + 1)
                    tokens_modulated(ps[0], XgT[:, n % 2], layer, 0).then_inc(S["xact"], 1)

                def hidden(r, n):
                    v = r * SLOTS + n
                    act.wait_ge(S["gu"], PRIMED + v + 1)
                    if not isinstance(v, int) or v >= 2:
                        act.wait_ge(S["hmid"], PRIMED + v - 1)
                    nc.scalar.activation(silu[:, n % 2, :], ps[2 + n % 2][:, 0:D_EXP], ACT.Silu).then_inc(S["silu"], 1)

                def step(r, n):
                    v = r * SLOTS + n
                    if not isinstance(r, int) or v + 1 < N_EXP:
                        hidden(r, n + 1)
                    act.wait_ge(S["hturn"], PRIMED + v + 1)
                    nc.scalar.activation(hmidT[:, n % 2, :, :].rearrange("p m n -> p (m n)"), ps[4 + n % 2][:, 0:2 * P],
                                         ACT.Copy).then_inc(S["hmt"], 1)
                    if not isinstance(r, int) or v + 2 < N_EXP:
                        tokens_in(r, n + 2)
                    act.wait_ge(S["down"], PRIMED + v + 1)
                    act.wait_ge(S["yfree"], PRIMED + v)
                    apart(act)
                    nc.scalar.activation(Y[:, n % 2, 0:512], ps[6][:, :], ACT.Copy,
                                         scale=by_slot[:, bass.ds(v, 1), 3:4].rearrange("p o c -> p (o c)")
                                         ).then_inc(S["yact"], 1)

                act.wait_ge(slots_ready[layer], 4)
                tokens_in(0, 0)
                hidden(0, 0)
                tokens_in(0, 1)
                with act.Fori(0, ROUNDS - 1) as r:
                    for n in range(SLOTS):
                        step(r, n)
                for n in range(SLOTS):
                    step(ROUNDS - 1, n)
                flag = act.value_load(many[0:1, layer:layer + 1], min_val=0, max_val=1)
                with act.If(flag == 1):
                    S = R_[layer]
                    with act.Fori(0, N_EXP) as e:
                        for b in range(3):
                            v = PRIMED + e * 3 + b
                            act.wait_ge(S["xturn"], v + 1)
                            tokens_modulated(ps[0], XgT[:, 0], layer, 0)
                            tokens_modulated(ps[1], XgT[:, 0], layer, 4).then_inc(S["xact"], 1)
                            act.wait_ge(S["gu"], v + 1)
                            nc.scalar.activation(silu[:, 0, :], ps[2][:, 0:D_EXP], ACT.Silu).then_inc(S["silu"], 1)
                            act.wait_ge(S["hturn"], v + 1)
                            nc.scalar.activation(hmidT[:, 0, :, :].rearrange("p m n -> p (m n)"), ps[4][:, 0:2 * P],
                                                 ACT.Copy).then_inc(S["hmt"], 1)

            attention(0)
            act.wait_ge(consts, 3)
            ada_rows("rest", 0)
            output(0)
            ada_rows("next", 1)
            route(0)
            experts(0)
            norm(1)
            for k, j in mine("xT1"):
                copy(XTk[:, k, :], j, bank(j)[:, :])
            keys_values("kv", 0)
            attention(1)
            output(1)
            route(1)
            experts(1)
            norm(3)

        @block.vector
        def _(dve):
            steps = Steps(dve, dve_step)
            link = steps.link

            def arrived(j):
                dve.wait_ge(product, j + 1)

            def mine(name):
                return [(n, j) for n, j in enumerate(stage[name]) if jobs[j] == "D"]

            def ada_sums():
                dve.wait_ge(acc_bias, 16)
                k = 0
                for q in range(3):
                    wait_item(dve, f"ada{q}")
                    w = slot(f"ada{q}")[:, 0:CHUNK[q] * PART].rearrange("p (k n) -> p k n", k=CHUNK[q])
                    for kk in range(CHUNK[q]):
                        ins = nc.vector.scalar_tensor_tensor(acc, w[:, kk, :], cond[:, k:k + 1], acc, ALU.mult, ALU.add)
                        k += 1
                        if kk == CHUNK[q] - 1:
                            ins.then_inc(ada_sum, 1)
                            dve.wait_ge(ada_sum, q + 1)
                        else:
                            link(ins)

            def ada_columns(name, layer, rows):
                (_, j), = mine(name)
                arrived(j)
                for n, r in enumerate(rows):
                    src = bank(j)[:, n * KD:(n + 1) * KD]
                    if r % 2:
                        last = nc.vector.tensor_scalar(adaC[:, layer, r, :], src, 1.0, None, ALU.add)
                    else:
                        last = nc.vector.tensor_copy(adaC[:, layer, r, :], src)
                last.then_inc(evac["D"], 1)

            for (n, j), (o, w) in zip(mine("bias"), ((0, 512), (512, 128), (640, 384))):
                arrived(j)
                nc.vector.tensor_scalar(biasrow[:, o:o + w], bank(j)[0:NH, 0:w], -1.0, None, ALU.mult).then_inc(evac["D"], 1)
            for i, j in mine("biasc"):
                arrived(j)
                nc.vector.tensor_scalar(BC[:, i, :, :].rearrange("p n h -> p (n h)"), bank(j)[:, 0:NC * NH], -1.0, None,
                                        ALU.mult).then_inc(evac["D"], 1)
            for b, j in mine("pos"):
                arrived(j)
                nc.vector.tensor_copy(posT[:, b, :], bank(j)[:, 0:CK]).then_inc(evac["D"], 1)
            dve.wait_ge(small_in, 16 * 7)
            link(nc.vector.tensor_scalar(nsink[:, :], nsink[:, :], -1.0, None, ALU.mult))
            wait_evacuated(dve, "cond")
            ada_sums()
            ada_columns("ada0", 0, (0, 1))

            def modulated(name, layer, sub):
                for k, j in mine(name):
                    arrived(j)
                    nc.vector.tensor_scalar(HT[:, k, :], bank(j)[:, :], adaC[:, layer, 2 * sub + 1, k:k + 1],
                                            adaC[:, layer, 2 * sub, k:k + 1], ALU.mult, ALU.add).then_inc(evac["D"], 1)

            def keys_values(name, b):
                for n, j in mine(name):
                    arrived(j)
                    if n < 2:
                        for half in range(2):
                            last = nc.vector.tensor_copy(KT[:, b, 2 * n + half, :], bank(j)[half * HD:(half + 1) * HD, :])
                    else:
                        last = nc.vector.tensor_copy(V[:, b, n - 2, :], bank(j)[:, 0:KVW])
                    last.then_inc(evac["D"], 1)

            wait_evacuated(dve, "ada0")
            modulated("hT0", 0, 0)
            for n, j in mine("kcvc"):
                arrived(j)
                split_halves(nc.vector.tensor_copy, KC2 if n < 2 else VC2, n % 2, bank(j)).then_inc(evac["D"], 1)
            keys_values("ksvs", 0)
            keys_values("kwvw", 1)
            for b, j in mine("posb"):
                arrived(j)
                nc.vector.tensor_copy(posb[:, b, :], bank(j)[:, 0:2]).then_inc(evac["D"], 1)
            (_, j), (_, jv) = mine("cmp")
            arrived(j)
            nc.vector.tensor_copy(KC[:, :, :].rearrange("p g n -> p (g n)"), bank(j)[0:HD, 0:NG * NC]).then_inc(evac["D"], 1)
            arrived(jv)
            nc.vector.tensor_copy(VC[0:NC, :], bank(jv)[0:NC, 0:KVW]).then_inc(evac["D"], 1)

            def attention(layer, first=0, last=NG, late=None):
                S = A[layer]
                sums_of = acc_rest if late == 0 else acc_next
                skip = PART if late == 0 else 0
                PIECE = 1024
                n_units = HPG * U[layer]
                nu = U[layer]
                per = HPG * (10 if layer == 0 else 3)
                with dve.Fori(first, last) as g:
                    steps.enter(g - first, per)

                    def late_piece(hh, n):
                        o = n * PIECE
                        if o >= SLOT - skip:
                            return
                        if n == 0:
                            s, before = items["late"]
                            dve.wait_ge(landed[s], g * (16 * HPG) + (before + 16 * (hh + 1)))
                            dve.wait_ge(late_sum, PRIMED + g * HPG + hh)
                            apart(dve)
                        k = g * HPG + (hh - first * HPG)
                        add = nc.vector.scalar_tensor_tensor(
                            sums_of[:, o:o + PIECE], slot("late")[:, skip + o:skip + o + PIECE],
                            cond[:, bass.ds(k, 1)], sums_of[:, o:o + PIECE], ALU.mult, ALU.add)
                        if o + PIECE == SLOT - skip:
                            add.then_inc(late_sum, 1)

                    def combine(hh):
                        h = g * HPG + hh
                        dve.wait_ge(S["pv"], PRIMED + g * n_units + (hh + 1) * nu)
                        dve.wait_ge(S["heads"], PRIMED + g * HPG + hh)
                        if layer == 1:
                            dve.wait_ge(S["cexp"], PRIMED + g * HPG + hh + 1)
                            link(nc.vector.tensor_tensor(small[:, 16:16 + nu], sums[:, hh % 2, 0:nu], sink_exp[:, hh % 2, :],
                                                         ALU.add))
                            link(nc.vector.reciprocal(small[:, 32:32 + nu], small[:, 16:16 + nu]))
                            nc.vector.tensor_tensor(osc[:, 0:nu, :],
                                                    ps[3][:, 0:nu * HD].rearrange("p (u d) -> p u d", d=HD),
                                                    small[:, 32:32 + nu].unsqueeze(2).to_broadcast([P, nu, HD]),
                                                    ALU.mult).then_inc(S["comb"], 1)
                            return
                        gates = GT[:, :, :].rearrange("p i (b h) -> p i b h", b=3)
                        rs = small[:, 0:nu].rearrange("p (i b) -> p i b", b=2)
                        link(nc.vector.reciprocal(small[:, 0:nu], sums[:, hh % 2, :]))
                        link(nc.vector.tensor_tensor(rs, rs, gates[:, :, 1:3, bass.ds(h, 1)].rearrange("p i b o -> p i (b o)"),
                                                     ALU.mult))
                        link(nc.vector.tensor_tensor(osc[:, :, :], ps[3][:, :].rearrange("p (u d) -> p u d", d=HD),
                                                     small[:, 0:nu].unsqueeze(2).to_broadcast([P, nu, HD]), ALU.mult))
                        dve.wait_ge(S["cpv"], PRIMED + g * HPG + hh + 1)
                        v = osc.rearrange("p (i b) d -> p i b d", b=2)[:, :, 0, :]
                        nc.vector.tensor_tensor(v, v, ps[0][:, 0:NT * HD].rearrange("p (i d) -> p i d", d=HD),
                                                ALU.add).then_inc(S["comb"], 1)

                    for u in range(n_units + LAG + 1):
                        hh, n = divmod(u, nu)
                        if u >= nu + LAG - 0 and (u - LAG) % nu == 0:
                            combine((u - LAG) // nu - 1)
                        if u < n_units:
                            i, b, k0, ext = units[layer][n]
                            col = i * BRANCHES[layer] + b
                            if layer == 0 and n == 1:
                                dve.wait_ge(S["cscore"], PRIMED + g * HPG + hh + 1)
                                dve.wait_ge(S["cturn"], PRIMED + g * HPG + hh)
                                link(nc.vector.tensor_tensor(
                                    Pc[:, :, 0:NC], ps[1][:, 0:NT * NCP].rearrange("p (i n) -> p i n", i=NT)[:, :, 0:NC],
                                    BC[:, :, :, bass.ds(g * HPG + hh, 1)].rearrange("p i n o -> p i (n o)"), ALU.add))
                                link(nc.vector.tensor_reduce(small[:, 40:44], Pc[:, :, 0:NC], AX.X, ALU.min))
                                nc.vector.tensor_tensor(Pc[:, :, 0:NC], Pc[:, :, 0:NC],
                                                        small[:, 40:44].unsqueeze(2).to_broadcast([P, NT, NC]),
                                                        ALU.subtract).then_inc(S["cshift"], 1)
                            if layer == 0 and n == 3:
                                dve.wait_ge(S["cexp"], PRIMED + g * HPG + hh + 1)
                                link(nc.vector.tensor_tensor(Pc[:, :, 0:NC], Pc[:, :, 0:NC], maskc[:, :, :], ALU.mult))
                                link(nc.vector.tensor_reduce(small[:, 44:48], Pc[:, :, 0:NC], AX.X, ALU.add))
                                link(nc.vector.tensor_scalar(small[:, 48:52], small[:, 44:48], 1e-30, None, ALU.max))
                                link(nc.vector.reciprocal(small[:, 52:56], small[:, 48:52]))
                                gates = GT[:, :, :].rearrange("p i (b h) -> p i b h", b=3)
                                link(nc.vector.tensor_tensor(small[:, 56:60], small[:, 52:56],
                                                             gates[:, :, 0, bass.ds(g * HPG + hh, 1)].rearrange("p i o -> p (i o)"),
                                                             ALU.mult))
                                nc.vector.tensor_tensor(Pc[:, :, 0:NC], Pc[:, :, 0:NC],
                                                        small[:, 56:60].unsqueeze(2).to_broadcast([P, NT, NC]),
                                                        ALU.mult).then_inc(S["cprob"], 1)
                            if layer == 1 and n == 0:
                                link(nc.vector.tensor_copy(sink_now[:, hh % 2:hh % 2 + 1], nsink[:, bass.ds(g * HPG + hh, 1)]))
                            dve.wait_ge(S["score"], PRIMED + g * n_units + u + 1)
                            dve.wait_ge(S["bias_odd" if hh % 2 else "bias_even"], g * (8 * HPG) + 16 * (hh // 2 + 1))
                            if u >= 2:
                                dve.wait_ge(S["expo"], PRIMED + g * n_units + u - 1)
                            apart(dve)
                            full = WIDEST[layer]
                            start = sink_now[:, hh % 2:hh % 2 + 1] if layer == 1 else 3.0e38
                            nc.vector.tensor_tensor_reduce(logits[:, u % 2, 0:ext], ps[4 + u % 2][:, 0:ext],
                                                           B[:, hh % 2, full - ext:full], 1.0, start, ALU.add, ALU.min,
                                                           mins[:, hh % 2, col:col + 1]).then_inc(S["logit"], 1)
                            if layer == 1 and n == NT - 1:
                                dve.wait_ge(S["logit"], PRIMED + g * n_units + u + 1)
                                nc.vector.tensor_scalar(sink_diff[:, hh % 2, :], mins[:, hh % 2, 0:NT],
                                                        sink_now[:, hh % 2:hh % 2 + 1], None,
                                                        ALU.subtract).then_inc(S["cprob"], 1)
                        v = u - LAG + 1
                        if 0 <= v < n_units and v % 2 == 1:
                            dve.wait_ge(S["turn"], PRIMED + g * n_units + v + 1)
                            if v >= 2:
                                dve.wait_ge(S["pv"], PRIMED + g * n_units + v - 1)
                            ext = units[layer][v % nu][3]
                            nc.vector.tensor_copy(probsT[:, 1, 0:ext], ps[7][:, 0:ext]).then_inc(S["pte_dve"], 1)
                        if late is not None and u < n_units:
                            late_piece(hh, n)
                steps.leave(last - first)

            def residual(n, i, b, branch, src_psum):
                x = X[:, i, b * 512:(b + 1) * 512]
                y = O[:, i, b * 512:(b + 1) * 512]
                ins = nc.vector.tensor_tensor(y, branch, G[:, n // 2, n % 2, b * 512:(b + 1) * 512], ALU.mult)
                if src_psum:
                    ins.then_inc(evac["D"], 1)
                    dve.wait_ge(evac["D"], src_psum)
                else:
                    link(ins)
                link(nc.vector.scalar_tensor_tensor(x, x, ALPHA, y, ALU.mult, ALU.add))
                link(nc.vector.bn_stats(stats[:, i, b, :], x))

            def norm_stats(n, i):
                link(nc.vector.bn_aggr(mv[:, i, 0:2], stats[:, i, :, :].rearrange("p b s -> p (b s)")))
                nc.vector.tensor_scalar(mv[:, i, 1:2], mv[:, i, 1:2], LN_EPS, None, ALU.add).then_inc(ln_var, 1)

            def norm_apply(n):
                for i in range(NT):
                    dve.wait_ge(ln_rstd, NT * n + i + 1)
                    nc.vector.scalar_tensor_tensor(mv[:, i, 3:4], mv[:, i, 0:1], -1.0, mv[:, i, 2:3], ALU.mult,
                                                   ALU.mult).then_inc(ln_nb, 1)
                dve.wait_ge(ln_in, 32 * (n + 1))
                for i in range(NT):
                    dve.wait_ge(ln_norm, NT * n + i + 1)
                    nc.vector.tensor_tensor(X[:, i, :], lnx[:, i % 2, :], lng, ALU.mult).then_inc(ln_gain, 1)

            def output(layer):
                for k, j in mine(f"oT{layer}"):
                    arrived(j)
                    nc.vector.tensor_copy(HT[:, k, :], bank(j)[:, :]).then_inc(evac["D"], 1)
                wait_evacuated(dve, "rest" if layer == 0 else "next")
                js = iter(stage[f"wo{layer}"])
                for i in range(NT):
                    for b in range(2):
                        j = next(js)
                        arrived(j)
                        residual(2 * layer, i, b, bank(j)[:, :], nth[j])
                    norm_stats(2 * layer, i)
                norm_apply(2 * layer)

            def route(layer):
                wait_evacuated(dve, "rest" if layer == 0 else "next")
                modulated(f"hf{layer}", layer, 1)
                wait_evacuated(dve, f"rout{layer}")
                s, sbias, rank, tmp = (rt[:, n, :, :] for n in range(4))
                score = rt[:, 5, :, 0:NE_GRP]
                best = rt[:, 6, :, 0:1]
                free = rt[:, 7, :, 0:1]
                hit = rt[:, 8, :, 0:NE_GRP]
                pair = rt[:, 9, :, 0:NE_GRP]
                tt = nc.vector.tensor_tensor

                def member(x, a):
                    return x.rearrange("p i (g e) -> p i g e", e=EPG)[:, :, :, a]

                link(tt(sbias, s, routb[:, :].unsqueeze(1).to_broadcast([P, NT, N_EXP]), ALU.add))
                link(nc.vector.memset(rank, 0.0))
                first = True
                for a in range(EPG):
                    for b in range(a + 1, EPG):
                        if first:
                            link(tt(score, member(sbias, a), member(sbias, b), ALU.add))
                            first = False
                        else:
                            link(tt(pair, member(sbias, a), member(sbias, b), ALU.add))
                            link(tt(score, score, pair, ALU.max))
                        link(tt(pair, member(sbias, b), member(sbias, a), ALU.is_gt))
                        link(tt(member(rank, a), member(rank, a), pair, ALU.add))
                        link(nc.vector.tensor_scalar(pair, pair, -1.0, 1.0, ALU.mult, ALU.add))
                        link(tt(member(rank, b), member(rank, b), pair, ALU.add))
                link(nc.vector.tensor_reduce(best.rearrange("p i o -> p (i o)"), score, AX.X, ALU.max))
                link(nc.vector.memset(free, 1.0))
                for a in range(NE_GRP):
                    link(tt(hit[:, :, a:a + 1], score[:, :, a:a + 1], best, ALU.is_ge))
                    link(tt(hit[:, :, a:a + 1], hit[:, :, a:a + 1], free, ALU.mult))
                    link(tt(free, free, hit[:, :, a:a + 1], ALU.subtract))
                link(nc.vector.tensor_scalar(sel, rank, 2.0, None, ALU.is_lt))
                for a in range(EPG):
                    link(tt(member(sel, a), member(sel, a), hit, ALU.mult))
                link(tt(tmp, sel, s, ALU.mult))
                link(nc.vector.tensor_reduce(best.rearrange("p i o -> p (i o)"), tmp, AX.X, ALU.add))
                link(nc.vector.reciprocal(free, best))
                link(tt(moeg[:, :, :], tmp, free.to_broadcast([P, NT, N_EXP]), ALU.mult))
                dve.wait_ge(consts, 7)
                number = tcol[:, :].unsqueeze(2).to_broadcast([P, NT, N_EXP])
                link(nc.vector.memset(rank, 0.0))
                for a in range(1, EPG):
                    link(tt(member(rank, a), member(rank, a - 1), member(sel, a - 1), ALU.add))
                tt(tmp, number, number, ALU.add).then_inc(routed[layer], 1)
                dve.wait_ge(routed[layer], 1)
                link(tt(routes[:, :, :, 1], tmp, rank, ALU.add))
                link(nc.vector.tensor_copy(routes[:, :, :, 0], number))
                link(nc.vector.memset(routes[:, :, :, 2], 1.0))
                link(nc.vector.tensor_copy(routes[:, :, :, 3], moeg[:, :, :]))
                j, = stage[f"place{layer}"]
                arrived(j)
                link(nc.vector.tensor_reduce(more[:, 0:1], bank(j)[:, NT * N_EXP:(NT + 1) * N_EXP], AX.X, ALU.max))
                nc.vector.scalar_tensor_tensor(place[:, :, :], bank(j)[:, 0:NT * N_EXP].rearrange("p (i e) -> p i e", i=NT),
                                               1.0, sel, ALU.add, ALU.mult).then_inc(evac["D"], 1)
                dve.wait_ge(evac["D"], nth[j])
                link(nc.vector.tensor_scalar(place[:, :, :], place[:, :, :], -1.0, None, ALU.add))
                link(nc.vector.tensor_scalar(many[:, layer:layer + 1], more[:, 0:1], float(P), None, ALU.is_gt))

                def collect(q):
                    j = stage[f"slots{layer}"][q]
                    arrived(j)
                    es = slice(q * EPG, (q + 1) * EPG)
                    nc.vector.tensor_copy(by_slot[:, es, :], bank(j)[:, 0:4 * EPG].rearrange("p (e c) -> p e c", c=4)
                                          ).then_inc(evac["D"], 1)
                    dve.wait_ge(evac["D"], nth[j])
                    link(nc.vector.tensor_scalar(more[:, 0:EPG], by_slot[:, es, 2], -NOWHERE, NOWHERE, ALU.mult, ALU.add))
                    link(tt(slot_rows[:, 0, es], by_slot[:, es, 0], more[:, 0:EPG], ALU.add))
                    tt(slot_rows[:, 1, es], by_slot[:, es, 1], more[:, 0:EPG], ALU.add).then_inc(slots_ready[layer], 1)
                    dve.wait_ge(slots_ready[layer], q + 1)

                for q in range(NE_GRP):
                    if q >= 2:
                        arrived(stage[f"slots{layer}"][q - 2])
                    for e in range(EPG):
                        last = tt(onehot[:, q % 2, e, :, :], row[:, :].unsqueeze(1).to_broadcast([P, NT, P]),
                                  place[:, :, q * EPG + e].unsqueeze(2).to_broadcast([P, NT, P]), ALU.is_equal)
                    last.then_inc(onehot_ready[layer], 1)
                    if q:
                        collect(q - 1)
                collect(NE_GRP - 1)

            def experts(layer):
                S = M[layer]

                def tokens_in(r, n):
                    dve.wait_ge(S["xturn"], PRIMED + r * SLOTS + n + 1)
                    for k in range(4, KD):
                        last = nc.vector.tensor_scalar(XgT[:, n % 2, k, :], ps[1][:, (k - 4) * P:(k - 3) * P],
                                                       adaC[:, layer, 3, k:k + 1], adaC[:, layer, 2, k:k + 1],
                                                       ALU.mult, ALU.add)
                    last.then_inc(S["xdve"], 1)

                def hidden(r, n):
                    v = r * SLOTS + n
                    dve.wait_ge(S["silu"], PRIMED + v + 1)
                    if not isinstance(v, int) or v >= 2:
                        dve.wait_ge(S["hturn"], PRIMED + v - 1)
                    nc.vector.tensor_tensor(hmid[:, n % 2, :], silu[:, n % 2, :], ps[2 + n % 2][:, D_EXP:2 * D_EXP],
                                            ALU.mult).then_inc(S["hmid"], 1)

                def step(r, n):
                    v = r * SLOTS + n
                    if not isinstance(r, int) or v + 1 < N_EXP:
                        hidden(r, n + 1)
                    if not isinstance(r, int) or v + 2 < N_EXP:
                        tokens_in(r, n + 2)
                    dve.wait_ge(S["down"], PRIMED + v + 1)
                    dve.wait_ge(S["yfree"], PRIMED + v)
                    nc.vector.tensor_scalar(Y[:, n % 2, 512:1024], ps[7][:, :],
                                            by_slot[:, bass.ds(v, 1), 3:4].rearrange("p o c -> p (o c)"), None,
                                            ALU.mult).then_inc(S["ydve"], 1)

                tokens_in(0, 0)
                hidden(0, 0)
                tokens_in(0, 1)
                with dve.Fori(0, ROUNDS - 1) as r:
                    for n in range(SLOTS):
                        step(r, n)
                for n in range(SLOTS):
                    step(ROUNDS - 1, n)
                flag = dve.value_load(many[0:1, layer:layer + 1], min_val=0, max_val=1)
                with dve.If(flag == 1):
                    more_tokens(layer)
                n = 2 * layer + 1
                for i in range(NT):
                    dve.wait_ge(answers_in[layer], 32 * NT)
                    link(nc.vector.tensor_tensor(O[:, i, :], O[:, i, :], Y1[:, i, :], ALU.add))
                    for b in range(2):
                        residual(n, i, b, O[:, i, b * 512:(b + 1) * 512], 0)
                    norm_stats(n, i)
                norm_apply(n)

            def more_tokens(layer):
                S = R_[layer]
                step_of_mine = more_step[layer]
                with dve.Fori(0, N_EXP) as e:
                    for b in range(3):
                        v = PRIMED + e * 3 + b
                        m = e * 9 + 3 * b
                        dve.wait_ge(S["free"], v)
                        nc.vector.tensor_scalar(more[:, 0:NT], place[:, :, bass.ds(e, 1)].rearrange("p i o -> p (i o)"),
                                                float(-P * (b + 1)), None, ALU.add).then_inc(step_of_mine, 1)
                        dve.wait_ge(step_of_mine, m + 1)
                        nc.vector.tensor_tensor(onehot[:, 0, 0, :, :], row[:, :].unsqueeze(1).to_broadcast([P, NT, P]),
                                                more[:, 0:NT].unsqueeze(2).to_broadcast([P, NT, P]),
                                                ALU.is_equal).then_inc(S["onehot"], 1)
                        dve.wait_ge(S["slots"], v + 1)
                        nc.vector.tensor_copy(more[:, 0:4], ps[5][:, 0:4]).then_inc(step_of_mine, 1)
                        dve.wait_ge(step_of_mine, m + 2)
                        nc.vector.tensor_scalar(more[:, 4:5], more[:, 2:3], -NOWHERE, NOWHERE, ALU.mult, ALU.add).then_inc(step_of_mine, 1)
                        dve.wait_ge(step_of_mine, m + 3)
                        nc.vector.tensor_tensor(more_rows[:, :], more[:, 0:2], more[:, 4:5].to_broadcast([P, 2]), ALU.add)\
                            .then_inc(S["rows"], 1)
                        dve.wait_ge(S["silu"], v + 1)
                        nc.vector.tensor_tensor(hmid[:, 0, :], silu[:, 0, :], ps[2][:, D_EXP:2 * D_EXP], ALU.mult)\
                            .then_inc(S["hmid"], 1)
                        dve.wait_ge(S["down"], v + 1)
                        for h in range(2):
                            last = nc.vector.tensor_scalar(Y[:, 0, h * 512:(h + 1) * 512], ps[6 + h][:, :], more[:, 3:4], None,
                                                           ALU.mult)
                        last.then_inc(S["y"], 1)
                dve.wait_ge(S["scatter"], 16 * 3 * N_EXP)

            dve.wait_ge(consts, 4)
            dve.wait_ge(acc_bias, 48)
            attention(0, 0, NG // 2, late=0)
            attention(0, NG // 2, NG, late=1)
            ada_columns("rest", 0, (2, 3))
            output(0)
            ada_columns("next", 1, (0, 1, 2, 3))
            route(0)
            experts(0)
            for k, (n, j) in enumerate([(n, j) for n, j in enumerate(stage["xT1"])]):
                dve.wait_ge(evac["A"], nth[j])
                nc.vector.tensor_scalar(HT[:, k, :], XTk[:, k, :], adaC[:, 1, 1, k:k + 1], adaC[:, 1, 0, k:k + 1],
                                        ALU.mult, ALU.add).then_inc(hT1_ready, 1)
            keys_values("kv", 0)
            attention(1)
            output(1)
            route(1)
            experts(1)


def win_gates(t):
    return t["nsa_w_in"][0][:, QW + 6 * KVW:NSA_IN].rearrange("(k p) n -> p k n", p=P)


def split_halves(copy, dst, m, src):
    for half in range(2):
        for odd in range(2):
            last = copy(dst[odd * HD:(odd + 1) * HD, 2 * m + half, :], src[half * HD:(half + 1) * HD, odd::2])
    return last


_INS = ["x", "c", "nsa_w_in", "cmp_k_w1", "cmp_k_w2", "cmp_v_w1", "cmp_v_w2", "cmp_k_pos", "cmp_v_pos", "nsa_w_out",
        "swa_w_q", "swa_sinks", "swa_w_out", "shared_w_kv", "rel_bias", "router_w", "router_b", "moe_w_gate",
        "moe_w_up", "moe_w_down", "ada_w", "ada_b", "ln_g", "ln_b"]


def kernel(**inputs):
    import concourse.bacc as bacc
    from concourse.bass_utils import run_bass_kernel_spmd

    nc = bacc.Bacc("TRN2", target_bir_lowering=False, num_devices=1)
    arrays, tensors = {}, {}
    for name, a in [(n, np.ascontiguousarray(inputs[n])) for n in _INS] + [("buckets", bucket_rows())]:
        arrays[f"in_{name}"] = a
        tensors[name] = nc.dram_tensor(f"in_{name}", a.shape, F32, kind="ExternalInput").ap()
    tensors["out"] = nc.dram_tensor("out", (1, T, D), F32, kind="ExternalOutput").ap()
    build(nc, tensors)
    r = run_bass_kernel_spmd(nc, [arrays], core_ids=[0])
    return r.results[0]["out"]
```

```python
from contextlib import ExitStack

import concourse.bass as bass
import numpy as np
from concourse import mybir

F32 = mybir.dt.float32
F16 = mybir.dt.float16
BF16 = mybir.dt.bfloat16
U32 = mybir.dt.uint32
ALU = mybir.AluOpType
ACT = mybir.ActivationFunctionType
AX = mybir.AxisListType

P = 128
D = 1024
T = 512
KD = D // P
NT = T // P
NH, NG, HD = 16, 4, 64
HPG = NH // NG
QW, KVW = NH * HD, NG * HD
NSA_IN = QW + 6 * KVW + 3 * NH
CMP_LEN, CMP_STRIDE = 32, 16
NC = T // CMP_STRIDE - 1
NCP = NC + 1
CK = CMP_LEN * HD // P
N_EXP, D_EXP = 16, 256
EPG = 4
NE_GRP = N_EXP // EPG
BUCKETS, MAX_DIST = 32, 128
WINDOW = 128
ALPHA = 4.0 ** 0.25
LN_EPS = 1e-5
SCALE = HD ** -0.5
MASKED = 1e30
NOWHERE = 65536.0
PART = 2048
SLOT = 6144
RING = 3


def bucket_rows():
    def one_hot(dist, valid):
        d = np.maximum(dist, 0)
        half = BUCKETS // 2
        large = half + (np.log(np.maximum(d, 1).astype(np.float32) / np.float32(half))
                        / np.float32(np.log(MAX_DIST / half)) * np.float32(half)).astype(np.int32)
        b = np.where(d < half, d, np.minimum(large, BUCKETS - 1))
        b = np.where(valid, b, BUCKETS)
        return (np.arange(BUCKETS + 1)[:, None] == b[None, :]).astype(np.float32)

    back = T - 1 - np.arange(640)
    near = 2 * WINDOW - 1 - np.arange(384)
    ahead = np.arange(1024) - T
    return np.concatenate([one_hot(back, back >= 0), one_hot(near, (near >= 0) & (near < WINDOW)),
                           one_hot(ahead, ahead >= 0)], axis=1)


BACK, NEAR, AHEAD = 0, 640, 1024


class Steps:

    def __init__(self, eng, sem):
        self.eng, self.sem, self.n, self.extra = eng, sem, 0, None

    def mark(self, ins):
        ins.then_inc(self.sem, 1)
        self.n += 1

    def wait(self):
        self.eng.wait_ge(self.sem, self.n if self.extra is None else self.extra + self.n)

    def link(self, ins):
        self.mark(ins)
        self.wait()

    def enter(self, it, per):
        self.extra, self.n0, self.per = it * per, self.n, per

    def leave(self, rounds):
        assert self.n - self.n0 == self.per, (self.n - self.n0, self.per)
        self.extra, self.n = None, self.n0 + rounds * self.per


def build(nc, t):
    with ExitStack() as ctx:
        def sb(name, shape):
            return ctx.enter_context(nc.sbuf_tensor(name, shape, F32))

        def sem(name):
            return ctx.enter_context(nc.semaphore(name))

        X = sb("X", [P, NT, D])
        XT = sb("XT", [P, KD * T])
        HT = sb("HT", [P, KD, T])
        O = sb("O", [P, NT, D])
        ring = sb("ring", [P, RING, SLOT])
        KTV = sb("KTV", [P, SLOT])
        G = sb("G", [P, 2, 2, D])
        WORK = sb("WORK", [P, 6144])
        ident = sb("ident", [P, P])
        ones = sb("ones", [P, P])
        cond = sb("cond", [P, KD])
        adaC = sb("adaC", [P, 2, 4, KD])
        GT = sb("GT", [P, NT, 3 * NH])
        routw = sb("routw", [P, KD, N_EXP])
        routb = sb("routb", [P, N_EXP])
        KC = sb("KC", [HD, NG, NC])
        VC = sb("VC", [NCP, KVW])
        maskc = sb("maskc", [P, NT, NC])
        nsink = sb("nsink", [P, NH])
        sums = sb("sums", [P, 2, 8])
        mins = sb("mins", [P, 2, 8])
        small = sb("small", [P, 64])
        moeg = sb("moeg", [P, NT, N_EXP])
        stats = sb("stats", [P, NT, 2, 6])
        mv = sb("mv", [P, NT, 4])
        nhalf = sb("nhalf", [P, 1])
        table = sb("table", [P, NH])
        relb = table[0:BUCKETS + 1, :]
        earlier = table[:, :].rearrange("p (a b) -> p a b", a=EPG)
        upper = sb("upper", [P, P])
        row = sb("row", [P, P])
        tcol = sb("tcol", [P, NT])
        slot_rows = ctx.enter_context(nc.sbuf_tensor("slot_rows", [P, 2, N_EXP], U32))
        many = ctx.enter_context(nc.sbuf_tensor("many", [P, 2], U32))
        more = small[:, 20:28]
        more_rows = ctx.enter_context(nc.sbuf_tensor("more_rows", [P, 2], U32))
        w2 = sb("w2", [P, 2, 2, HD])

        BC = XT[:, 0:NT * NC * NH].rearrange("p (i n h) -> p i n h", i=NT, n=NC)
        acc = XT[:, PART:2 * PART]
        acc_rest = ring[:, 2, PART:SLOT]
        acc_next = ring[:, 0, :]
        PcT = XT[0:NCP, PART:PART + T]
        Pc = XT[:, PART + T:PART + T + P].rearrange("p (i n) -> p i n", i=NT)
        XTk = XT[:, :].rearrange("p (k t) -> p k t", k=KD)
        OH = O[0:BUCKETS + 1, 0:2, :].rearrange("p a n -> p (a n)")
        KC2 = XT[:, PART:PART + (NG + 1) * 256].rearrange("p (g u) -> p g u", u=256)
        VC2 = O[:, 2:4, :].rearrange("p a n -> p (a n)")[:, 0:(NG + 1) * 256].rearrange("p (g u) -> p g u", u=256)
        table_parts = WORK[0:BUCKETS + 1, 512:512 + 3 * NH // 2].bitcast(BF16).rearrange("p (c h) -> p c h", c=3)
        table_left = WORK[0:BUCKETS + 1, 544:544 + NH]
        OH16 = WORK[0:BUCKETS + 1, 0:512].bitcast(BF16)
        KT = KTV[0:HD, 0:2 * NG * T].rearrange("p (b g t) -> p b g t", b=2, g=NG)
        V = KTV[:, 2 * NG * T:].rearrange("p (b i n) -> p b i n", b=2, i=NT)
        OT = O[:, :, :].rearrange("p i n -> p (i n)").rearrange("p (k t) -> p k t", k=KD)
        LP = WORK[:, 0:3072].rearrange("p (b n) -> p b n", b=4)
        spare = G[:, 0, :, :].rearrange("p s n -> p (s n)")
        PT = [XT[:, 2688:2688 + 10 * P], spare[:, 0:10 * P]]
        VG = spare[:, 10 * P:10 * P + 2 * NT * HD].rearrange("p (b i d) -> p b i d", b=2, i=NT)
        VCG = spare[0:NCP, 14 * P:14 * P + HD]
        QT = WORK[0:HD, 3072:5120].rearrange("p (h t) -> p h t", h=HPG)
        B = WORK[:, 5120:6144].rearrange("p (b n) -> p b n", b=2)
        glw = WORK[:, 3072:3072 + KD * 3 * NH].rearrange("p (k n) -> p k n", k=KD)
        posT = WORK[:, 3584:3584 + 2 * CK].rearrange("p (b k) -> p b k", b=2)
        posb = WORK[:, 3648:3648 + 4].rearrange("p (b m) -> p b m", b=2)
        hid = WORK[:, 4096:4096 + 4 * P].rearrange("p (b m n) -> p b m n", b=2, m=2)
        c8 = WORK[0:KD, 4608:4608 + P]
        pos16 = WORK[0:CK, 4736:4736 + 2 * P].rearrange("p (b n) -> p b n", b=2)
        biasrow = WORK[0:NH, 5120:6144]
        gatesT = WORK[0:3 * NH, 1024:1024 + T]
        sink_now = small[:, 62:64]
        inverse = small[:, 32:36]
        minus_one = small[:, 30:31]
        gates_now = small[:, 0:16].rearrange("p (b u) -> p b u", b=2)
        lng, lnb = XT[:, 0:D], XT[:, D:2 * D]
        Xg = WORK[:, 0:2 * D].rearrange("p (b n) -> p b n", b=2)
        XgT = HT[:, 0:4, :].rearrange("p a n -> p (a n)").rearrange("p (b k s) -> p b k s", b=2, k=KD)
        hmidT = HT[:, 4, :].rearrange("p (b m s) -> p b m s", b=2, m=2)
        ROUTE = 6
        routes = HT[:, 5, 0:NT * N_EXP * ROUTE // 2].bitcast(F16).rearrange("p (i e c) -> p i e c", i=NT, e=N_EXP)
        place = HT[:, 5, 256:256 + NT * N_EXP].rearrange("p (i e) -> p i e", i=NT)
        by_slot = HT[:, 5, 320:320 + 4 * N_EXP].rearrange("p (e c) -> p e c", c=4)
        Y = WORK[:, 2 * D:4 * D].rearrange("p (b n) -> p b n", b=2)
        silu = WORK[:, 5120:5632].rearrange("p (b n) -> p b n", b=2)
        hmid = WORK[:, 5632:6144].rearrange("p (b n) -> p b n", b=2)
        Y1 = HT[:, :, :].rearrange("p k t -> p (k t)").rearrange("p (i n) -> p i n", i=NT)
        onehot = O[:, :, :].rearrange("p i n -> p (i n)").bitcast(F16).rearrange("p (e i s) -> p e i s", e=N_EXP, i=NT)
        rt = WORK[:, 4096:4096 + 1024].rearrange("p (s i e) -> p s i e", s=16, i=NT)
        sel = rt[:, 4, :, :]
        ROUTED_FIRST = [slice(0, EPG), slice(EPG, N_EXP)]

        ps = [ctx.enter_context(nc.psum_tensor(f"ps{i}", [P, 512], F32)) for i in range(8)]
        JB = 4

        scratch_back = nc.dram_tensor("scratch_back", [NH, 640], F32, kind="Internal").ap()
        scratch_near = nc.dram_tensor("scratch_near", [NH, 384], F32, kind="Internal").ap()
        bias_back = nc.dram_tensor("bias_back", [NH, P, T], F32, kind="Internal").ap()
        bias_near = nc.dram_tensor("bias_near", [NH, P, 2 * WINDOW], F32, kind="Internal").ap()
        tokens = [nc.dram_tensor(f"tokens{n}", [T, D], F32, kind="Internal").ap() for n in range(2)]
        answers = [nc.dram_tensor(f"answers{n}", [2 * T, D], F32, kind="Internal").ap() for n in range(2)]

        jobs, stage = [], {}

        def plan(name, engines):
            stage[name] = range(len(jobs), len(jobs) + len(engines))
            jobs.extend(engines)

        plan("cond", "A")
        plan("bias", "DDD")
        plan("biasc", "AAAA")
        plan("pos", "AA")
        for layer in range(2):
            if layer == 0:
                plan("ada0", "D")
                plan("hT0", "ADADADAD")
                plan("kcvc", "ADAD")
                plan("ksvs", "ADADAD")
                plan("kwvw", "ADADAD")
                plan("gl", "A")
                plan("hid", "AAAA")
                plan("glT", "A")
                plan("cmp", "DD")
                plan("rest", "DAAAA")
            else:
                for i in range(NT):
                    plan(f"xT1.{i}", "AD")
                plan("kv", "ADADAD")
            for i in range(NT):
                plan(f"wo{layer}.{i}", "DD")
                if i == NT - 1 and layer == 0:
                    plan("next", "DAAAA")
                if i:
                    plan(f"hf{layer}.{i - 1}", "AD")
            plan(f"hf{layer}.{NT - 1}", "AD")
            plan(f"rout{layer}", "A")
            plan(f"place{layer}", "D")
            plan(f"slots{layer}", "DD")
        product = sem("product")
        evac = {"A": sem("evac_act"), "D": sem("evac_dve")}
        nth = [jobs[:j + 1].count(jobs[j]) for j in range(len(jobs))]

        def bank(j):
            return ps[j % JB]

        def wait_bank(eng, j):
            if j >= JB:
                eng.wait_ge(evac[jobs[j - JB]], nth[j - JB])

        def wait_evacuated(eng, name, last=None):
            js = list(stage[name])[:last]
            for e in "AD":
                own = [nth[j] for j in js if jobs[j] == e]
                if own:
                    eng.wait_ge(evac[e], own[-1])

        loaded = [0] * (RING + 1)
        items = {}

        def item(name, slot, rounds=1):
            items[name] = (slot, loaded[slot])
            loaded[slot] += 16 * rounds

        first_items = [f"ada{q}" for q in range(3)] + ["kcvc", "ksvs", "kwvw", "w1k", "w1v"]
        for n, name in enumerate(first_items):
            item(name, n % RING)
        item("wq0", 2, NG)
        item("late", 1, NH)
        item("wo0.0", 3)
        item("wo0.1", 1)
        SLOTS = RING + 1
        ROUNDS = N_EXP // SLOTS
        before_experts = {0: list(loaded)}
        for n in range(SLOTS):
            loaded[n] += 48 * ROUNDS
        item("wkv", 0)
        item("wq1", 1, NG)
        item("wo1.0", 2)
        item("wo1.1", 0)
        before_experts[1] = list(loaded)

        landed = [sem(f"landed{s}") for s in range(RING + 1)]

        def slot(name):
            s = items[name][0]
            return ring[:, s, :] if s < RING else KTV[:, :]

        def late_columns(layer, part):
            first = PART if layer == 0 else 0
            n = (SLOT - first) // 2
            return slice(first + part * n, first + (part + 1) * n)

        def wait_item(eng, name):
            s, before = items[name]
            eng.wait_ge(landed[s], before + 16)

        x_in, c_in, small_in, oh_in, acc_zero, acc_bias, gl_in, ln_in = map(sem, (
            "x_in", "c_in", "small_in", "oh_in", "acc_zero", "acc_bias", "gl_in", "ln_in"))
        consts, rel_ready, vrow_ready, vrow_out, toeplitz = map(sem, (
            "consts", "rel_ready", "vrow_ready", "vrow_out", "toeplitz"))
        table_split, pos_zero, pos_ready, pos_share = map(sem, ("table_split", "pos_zero", "pos_ready", "pos_share"))
        ada_sum = sem("ada_sum")
        late_second = sem("late_second")
        late_sum = [sem(f"late_sum{n}") for n in range(2)]
        dve_step, act_step, pool_step = sem("dve_step"), sem("act_step"), sem("pool_step")
        names = ("qproj qt bias_even bias_odd vg score logit expo inverse scaled turn pte_act pte_dve pv cscore cshift cexp cprob "
                 "cturn cpt heads").split()
        A = [{n: sem(f"{n}{layer}") for n in names} for layer in range(2)]
        mnames = "xturn xact xdve gu silu hmid hturn hmt down ydve yfree".split()
        M = [{n: sem(f"m_{n}{layer}") for n in mnames} for layer in range(2)]
        PRIMED = 1
        ln_var, ln_rstd, ln_done = (sem(f"ln_{n}") for n in ("var", "rstd", "done"))
        routed = [sem(f"routed{n}") for n in range(2)]
        onehot_ready = [sem(f"onehot{n}") for n in range(2)]
        slots_ready = [sem(f"slots_ready{n}") for n in range(2)]
        tokens_out = [sem(f"tokens_out{n}") for n in range(2)]
        gathered = [[sem(f"gathered{n}{b}") for b in range(2)] for n in range(2)]
        scattered = [[sem(f"scattered{n}{b}") for b in range(2)] for n in range(2)]
        answers_in = [sem(f"answers_in{i}") for i in range(NT)]
        answers_sum = sem("answers_sum")
        rnames = "w onehot rows slots gather xturn xact gu silu hmid hturn hmt down y scatter free".split()
        FURTHER = [{n: sem(f"r_{n}{layer}") for n in rnames} for layer in range(2)]
        more_step = [sem(f"more_step{n}") for n in range(2)]
        WS = [[2, 0, 1, 3], [3, 1, 2, 0]]
        stored = sem("stored")
        hT1_ready = sem("hT1_ready")

        def expert_slot(layer, n):
            s = WS[layer][n % SLOTS]
            return ring[:, s, :] if s < RING else KTV[:, :]

        def gate_up(w):
            return w[:, 0:4096].rearrange("p (b k n) -> p k b n", b=2, k=KD)

        def down(w):
            return w[:, 4096:6144].rearrange("p (k n) -> p k n", k=2)

        def apart(eng):
            eng.nop(nofuse=True)

        CHUNK = [3, 3, 2]

        U = [2 * NT, NT]
        units = [[(i, b, 0, P * (i + 1)) for b in range(2) for i in range(NT)],
                 [(i, 0, P * max(i - 1, 0), P * min(i + 1, 2)) for i in range(NT)]]
        BRANCHES = [2, 1]
        WIDEST = [T, 2 * WINDOW]
        LAG = 3
        INVERTS = (1,)
        def pt_block(layer, k, i):
            return k + i if layer == 1 else 3 * k + i if k < 2 else 7 + (i - 2) + (k - 2)

        def pt_copies(layer, i):
            if layer == 1:
                return [(max(2 * i - 1, 0), 1, min(i + 1, 2), 0)]
            return [(i, 3, min(i + 1, 2), 0)] + ([(pt_block(0, 2, i), 1, i - 1, 2 * P)] if i >= 2 else [])

        def pt_part(half, first, step, n):
            blocks = PT[half][:, 0:10 * P].rearrange("p (n q) -> p n q", q=P)
            return blocks[:, first:first + (n - 1) * step + 1:step, :]

        def copy_turned(copy, layer, half, i, bank_):
            for first, step, n, c in pt_copies(layer, i):
                last = copy(pt_part(half, first, step, n), bank_[:, c:c + n * P].rearrange("p (n q) -> p n q", q=P))
            return last

        block = ctx.enter_context(nc.Block())

        @block.sync
        def _(sp):
            def load(name, dst, src, after=None):
                if after is not None:
                    for s, v in after:
                        sp.wait_ge(s, v)
                sp.dma_start(dst, src).then_inc(landed[items[name][0]], 16)

            def ada_item(q, after):
                k0, n = sum(CHUNK[:q]), CHUNK[q]
                name = f"ada{q}"
                load(name, slot(name)[:, 0:n * PART].rearrange("p (k n) -> p k n", k=n),
                     t["ada_w"][0, k0 * P:(k0 + n) * P, 0:PART].rearrange("(k p) n -> p k n", p=P), after)

            def matrix(name, src, after):
                k, n = src.shape[0] // P, src.shape[1]
                load(name, slot(name)[:, 0:k * n].rearrange("p (k n) -> p k n", k=k),
                     src.rearrange("(k p) n -> p k n", p=P), after)

            def used(names):
                out = []
                for n in names:
                    if isinstance(n, tuple):
                        out.append(n)
                    else:
                        out.append((product, stage[n][-1] + 1))
                return out

            for sems in A + M + FURTHER:
                for n, primed in sems.items():
                    if n not in ("bias_even", "bias_odd", "w", "gather", "scatter"):
                        sp.sem_inc(primed, PRIMED)
            sp.dma_start(c8, t["c"].rearrange("o (k p) -> (o k) p", p=P)).then_inc(c_in, 16)
            for n in range(2):
                sp.sem_inc(late_sum[n], PRIMED)
            win = t["nsa_w_in"][0]
            c0 = QW
            release = {f"ada{q}": [(ada_sum, q + 1)] for q in range(3)}
            release |= {"kcvc": used(["kcvc"]), "ksvs": used(["ksvs"]), "kwvw": used(["kwvw"])}
            for n, name in enumerate(first_items):
                freed = release[first_items[n - RING]] if n >= RING else None
                if name.startswith("ada"):
                    ada_item(int(name[3]), freed)
                elif name in ("kcvc", "ksvs", "kwvw"):
                    b = {"kcvc": 0, "ksvs": 1, "kwvw": 2}[name]
                    matrix(name, win[:, c0 + 2 * b * KVW:c0 + 2 * (b + 1) * KVW], freed)
                else:
                    matrix(name, t["cmp_k_w1" if name == "w1k" else "cmp_v_w1"][0], freed)
                if name == "ada0":
                    sp.wait_ge(acc_zero, 1)
                    sp.dma_start(acc[0:1, :], t["ada_b"][0:1, 0:PART]).then_inc(acc_bias, 16)
                if name == "ada2":
                    sp.dma_start(X[:, :, :], t["x"].rearrange("o (i p) n -> p (o i) n", p=P)).then_inc(x_in, 16)

            def attention_loads(layer, first=0, last=NG, late=None):
                S = A[layer]
                wq = win[:, 0:QW] if layer == 0 else t["swa_w_q"][0]
                name = f"wq{layer}"
                dst = slot(name)[:, 0:KD * KVW].rearrange("p (k n) -> p k n", k=KD)
                width = WIDEST[layer]
                table = bias_back if layer == 0 else bias_near
                with sp.Fori(first, last) as g:
                    sp.wait_ge(S["qproj"], PRIMED + g * 2)
                    sp.dma_start(dst, wq[:, bass.ds(g * KVW, KVW)].rearrange("(k p) n -> p k n", p=P))\
                        .then_inc(landed[items[name][0]], 16)
                    for hh in range(HPG):
                        if hh >= 2:
                            sp.wait_ge(S["logit"], PRIMED + g * (HPG * U[layer]) + (hh - 1) * U[layer])
                        else:
                            sp.wait_ge(S["logit"], PRIMED + g * (HPG * U[layer]))
                        sp.dma_start(B[:, hh % 2, 0:width],
                                     table[bass.ds(g * HPG + hh, 1)].rearrange("o p n -> p (o n)"))\
                            .then_inc(S["bias_odd" if hh % 2 else "bias_even"], 16)
                        if late is not None:
                            k = g * HPG + (hh - first * HPG)
                            w = t["ada_w"][late].rearrange("(k p) n -> p k n", p=P)
                            sp.wait_ge(product, stage["hid"][-1] + 1)
                            for part, done in enumerate((landed[items["late"][0]], late_second)):
                                sp.wait_ge(late_sum[part], PRIMED + g * HPG + hh)
                                cols = late_columns(late, part)
                                sp.dma_start(slot("late")[:, cols], w[:, bass.ds(k, 1), cols].rearrange("p o n -> p (o n)"))\
                                    .then_inc(done, 16)

            sp.wait_ge(product, stage["kwvw"][-1] + 1)
            sp.wait_ge(acc_zero, 2)
            sp.dma_start(acc_rest[0:1, :], t["ada_b"][0:1, PART:]).then_inc(acc_bias, 16)
            sp.wait_ge(toeplitz, 32)
            attention_loads(0, 0, NG // 2, late=0)
            sp.wait_ge(acc_bias, 32)
            sp.wait_ge(acc_zero, 3)
            sp.dma_start(acc_next[0:1, :], t["ada_b"][1:2, :]).then_inc(acc_bias, 16)
            attention_loads(0, NG // 2, NG, late=1)
            sp.wait_ge(late_sum[1], PRIMED + NH)
            matrix("wo0.1", t["nsa_w_out"][0][:, 512:1024], None)
            sp.wait_ge(A[0]["heads"], PRIMED + NH)
            matrix("wo0.0", t["nsa_w_out"][0][:, 0:512], None)

            def norm_params(n):
                layer, sub = n // 2, n % 2
                sp.dma_start(lng, t["ln_g"][layer, sub:sub + 1, :].to_broadcast([P, D])).then_inc(ln_in, 16)
                sp.dma_start(lnb, t["ln_b"][layer, sub:sub + 1, :].to_broadcast([P, D])).then_inc(ln_in, 16)

            def expert_load(layer, dst, e, done):
                for j, w in enumerate(("moe_w_gate", "moe_w_up")):
                    sp.dma_start(dst[:, j * 2048:(j + 1) * 2048].rearrange("p (k n) -> p k n", k=KD),
                                 t[w][layer][bass.ds(e, 1)].rearrange("o (k p) n -> p (o k) n", p=P)).then_inc(done, 16)
                sp.dma_start(down(dst), t["moe_w_down"][layer][bass.ds(e, 1)].rearrange("o (k p) n -> p (o k) n", p=P))\
                    .then_inc(done, 16)

            def expert_loads(layer):
                with sp.Fori(1, ROUNDS) as r:
                    for n in range(SLOTS):
                        sp.wait_ge(M[layer]["down"], PRIMED + r * SLOTS + (n + 1 - SLOTS))
                        expert_load(layer, expert_slot(layer, n), r * SLOTS + n, landed[WS[layer][n]])

            def more_loads(layer):
                with sp.Fori(0, N_EXP) as e:
                    sp.wait_ge(FURTHER[layer]["down"], PRIMED + e * 3)
                    expert_load(layer, ring[:, 0, :], e, FURTHER[layer]["w"])

            def answers_back(layer):
                for b in range(2):
                    sp.wait_ge(scattered[layer][b], 16 * N_EXP // 2)
                src = answers[layer].rearrange("(i p r) n -> p i r n", p=P, r=2)
                for i in range(NT):
                    sp.dma_start(O[:, i, :], src[:, i, 0, :]).then_inc(answers_in[i], 16)
                    sp.dma_start(Y1[:, i, :], src[:, i, 1, :]).then_inc(answers_in[i], 16)

            def general(layer):
                sp.wait_ge(M[layer]["down"], PRIMED + N_EXP)
                sp.wait_ge(slots_ready[layer], 2)
                flag = sp.value_load(many[0:1, layer:layer + 1], min_val=0, max_val=1)
                with sp.If(flag == 1):
                    more_loads(layer)
                    sp.wait_ge(FURTHER[layer]["scatter"], 16 * 3 * N_EXP)

            def first_expert(layer, n):
                expert_load(layer, expert_slot(layer, n), n, landed[WS[layer][n]])

            norm_params(0)
            sp.wait_ge(product, stage["rest"][-1] + 1)
            first_expert(0, 0)
            sp.wait_ge(product, stage["next"][-1] + 1)
            first_expert(0, 1)
            for n in (2, 3):
                first_expert(0, n)
            for i in range(NT):
                sp.wait_ge(ln_done, 0 * NT + i + 1)
                sp.dma_start(tokens[0][i * P:(i + 1) * P, :], X[:, i, :]).then_inc(tokens_out[0], 16)
            norm_params(1)
            expert_loads(0)
            general(0)
            answers_back(0)
            matrix("wkv", t["shared_w_kv"], None)
            attention_loads(1)
            matrix("wo1.0", t["swa_w_out"][0][:, 0:512], None)
            matrix("wo1.1", t["swa_w_out"][0][:, 512:1024], [(product, stage["kv"][-1] + 1)])
            sp.wait_ge(A[1]["heads"], PRIMED + NH)
            norm_params(2)
            first_expert(1, 0)
            first_expert(1, 1)
            sp.wait_ge(product, stage[f"wo1.{NT - 1}"][-1] + 1)
            for n in (2, 3):
                first_expert(1, n)
            for i in range(NT):
                sp.wait_ge(ln_done, 2 * NT + i + 1)
                sp.dma_start(tokens[1][i * P:(i + 1) * P, :], X[:, i, :]).then_inc(tokens_out[1], 16)
            norm_params(3)
            expert_loads(1)
            general(1)
            answers_back(1)
            for i in range(NT):
                sp.wait_ge(ln_done, 3 * NT + i + 1)
                sp.dma_start(t["out"][0, i * P:(i + 1) * P, :], X[:, i, :]).then_inc(stored, 16)
            sp.wait_ge(stored, 16 * NT)

        @block.gpsimd
        def _(pool):
            steps = Steps(pool, pool_step)
            nc.gpsimd.memset(ones[:, :], 1.0).then_inc(consts, 1)
            nc.gpsimd.memset(nhalf[:, :], -0.5).then_inc(consts, 1)
            steps.link(nc.gpsimd.memset(minus_one[:, :], -1.0))
            steps.link(nc.gpsimd.memset(ident[:, :], 0.0))
            nc.gpsimd.affine_select(out=ident[:, :], in_=ident[:, :], compare_op=ALU.not_equal, fill=1.0, base=0,
                                    pattern=[[-1, P]], channel_multiplier=1).then_inc(consts, 1)
            steps.link(nc.gpsimd.memset(maskc[:, :, :], 1.0))
            nc.gpsimd.affine_select(out=maskc[:, :, :], in_=maskc[:, :, :], compare_op=ALU.is_ge, fill=0.0,
                                    base=1 - CMP_LEN, pattern=[[P, NT], [-CMP_STRIDE, NC]],
                                    channel_multiplier=1).then_inc(consts, 1)
            steps.link(nc.gpsimd.memset(relb, MASKED * -1.0))
            steps.link(nc.gpsimd.memset(upper[:, :], 1.0))
            nc.gpsimd.affine_select(out=upper[:, :], in_=upper[:, :], compare_op=ALU.is_gt, fill=0.0, base=0,
                                    pattern=[[1, P]], channel_multiplier=-1).then_inc(consts, 1)
            nc.gpsimd.iota(row[:, :], pattern=[[1, P]], base=0, channel_multiplier=0,
                           allow_small_or_imprecise_dtypes=True).then_inc(consts, 1)
            nc.gpsimd.iota(tcol[:, :], pattern=[[P, NT]], base=0, channel_multiplier=1,
                           allow_small_or_imprecise_dtypes=True).then_inc(consts, 1)
            nc.gpsimd.memset(VC2[:, NG, :], 0.0).then_inc(pos_zero, 1)
            pool.dma_start(relb[0:BUCKETS, :], t["rel_bias"]).then_inc(rel_ready, 16)
            pool.dma_start(OH, t["buckets"]).then_inc(oh_in, 16)
            pool.dma_start(pos16[:, 0, :], t["cmp_k_pos"].rearrange("o (k l) d -> (o k) (l d)", l=2)).then_inc(small_in, 16)
            pool.dma_start(pos16[:, 1, :], t["cmp_v_pos"].rearrange("o (k l) d -> (o k) (l d)", l=2)).then_inc(small_in, 16)
            pool.dma_start(glw, win_gates(t)).then_inc(gl_in, 16)
            pool.dma_start(w2[:, 0], t["cmp_k_w2"][0].rearrange("(m p) n -> p m n", p=P)).then_inc(small_in, 16)
            pool.dma_start(w2[:, 1], t["cmp_v_w2"][0].rearrange("(m p) n -> p m n", p=P)).then_inc(small_in, 16)
            pool.dma_start(routw[:, :, :], t["router_w"].rearrange("(k p) n -> p k n", p=P)).then_inc(small_in, 16)
            pool.dma_start(routb[:, :], t["router_b"].rearrange("(o n) -> o n", o=1).to_broadcast([P, N_EXP])).then_inc(small_in, 16)
            pool.dma_start(nsink[:, :], t["swa_sinks"].to_broadcast([P, NH])).then_inc(small_in, 16)
            nc.gpsimd.memset(acc, 0.0).then_inc(acc_zero, 1)
            wait_evacuated(pool, "bias")
            pool.dma_start(scratch_back, biasrow[:, 0:640]).then_inc(vrow_out, 16)
            pool.dma_start(scratch_near, biasrow[:, 640:1024]).then_inc(vrow_out, 16)
            pool.wait_ge(vrow_out, 32)
            pool.wait_ge(x_in, 16)
            for src, dst, n, width in ((scratch_back, bias_back, T, 640), (scratch_near, bias_near, 2 * WINDOW, 384)):
                shifted = bass.AP(tensor=src.tensor, offset=P - 1, ap=[[width, NH], [-1, P], [1, n]])
                pool.dma_start(dst, shifted).then_inc(toeplitz, 16)

            def scale(layer):
                S = A[layer]
                n_units = HPG * U[layer]
                with pool.Fori(0, NG) as g:
                    pool.wait_ge(S["heads"], PRIMED + g * HPG)
                    apart(pool)
                    last = nc.gpsimd.tensor_copy(VG[:, 0:BRANCHES[layer]].rearrange("p b i d -> p (b i) d"),
                                                 V[:, 0:BRANCHES[layer], :, bass.ds(g * HD, HD)].rearrange(
                                                     "p b i d -> p (b i) d"))
                    if layer == 0:
                        last = nc.gpsimd.tensor_copy(VCG[0:NC, :], VC[0:NC, bass.ds(g * HD, HD)])
                    last.then_inc(S["vg"], 1)
                    for u in range(n_units):
                        hh, n = divmod(u, U[layer])
                        i, b, k0, ext = units[layer][n]
                        col = i * BRANCHES[layer] + b
                        pool.wait_ge(S["expo"], PRIMED + g * n_units + u + 1)
                        p = LP[:, u % 4, 0:ext]
                        if layer not in INVERTS:
                            nc.gpsimd.tensor_tensor(inverse[:, u % 4:u % 4 + 1], sums[:, hh % 2, col:col + 1], minus_one[:, :],
                                                    ALU.pow).then_inc(S["inverse"], 1)
                        pool.wait_ge(S["inverse"], PRIMED + g * n_units + u + 1)
                        apart(pool)
                        if layer == 0:
                            ins = nc.gpsimd.tensor_scalar(p, p, inverse[:, u % 4:u % 4 + 1],
                                                          gates_now[:, hh % 2, col:col + 1], ALU.mult, ALU.mult)
                        else:
                            ins = nc.gpsimd.tensor_scalar(p, p, inverse[:, u % 4:u % 4 + 1], None, ALU.mult)
                        ins.then_inc(S["scaled"], 1)

            def norm(n):
                for i in range(NT):
                    if n % 2 and i + 1 < NT:
                        pool.wait_ge(answers_in[i + 1], 32 * (n // 2 + 1))
                        nc.gpsimd.tensor_tensor(O[:, i + 1, :], O[:, i + 1, :], Y1[:, i + 1, :], ALU.add)\
                            .then_inc(answers_sum, 1)
                    pool.wait_ge(ln_var, NT * n + i + 1)
                    nc.gpsimd.tensor_tensor(mv[:, i, 2:3], mv[:, i, 1:2], nhalf[:, :], ALU.pow).then_inc(ln_rstd, 1)

            def gather(dst, rows, layer):
                return nc.gpsimd.indirect_dma_start(dst, None, tokens[layer], bass.IndirectOffsetOnAxis(ap=rows, axis=0),
                                                    bounds_check=T - 1, oob_is_err=False)

            def scatter(src, rows, layer):
                return nc.gpsimd.indirect_dma_start(answers[layer], bass.IndirectOffsetOnAxis(ap=rows, axis=0), src, None,
                                                    bounds_check=2 * T - 1, oob_is_err=False)

            def experts(layer):
                S = M[layer]

                def fetch(e):
                    pool.wait_ge(slots_ready[layer], 1 if e < EPG else 2)
                    if e >= 2:
                        pool.wait_ge(S["xturn"], PRIMED + e - 1)
                    gather(Xg[:, e % 2, :], slot_rows[:, 0, e:e + 1], layer).then_inc(gathered[layer][e % 2], 16)

                pool.wait_ge(routed[layer], 1)
                steps.link(nc.gpsimd.memset(Xg[:, :, :], 0.0))
                pool.wait_ge(tokens_out[layer], 16 * NT)
                fetch(0)
                fetch(1)
                fetch(2)
                pool.sem_inc(S["yfree"], 1)
                for e in range(N_EXP):
                    if e + 3 < N_EXP:
                        fetch(e + 3)
                    pool.wait_ge(S["ydve"], PRIMED + e + 1)
                    scatter(Y[:, e % 2, :], slot_rows[:, 1, e:e + 1], layer).then_inc(scattered[layer][e % 2], 16)
                    if e:
                        pool.wait_ge(scattered[layer][(e - 1) % 2], 16 * ((e - 1) // 2 + 1))
                        pool.sem_inc(S["yfree"], 1)
                for b in range(2):
                    pool.wait_ge(scattered[layer][b], 16 * N_EXP // 2)
                flag = pool.value_load(many[0:1, layer:layer + 1], min_val=0, max_val=1)
                with pool.If(flag == 1):
                    more_tokens(layer)

            def more_tokens(layer):
                S = FURTHER[layer]
                with pool.Fori(0, N_EXP) as e:
                    for b in range(3):
                        pool.wait_ge(S["rows"], PRIMED + e * 3 + (b + 1))
                        apart(pool)
                        gather(Xg[:, 0, :], more_rows[:, 0:1], layer).then_inc(S["gather"], 16)
                        pool.wait_ge(S["y"], PRIMED + e * 3 + (b + 1))
                        apart(pool)
                        scatter(Y[:, 0, :], more_rows[:, 1:2], layer).then_inc(S["scatter"], 16)
                        pool.wait_ge(S["scatter"], e * 48 + 16 * (b + 1))
                        pool.sem_inc(S["free"], 1)

            pool.wait_ge(product, stage["ada0"][-1] + 1)
            nc.gpsimd.memset(KC2[:, NG, :], 0.0).then_inc(pos_zero, 1)
            pool.wait_ge(product, stage["kwvw"][-1] + 1)
            steps.link(nc.gpsimd.memset(earlier, 1.0))
            nc.gpsimd.affine_select(out=earlier, in_=earlier, compare_op=ALU.is_gt, fill=0.0, base=0,
                                    pattern=[[1, EPG], [-1, EPG]], channel_multiplier=0).then_inc(consts, 1)
            nc.gpsimd.memset(acc_rest, 0.0).then_inc(acc_zero, 1)
            pool.wait_ge(product, stage["hid"][1] + 1)
            nc.gpsimd.memset(acc_next, 0.0).then_inc(acc_zero, 1)
            pool.wait_ge(product, stage["cmp"][-1] + 1)
            for name in ("ksvs", "kwvw", "cmp"):
                wait_evacuated(pool, name)
            scale(0)
            norm(0)
            experts(0)
            norm(1)
            wait_evacuated(pool, "kv")
            scale(1)
            norm(2)
            experts(1)
            norm(3)

        @block.tensor
        def _(pe):
            def mm(out, lhsT, rhs, start, stop):
                return nc.tensor.matmul(out, lhsT, rhs, start=start, stop=stop)

            def ada(name, sums_of, cols, gates):
                js = iter(stage[name])
                j = next(js)
                wait_bank(pe, j)
                for n, q in enumerate(cols):
                    last = mm(bank(j)[:, n:n + 1], sums_of[:, q * P:(q + 1) * P], ones[:, 0:1], True, True)
                last.then_inc(product, 1)
                for o in gates:
                    j = next(js)
                    wait_bank(pe, j)
                    mm(bank(j)[:, :], ones[:, :], sums_of[:, o:o + 512], True, True).then_inc(product, 1)

            def turn(name, rows):
                for k, j in enumerate(stage[name]):
                    wait_bank(pe, j)
                    for i in range(NT):
                        last = nc.tensor.transpose(bank(j)[:, i * P:(i + 1) * P], rows[:, i, k * P:(k + 1) * P], ident[:, :])
                    last.then_inc(product, 1)

            def by_columns(js, w, cols, src):
                for j, c in zip(js, cols):
                    wait_bank(pe, j)
                    for k in range(KD):
                        last = mm(bank(j)[:, :], w[:, k, c:c + P], src[:, k, :], k == 0, k == KD - 1)
                    last.then_inc(product, 1)

            def by_tokens(js, w, c, n, src):
                for i, j in enumerate(js):
                    wait_bank(pe, j)
                    for k in range(KD):
                        last = mm(bank(j)[:, 0:n], src[:, k, i * P:(i + 1) * P], w[:, k, c:c + n], k == 0, k == KD - 1)
                    last.then_inc(product, 1)

            def as_matrix(name, n=512, k=KD):
                return slot(name)[:, 0:k * n].rearrange("p (k n) -> p k n", k=k)

            pe.wait_ge(consts, 3)
            pe.wait_ge(c_in, 16)
            j, = stage["cond"]
            nc.tensor.transpose(bank(j)[:, 0:KD], c8, ident[0:KD, 0:KD]).then_inc(product, 1)
            pe.wait_ge(rel_ready, 16)
            pe.wait_ge(oh_in, 16)
            pe.wait_ge(pool_step, 4)
            for j, (o, n) in zip(stage["bias"], ((BACK, 512), (BACK + 512, 128), (NEAR, 384))):
                mm(bank(j)[0:NH, 0:n], relb, OH[:, o:o + n], True, True).then_inc(product, 1)
            pe.wait_ge(table_split, 1)
            for i, j in enumerate(stage["biasc"]):
                wait_bank(pe, j)
                for n in range(NC):
                    o = T + i * P - n * CMP_STRIDE - (CMP_LEN - 1)
                    for part in range(3):
                        last = mm(bank(j)[:, n * NH:(n + 1) * NH], OH16[:, o:o + P], table_parts[:, part, :],
                                  part == 0, part == 2)
                last.then_inc(product, 1)
            pe.wait_ge(small_in, 16 * 7)
            for b, j in enumerate(stage["pos"]):
                wait_bank(pe, j)
                nc.tensor.transpose(bank(j)[:, 0:CK], pos16[:, b, :], ident[0:CK, 0:CK]).then_inc(product, 1)
            pe.wait_ge(ada_sum, 3)
            ada("ada0", acc, range(2 * KD), ())
            pe.wait_ge(x_in, 16)
            turn("hT0", X)
            wait_evacuated(pe, "hT0")
            wait_item(pe, "kcvc")
            by_columns(stage["kcvc"], as_matrix("kcvc"), (0, P, 2 * P, 3 * P), HT)
            for name in ("ksvs", "kwvw"):
                wait_item(pe, name)
                by_columns(stage[name][0:2], as_matrix(name), (0, P), HT)
                by_tokens(stage[name][2:], as_matrix(name), KVW, KVW, HT)
            pe.wait_ge(gl_in, 16)
            j, = stage["gl"]
            wait_bank(pe, j)
            for k in range(KD):
                last = mm(bank(j)[0:3 * NH, :], glw[:, k, :], HT[:, k, :], k == 0, k == KD - 1)
            last.then_inc(product, 1)
            wait_evacuated(pe, "kcvc")
            pe.wait_ge(pos_ready, 2)
            js = iter(stage["hid"])
            for name, src in (("w1k", KC2), ("w1v", VC2)):
                wait_item(pe, name)
                for m in range(2):
                    j = next(js)
                    wait_bank(pe, j)
                    for k in range(CK):
                        last = mm(bank(j)[:, 0:(NG + 1) * NC], as_matrix(name, 256, CK)[:, k, m * P:(m + 1) * P],
                                  src[:, :, k:k + 8 * (NC - 1) + 1:8], k == 0, k == CK - 1)
                    last.then_inc(product, 1)
            j, = stage["glT"]
            wait_bank(pe, j)
            wait_evacuated(pe, "gl")
            for i in range(NT):
                last = nc.tensor.transpose(bank(j)[:, i * 3 * NH:(i + 1) * 3 * NH], gatesT[:, i * P:(i + 1) * P],
                                           ident[0:3 * NH, 0:3 * NH])
            last.then_inc(product, 1)
            wait_evacuated(pe, "hid")
            j, jv = stage["cmp"]
            wait_bank(pe, j)
            for m in range(2):
                last = mm(bank(j)[0:HD, 0:NG * NC], w2[:, 0, m, :], hid[:, 0, m, 0:NG * NC], m == 0, m == 1)
            last.then_inc(product, 1)
            wait_bank(pe, jv)
            for g in range(NG):
                for m in range(2):
                    last = mm(bank(jv)[0:NC, g * HD:(g + 1) * HD], hid[:, 1, m, g * NC:(g + 1) * NC], w2[:, 1, m, :],
                              m == 0, m == 1)
            last.then_inc(product, 1)

            def attention(layer):
                S = A[layer]
                n_units = HPG * U[layer]
                w = slot(f"wq{layer}")[:, 0:KD * KVW].rearrange("p (k n) -> p k n", k=KD)
                s, before = items[f"wq{layer}"]
                with pe.Fori(0, NG) as g:
                    def scores(u):
                        i, b, k0, ext = units[layer][u % U[layer]]
                        if u >= 2:
                            pe.wait_ge(S["logit"], PRIMED + g * n_units + u - 1)
                        apart(pe)
                        mm(ps[4 + u % 2][:, 0:ext], QT[:, u // U[layer], i * P:(i + 1) * P],
                           KT[:, b, bass.ds(g, 1), k0:k0 + ext].rearrange("p o t -> p (o t)"), True, True)\
                            .then_inc(S["score"], 1)

                    def turns(u):
                        ext = units[layer][u % U[layer]][3]
                        pe.wait_ge(S["scaled"], PRIMED + g * n_units + u + 1)
                        if u >= 2:
                            pe.wait_ge(S["pte_act" if u % 2 == 0 else "pte_dve"], PRIMED + g * (n_units // 2) + u // 2)
                        for k in range(ext // P):
                            last = nc.tensor.transpose(ps[6 + u % 2][:, k * P:(k + 1) * P],
                                                       LP[:, u % 4, k * P:(k + 1) * P], ident[:, :])
                        last.then_inc(S["turn"], 1)

                    def values(q):
                        hh, b = divmod(q, BRANCHES[layer])
                        out = ps[0 if hh % 2 else 3]
                        for engine in ("act", "dve"):
                            pe.wait_ge(S[f"pte_{engine}"], PRIMED + g * (n_units // 2) + 2 * q + 2)
                        if q == 0:
                            pe.wait_ge(S["vg"], PRIMED + g + 1)
                        if b == 0:
                            pe.wait_ge(S["heads"], PRIMED + g * HPG + max(hh - 1, 0))
                        for k in (0, 2, 1, 3) if layer == 1 else range(NT):
                            n = min(NT - k, 2) if layer == 1 else NT - k
                            first = pt_block(layer, k, k)
                            ends = layer == 1 and k == NT - 1
                            last = mm(out[0:HD, k * P:(k + n) * P], VG[:, b, k, :], PT[q % 2][:, first * P:(first + n) * P],
                                      b == 0 and k == 0, ends)
                        if layer == 0 and b == 1:
                            pe.wait_ge(S["cpt"], PRIMED + g * HPG + hh + 1)
                            last = mm(out[0:HD, :], VCG[0:NC, :], PcT[0:NC, :], False, True)
                        last.then_inc(S["pv"], 1)

                    pe.wait_ge(landed[s], g * 16 + (before + 16))
                    if layer == 0:
                        pe.wait_ge(S["cpt"], PRIMED + g * HPG)
                        pe.wait_ge(S["cshift"], PRIMED + g * HPG)
                    for m in range(2):
                        for k in range(KD):
                            last = mm(ps[1 + m][:, :], w[:, k, m * P:(m + 1) * P], HT[:, k, :], k == 0, k == KD - 1)
                        last.then_inc(S["qproj"], 1)
                    pe.wait_ge(S["qt"], PRIMED + g * 2 + 2)
                    for u in range(n_units + LAG + 1):
                        hh, n = divmod(u, U[layer])
                        if u < n_units:
                            if layer == 0 and n == 0:
                                if hh:
                                    pe.wait_ge(S["cshift"], PRIMED + g * HPG + hh)
                                apart(pe)
                                for i in range(NT):
                                    last = mm(ps[1][:, i * NCP:i * NCP + NC], QT[:, hh, i * P:(i + 1) * P],
                                              KC[:, bass.ds(g, 1), :].rearrange("p o n -> p (o n)"), True, True)
                                last.then_inc(S["cscore"], 1)
                            scores(u)
                        if 0 <= u - LAG < n_units:
                            turns(u - LAG)
                        if layer == 0 and n == 5 and u < n_units:
                            pe.wait_ge(S["cprob"], PRIMED + g * HPG + hh + 1)
                            if hh:
                                pe.wait_ge(S["cpt"], PRIMED + g * HPG + hh)
                            for i in range(NT):
                                last = nc.tensor.transpose(ps[2][0:NC, i * P:(i + 1) * P], Pc[:, i, 0:NC], ident[:, :])
                            last.then_inc(S["cturn"], 1)
                        if u >= LAG + 4 and (u - LAG) % 4 == 0:
                            values((u - LAG) // 4 - 1)

            def turn_tile(name, i):
                for h, j in enumerate(stage[name]):
                    wait_bank(pe, j)
                    for k in range(4):
                        last = nc.tensor.transpose(bank(j)[:, k * P:(k + 1) * P], X[:, i, (4 * h + k) * P:(4 * h + k + 1) * P],
                                                   ident[:, :])
                    last.then_inc(product, 1)

            def output(layer):
                pe.wait_ge(A[layer]["heads"], PRIMED + NH)

                def normed(i):
                    pe.wait_ge(ln_done, NT * (2 * layer) + i + 1)
                    turn_tile(f"hf{layer}.{i}", i)

                def router(i):
                    wait_evacuated(pe, f"hf{layer}.{i}")
                    for k in range(KD):
                        last = mm(ps[4][:, i * N_EXP:(i + 1) * N_EXP], HT[:, k, i * P:(i + 1) * P], routw[:, k, :],
                                  k == 0, k == KD - 1)
                    return last

                for i in range(NT):
                    for b, j in enumerate(stage[f"wo{layer}.{i}"]):
                        name = f"wo{layer}.{b}"
                        wait_item(pe, name)
                        wait_bank(pe, j)
                        for k in range(KD):
                            last = mm(bank(j)[:, :], OT[:, k, i * P:(i + 1) * P], as_matrix(name)[:, k, :],
                                      k == 0, k == KD - 1)
                        last.then_inc(product, 1)
                    if i == NT - 1 and layer == 0:
                        ada("next", acc_next, [*range(2 * KD), *range(3 * KD, 5 * KD)],
                            (2 * D, 2 * D + 512, 5 * D, 5 * D + 512))
                    if i:
                        normed(i - 1)
                for i in range(NT - 1):
                    router(i)
                normed(NT - 1)
                router(NT - 1).then_inc(product, 1)

            def find_slots(layer):
                j, = stage[f"place{layer}"]
                wait_bank(pe, j)
                pe.wait_ge(routed[layer], 1)
                chosen = sel.rearrange("p i e -> p (i e)")
                mm(bank(j)[:, 0:NT * N_EXP], upper[:, :], chosen, True, True)
                mm(bank(j)[:, NT * N_EXP:2 * NT * N_EXP], ones[:, :], chosen, True, True).then_inc(product, 1)
                for q, j in enumerate(stage[f"slots{layer}"]):
                    wait_bank(pe, j)
                    pe.wait_ge(onehot_ready[layer], q + 1)
                    for e in range(N_EXP)[ROUTED_FIRST[q]]:
                        for i in range(NT):
                            last = mm(bank(j)[:, e * ROUTE:(e + 1) * ROUTE], onehot[:, e, i, :], routes[:, i, e, :],
                                      i == 0, i == NT - 1)
                    last.then_inc(product, 1)

            def turn_tokens(src, banks):
                for k in range(KD):
                    last = nc.tensor.transpose(ps[banks[k // 4]][:, (k % 4) * P:(k % 4 + 1) * P],
                                               src[:, k * P:(k + 1) * P], ident[:, :])
                return last

            def experts(layer):
                S = M[layer]

                def tokens_in(r, n):
                    v = r * SLOTS + n
                    pe.wait_ge(gathered[layer][n % 2], r * 32 + 16 * (n // 2 + 1))
                    pe.wait_ge(S["xact"], PRIMED + v)
                    pe.wait_ge(S["xdve"], PRIMED + v)
                    turn_tokens(Xg[:, n % 2, :], (0, 1)).then_inc(S["xturn"], 1)

                def hidden(r, n):
                    v = r * SLOTS + n
                    pe.wait_ge(landed[WS[layer][n % SLOTS]], r * 48 + (before_experts[layer][WS[layer][n % SLOTS]] + 48 * (n // SLOTS + 1)))
                    pe.wait_ge(S["xact"], PRIMED + v + 1)
                    pe.wait_ge(S["xdve"], PRIMED + v + 1)
                    if not isinstance(v, int) or v >= 2:
                        pe.wait_ge(S["hmid"], PRIMED + v - 1)
                    w = gate_up(expert_slot(layer, n))
                    for k in range(KD):
                        last = mm(ps[2 + n % 2][:, :], XgT[:, n % 2, k, :], w[:, k, :, :], k == 0, k == KD - 1)
                    last.then_inc(S["gu"], 1)

                def step(r, n):
                    v = r * SLOTS + n
                    if not isinstance(r, int) or v + 1 < N_EXP:
                        hidden(r, n + 1)
                    pe.wait_ge(S["hmid"], PRIMED + v + 1)
                    for m in range(2):
                        last = nc.tensor.transpose(ps[4 + n % 2][:, m * P:(m + 1) * P], hmid[:, n % 2, m * P:(m + 1) * P],
                                                   ident[:, :])
                    last.then_inc(S["hturn"], 1)
                    if not isinstance(r, int) or v + 2 < N_EXP:
                        tokens_in(r, n + 2)
                    pe.wait_ge(S["hmt"], PRIMED + v + 1)
                    pe.wait_ge(S["ydve"], PRIMED + v)
                    w = down(expert_slot(layer, n))
                    for b in range(2):
                        for k in range(2):
                            last = mm(ps[6 + b][:, :], hmidT[:, n % 2, k, :], w[:, k, b * 512:(b + 1) * 512], k == 0, k == 1)
                    last.then_inc(S["down"], 1)

                wait_all(f"slots{layer}")
                tokens_in(0, 0)
                hidden(0, 0)
                tokens_in(0, 1)
                with pe.Fori(0, ROUNDS - 1) as r:
                    for n in range(SLOTS):
                        step(r, n)
                for n in range(SLOTS):
                    step(ROUNDS - 1, n)
                flag = pe.value_load(many[0:1, layer:layer + 1], min_val=0, max_val=1)
                with pe.If(flag == 1):
                    more_tokens(layer)

            def more_tokens(layer):
                S = FURTHER[layer]
                pe.wait_ge(M[layer]["ydve"], PRIMED + N_EXP)
                with pe.Fori(0, N_EXP) as e:
                    for b in range(3):
                        v = PRIMED + e * 3 + b
                        pe.wait_ge(S["onehot"], v + 1)
                        apart(pe)
                        for i in range(NT):
                            last = mm(ps[5][:, 0:ROUTE], onehot[:, 0, i, :],
                                      routes[:, i, bass.ds(e, 1), :].rearrange("p o c -> p (o c)"), i == 0, i == NT - 1)
                        last.then_inc(S["slots"], 1)
                        pe.wait_ge(S["gather"], e * 48 + 16 * (b + 1))
                        turn_tokens(Xg[:, 0, :], (0, 1)).then_inc(S["xturn"], 1)
                        pe.wait_ge(S["w"], e * 48 + 48)
                        pe.wait_ge(S["xact"], v + 1)
                        for k in range(KD):
                            last = mm(ps[2][:, :], XgT[:, 0, k, :], gate_up(ring[:, 0, :])[:, k, :, :], k == 0, k == KD - 1)
                        last.then_inc(S["gu"], 1)
                        pe.wait_ge(S["hmid"], v + 1)
                        for m in range(2):
                            last = nc.tensor.transpose(ps[4][:, m * P:(m + 1) * P], hmid[:, 0, m * P:(m + 1) * P], ident[:, :])
                        last.then_inc(S["hturn"], 1)
                        pe.wait_ge(S["hmt"], v + 1)
                        for h in range(2):
                            for k in range(2):
                                last = mm(ps[6 + h][:, :], hmidT[:, 0, k, :], down(ring[:, 0, :])[:, k, h * 512:(h + 1) * 512],
                                          k == 0, k == 1)
                        last.then_inc(S["down"], 1)

            def wait_all(last):
                for e in "AD":
                    pe.wait_ge(evac[e], max(nth[j] for j in range(stage[last][-1] + 1) if jobs[j] == e))

            wait_all("cmp")
            attention(0)
            pe.wait_ge(late_sum[1], PRIMED + NH)
            pe.wait_ge(A[0]["heads"], PRIMED + NH)
            ada("rest", acc_rest, range(KD, 3 * KD), (0, 512, 3 * D, 3 * D + 512))
            output(0)
            find_slots(0)
            experts(0)
            for i in range(NT):
                pe.wait_ge(ln_done, NT + i + 1)
                turn_tile(f"xT1.{i}", i)
            for i in range(NT):
                wait_evacuated(pe, f"xT1.{i}")
            wait_item(pe, "wkv")
            by_columns(stage["kv"][0:2], as_matrix("wkv"), (0, P), XTk)
            by_tokens(stage["kv"][2:], as_matrix("wkv"), KVW, KVW, XTk)
            pe.wait_ge(hT1_ready, KD)
            wait_all("kv")
            attention(1)
            output(1)
            find_slots(1)
            experts(1)

        @block.scalar
        def _(act):
            steps = Steps(act, act_step)

            def arrived(j):
                act.wait_ge(product, j + 1)

            def copy(out, j, src, scale=1.0):
                arrived(j)
                nc.scalar.activation(out, src, ACT.Copy, scale=scale).then_inc(evac["A"], 1)

            def mine(name):
                return [(n, j) for n, j in enumerate(stage[name]) if jobs[j] == "A"]

            (_, j), = mine("cond")
            arrived(j)
            nc.scalar.activation(cond[:, :], bank(j)[:, 0:KD], ACT.Silu).then_inc(evac["A"], 1)
            for i, j in mine("biasc"):
                copy(BC[:, i, :, :].rearrange("p n h -> p (n h)"), j, bank(j)[:, 0:NC * NH], -1.0)
            for b, j in mine("pos"):
                copy(posT[:, b, :], j, bank(j)[:, 0:CK])
            wait_evacuated(act, "pos")

            def modulated(name, layer, sub):
                for k, j in mine(name):
                    arrived(j)
                    nc.scalar.activation(HT[:, k, :], bank(j)[:, :], ACT.Identity,
                                         bias=adaC[:, layer, 2 * sub, k:k + 1],
                                         scale=adaC[:, layer, 2 * sub + 1, k:k + 1]).then_inc(evac["A"], 1)

            def modulated_tile(layer, i):
                (_, j), = mine(f"hf{layer}.{i}")
                arrived(j)
                for k in range(4):
                    last = nc.scalar.activation(HT[:, k, i * P:(i + 1) * P], bank(j)[:, k * P:(k + 1) * P], ACT.Identity,
                                                bias=adaC[:, layer, 2, k:k + 1], scale=adaC[:, layer, 3, k:k + 1])
                last.then_inc(evac["A"], 1)

            def ada_rows(name, layer):
                for n, j in mine(name):
                    arrived(j)
                    sub, q = divmod(n - 1, 2)
                    nc.scalar.activation(G[:, layer, sub, q * 512:(q + 1) * 512], bank(j)[:, :], ACT.Identity,
                                         bias=ones[:, 0:1]).then_inc(evac["A"], 1)

            wait_evacuated(act, "ada0")
            modulated("hT0", 0, 0)
            act.wait_ge(pos_zero, 2)
            for b, dst in enumerate((KC2, VC2)):
                nc.scalar.activation(dst[:, NG, 0:CK], posT[:, b, :], ACT.Copy).then_inc(pos_ready, 1)
            for n, j in mine("kcvc"):
                arrived(j)
                split_halves(lambda o, i: nc.scalar.activation(o, i, ACT.Copy), KC2 if n < 2 else VC2, n % 2, bank(j)).then_inc(evac["A"], 1)

            def keys_values(name, b):
                for n, j in mine(name):
                    arrived(j)
                    if n < 2:
                        for half in range(2):
                            last = nc.scalar.activation(KT[:, b, 2 * n + half, :], bank(j)[half * HD:(half + 1) * HD, :], ACT.Copy)
                    else:
                        last = nc.scalar.activation(V[:, b, n - 2, :], bank(j)[:, 0:KVW], ACT.Copy)
                    last.then_inc(evac["A"], 1)

            keys_values("ksvs", 0)
            keys_values("kwvw", 1)
            (_, j), = mine("gl")
            arrived(j)
            nc.scalar.activation(gatesT, bank(j)[0:3 * NH, :], ACT.Sigmoid).then_inc(evac["A"], 1)
            for n, j in mine("hid"):
                act.wait_ge(pos_share, n + 1)
                nc.scalar.activation(hid[:, n // 2, n % 2, 0:NG * NC], bank(j)[:, 0:NG * NC], ACT.Gelu_apprx_tanh,
                                     bias=posb[:, n // 2, n % 2:n % 2 + 1]).then_inc(evac["A"], 1)
            (_, j), = mine("glT")
            copy(GT[:, :, :].rearrange("p i n -> p (i n)"), j, bank(j)[:, 0:NT * 3 * NH])

            def attention(layer):
                S = A[layer]
                n_units = HPG * U[layer]
                with act.Fori(0, NG) as g:
                    for m in range(2):
                        act.wait_ge(S["qproj"], PRIMED + g * 2 + m + 1)
                        for half in range(2):
                            last = nc.scalar.activation(QT[:, 2 * m + half, :], ps[1 + m][half * HD:(half + 1) * HD, :],
                                                        ACT.Copy, scale=-SCALE)
                        last.then_inc(S["qt"], 1)
                    for u in range(n_units + LAG + 2):
                        hh, n = divmod(u, U[layer])
                        if u < n_units:
                            i, b, k0, ext = units[layer][n]
                            col = i * BRANCHES[layer] + b
                            if layer == 0 and n == 1:
                                act.wait_ge(S["cshift"], PRIMED + g * HPG + hh + 1)
                                nc.scalar.activation(Pc[:, :, 0:NC], Pc[:, :, 0:NC], ACT.Exp, scale=-1.0).then_inc(S["cexp"], 1)
                            act.wait_ge(S["logit"], PRIMED + g * n_units + u + 1)
                            p = LP[:, u % 4, 0:ext + layer]
                            nc.scalar.activation(p, p, ACT.Exp, scale=-1.0, bias=mins[:, hh % 2, col:col + 1],
                                                 accum_out=sums[:, hh % 2, col:col + 1]).then_inc(S["expo"], 1)
                            if layer == 0 and n == 6:
                                act.wait_ge(S["cturn"], PRIMED + g * HPG + hh + 1)
                                nc.scalar.activation(PcT[0:NC, :], ps[2][0:NC, :], ACT.Copy).then_inc(S["cpt"], 1)
                        v = u - LAG
                        if 0 <= v < n_units and v % 2 == 0:
                            act.wait_ge(S["turn"], PRIMED + g * n_units + v + 1)
                            q = v // 4
                            if q >= 2:
                                act.wait_ge(S["pv"], PRIMED + g * (HPG * BRANCHES[layer]) + q - 1)
                            copy_turned(lambda o, x: nc.scalar.activation(o, x, ACT.Copy), layer, q % 2,
                                        units[layer][v % U[layer]][0], ps[6]).then_inc(S["pte_act"], 1)
                        q, r = divmod(u - LAG - 1, 4)
                        if r == 0 and q >= 1 and q % BRANCHES[layer] == 0:
                            done = q // BRANCHES[layer] - 1
                            act.wait_ge(S["pv"], PRIMED + g * (HPG * BRANCHES[layer]) + q)
                            apart(act)
                            half = done % 2
                            nc.scalar.activation(OT[half * HD:(half + 1) * HD, bass.ds(g * 2 + done // 2, 1), :].rearrange(
                                "p o t -> p (o t)"), ps[0 if half else 3][0:HD, :], ACT.Copy).then_inc(S["heads"], 1)

            def output(layer):
                wait_evacuated(act, "rest")
                for i in range(NT):
                    if i == NT - 1 and layer == 0:
                        ada_rows("next", 1)
                        wait_evacuated(act, "next")
                    if i:
                        modulated_tile(layer, i - 1)
                modulated_tile(layer, NT - 1)
                (_, j), = mine(f"rout{layer}")
                arrived(j)
                nc.scalar.activation(rt[:, 0, :, :].rearrange("p i e -> p (i e)"), ps[4][:, 0:NT * N_EXP],
                                     ACT.Sigmoid).then_inc(evac["A"], 1)

            def tokens_modulated(src, dst, layer, k0):
                for k in range(4):
                    last = nc.scalar.activation(dst[:, k0 + k, :], src[:, k * P:(k + 1) * P], ACT.Identity,
                                                bias=adaC[:, layer, 2, k0 + k:k0 + k + 1],
                                                scale=adaC[:, layer, 3, k0 + k:k0 + k + 1])
                return last

            def experts(layer):
                S = M[layer]

                def tokens_in(r, n):
                    act.wait_ge(S["xturn"], PRIMED + r * SLOTS + n + 1)
                    tokens_modulated(ps[0], XgT[:, n % 2], layer, 0).then_inc(S["xact"], 1)

                def hidden(r, n):
                    v = r * SLOTS + n
                    act.wait_ge(S["gu"], PRIMED + v + 1)
                    if not isinstance(v, int) or v >= 2:
                        act.wait_ge(S["hmid"], PRIMED + v - 1)
                    nc.scalar.activation(silu[:, n % 2, :], ps[2 + n % 2][:, 0:D_EXP], ACT.Silu).then_inc(S["silu"], 1)

                def step(r, n):
                    v = r * SLOTS + n
                    if not isinstance(r, int) or v + 1 < N_EXP:
                        hidden(r, n + 1)
                    act.wait_ge(S["hturn"], PRIMED + v + 1)
                    nc.scalar.activation(hmidT[:, n % 2, :, :].rearrange("p m n -> p (m n)"), ps[4 + n % 2][:, 0:2 * P],
                                         ACT.Copy).then_inc(S["hmt"], 1)
                    if not isinstance(r, int) or v + 2 < N_EXP:
                        tokens_in(r, n + 2)

                act.wait_ge(slots_ready[layer], 2)
                tokens_in(0, 0)
                hidden(0, 0)
                tokens_in(0, 1)
                with act.Fori(0, ROUNDS - 1) as r:
                    for n in range(SLOTS):
                        step(r, n)
                for n in range(SLOTS):
                    step(ROUNDS - 1, n)
                flag = act.value_load(many[0:1, layer:layer + 1], min_val=0, max_val=1)
                with act.If(flag == 1):
                    S = FURTHER[layer]
                    with act.Fori(0, N_EXP) as e:
                        for b in range(3):
                            v = PRIMED + e * 3 + b
                            act.wait_ge(S["xturn"], v + 1)
                            tokens_modulated(ps[0], XgT[:, 0], layer, 0)
                            tokens_modulated(ps[1], XgT[:, 0], layer, 4).then_inc(S["xact"], 1)
                            act.wait_ge(S["gu"], v + 1)
                            nc.scalar.activation(silu[:, 0, :], ps[2][:, 0:D_EXP], ACT.Silu).then_inc(S["silu"], 1)
                            act.wait_ge(S["hturn"], v + 1)
                            nc.scalar.activation(hmidT[:, 0, :, :].rearrange("p m n -> p (m n)"), ps[4][:, 0:2 * P],
                                                 ACT.Copy).then_inc(S["hmt"], 1)

            attention(0)
            act.wait_ge(consts, 3)
            ada_rows("rest", 0)
            output(0)
            experts(0)
            act.wait_ge(ln_done, 2 * NT)
            for i in range(NT):
                (_, j), = mine(f"xT1.{i}")
                copy(XTk[:, 0:4, i * P:(i + 1) * P], j, bank(j)[:, :].rearrange("p (k t) -> p k t", k=4))
            keys_values("kv", 0)
            attention(1)
            output(1)
            experts(1)

        @block.vector
        def _(dve):
            steps = Steps(dve, dve_step)
            link = steps.link

            def arrived(j):
                dve.wait_ge(product, j + 1)

            def mine(name):
                return [(n, j) for n, j in enumerate(stage[name]) if jobs[j] == "D"]

            def ada_sums():
                dve.wait_ge(acc_bias, 16)
                k = 0
                for q in range(3):
                    wait_item(dve, f"ada{q}")
                    w = slot(f"ada{q}")[:, 0:CHUNK[q] * PART].rearrange("p (k n) -> p k n", k=CHUNK[q])
                    for kk in range(CHUNK[q]):
                        ins = nc.vector.scalar_tensor_tensor(acc, w[:, kk, :], cond[:, k:k + 1], acc, ALU.mult, ALU.add)
                        k += 1
                        if kk == CHUNK[q] - 1:
                            ins.then_inc(ada_sum, 1)
                            dve.wait_ge(ada_sum, q + 1)
                        else:
                            link(ins)

            def ada_columns(name, layer, rows):
                (_, j), = mine(name)
                arrived(j)
                for n, r in enumerate(rows):
                    src = bank(j)[:, n * KD:(n + 1) * KD]
                    if r % 2:
                        last = nc.vector.tensor_scalar(adaC[:, layer, r, :], src, 1.0, None, ALU.add)
                    else:
                        last = nc.vector.tensor_copy(adaC[:, layer, r, :], src)
                last.then_inc(evac["D"], 1)

            dve.wait_ge(rel_ready, 16)
            dve.wait_ge(pool_step, 4)
            dve.wait_ge(oh_in, 16)
            nc.vector.tensor_copy(OH16, OH[:, AHEAD:AHEAD + 1024])
            link(nc.vector.tensor_copy(table_parts[:, 0, :], relb))
            link(nc.vector.tensor_tensor(table_left, relb, table_parts[:, 0, :], ALU.subtract))
            link(nc.vector.tensor_copy(table_parts[:, 1, :], table_left))
            link(nc.vector.tensor_tensor(table_left, table_left, table_parts[:, 1, :], ALU.subtract))
            nc.vector.tensor_copy(table_parts[:, 2, :], table_left).then_inc(table_split, 1)
            for (n, j), (o, w) in zip(mine("bias"), ((0, 512), (512, 128), (640, 384))):
                arrived(j)
                nc.vector.tensor_scalar(biasrow[:, o:o + w], bank(j)[0:NH, 0:w], -1.0, None, ALU.mult).then_inc(evac["D"], 1)
            wait_evacuated(dve, "cond")
            ada_sums()
            ada_columns("ada0", 0, (0, 1))

            def modulated(name, layer, sub):
                for k, j in mine(name):
                    arrived(j)
                    nc.vector.tensor_scalar(HT[:, k, :], bank(j)[:, :], adaC[:, layer, 2 * sub + 1, k:k + 1],
                                            adaC[:, layer, 2 * sub, k:k + 1], ALU.mult, ALU.add).then_inc(evac["D"], 1)

            def keys_values(name, b):
                for n, j in mine(name):
                    arrived(j)
                    if n < 2:
                        for half in range(2):
                            last = nc.vector.tensor_copy(KT[:, b, 2 * n + half, :], bank(j)[half * HD:(half + 1) * HD, :])
                    else:
                        last = nc.vector.tensor_copy(V[:, b, n - 2, :], bank(j)[:, 0:KVW])
                    last.then_inc(evac["D"], 1)

            wait_evacuated(dve, "ada0")
            modulated("hT0", 0, 0)
            for n, j in mine("kcvc"):
                arrived(j)
                split_halves(nc.vector.tensor_copy, KC2 if n < 2 else VC2, n % 2, bank(j)).then_inc(evac["D"], 1)
            keys_values("ksvs", 0)
            keys_values("kwvw", 1)
            dve.wait_ge(small_in, 16 * 7)
            link(nc.vector.tensor_scalar(nsink[:, :], nsink[:, :], -1.0, None, ALU.mult))
            for n, j in enumerate(stage["hid"]):
                arrived(j)
                nc.vector.tensor_copy(posb[:, n // 2, n % 2:n % 2 + 1], bank(j)[:, NG * NC:NG * NC + 1]).then_inc(pos_share, 1)
            (_, j), (_, jv) = mine("cmp")
            arrived(j)
            nc.vector.tensor_copy(KC[:, :, :].rearrange("p g n -> p (g n)"), bank(j)[0:HD, 0:NG * NC]).then_inc(evac["D"], 1)
            arrived(jv)
            nc.vector.tensor_copy(VC[0:NC, :], bank(jv)[0:NC, 0:KVW]).then_inc(evac["D"], 1)

            def attention(layer, first=0, last=NG, late=None):
                S = A[layer]
                sums_of = acc_rest if late == 0 else acc_next
                skip = PART if late == 0 else 0
                PIECE = 1024
                n_units = HPG * U[layer]
                nu = U[layer]
                per = HPG * (7 if layer == 0 else 0)
                with dve.Fori(first, last) as g:
                    steps.enter(g - first, per)

                    def late_piece(hh, n):
                        cols = late_columns(late, n // 4)
                        pieces = (cols.stop - cols.start) // PIECE
                        at = {2: (2, 3), 3: (1, 2, 3)}[pieces]
                        if n % 4 not in at:
                            return
                        o = cols.start + at.index(n % 4) * PIECE
                        if n % 4 == at[0]:
                            if n < 4:
                                s, before = items["late"]
                                dve.wait_ge(landed[s], g * (16 * HPG) + (before + 16 * (hh + 1)))
                            else:
                                dve.wait_ge(late_second, g * (16 * HPG) + 16 * (hh + 1))
                            dve.wait_ge(late_sum[n // 4], PRIMED + g * HPG + hh)
                            apart(dve)
                        k = g * HPG + (hh - first * HPG)
                        total = sums_of[:, o - skip:o - skip + PIECE]
                        add = nc.vector.scalar_tensor_tensor(total, slot("late")[:, o:o + PIECE], cond[:, bass.ds(k, 1)],
                                                             total, ALU.mult, ALU.add)
                        if o + PIECE == cols.stop:
                            add.then_inc(late_sum[n // 4], 1)

                    for u in range(n_units + LAG + 1):
                        hh, n = divmod(u, nu)
                        if u < n_units:
                            i, b, k0, ext = units[layer][n]
                            col = i * BRANCHES[layer] + b
                            if layer == 0 and n == 1:
                                dve.wait_ge(S["cscore"], PRIMED + g * HPG + hh + 1)
                                dve.wait_ge(S["cturn"], PRIMED + g * HPG + hh)
                                link(nc.vector.tensor_tensor(
                                    Pc[:, :, 0:NC], ps[1][:, 0:NT * NCP].rearrange("p (i n) -> p i n", i=NT)[:, :, 0:NC],
                                    BC[:, :, :, bass.ds(g * HPG + hh, 1)].rearrange("p i n o -> p i (n o)"), ALU.add))
                                link(nc.vector.tensor_reduce(small[:, 40:44], Pc[:, :, 0:NC], AX.X, ALU.min))
                                nc.vector.tensor_tensor(Pc[:, :, 0:NC], Pc[:, :, 0:NC],
                                                        small[:, 40:44].unsqueeze(2).to_broadcast([P, NT, NC]),
                                                        ALU.subtract).then_inc(S["cshift"], 1)
                            if layer == 0 and n == 3:
                                dve.wait_ge(S["cexp"], PRIMED + g * HPG + hh + 1)
                                link(nc.vector.tensor_tensor(Pc[:, :, 0:NC], Pc[:, :, 0:NC], maskc[:, :, :], ALU.mult))
                                link(nc.vector.tensor_reduce(small[:, 44:48], Pc[:, :, 0:NC], AX.X, ALU.add))
                                link(nc.vector.tensor_scalar(small[:, 48:52], small[:, 44:48], 1e-30, None, ALU.max))
                                link(nc.vector.reciprocal(small[:, 52:56], small[:, 48:52]))
                                gates = GT[:, :, :].rearrange("p i (b h) -> p i b h", b=3)
                                link(nc.vector.tensor_tensor(small[:, 56:60], small[:, 52:56],
                                                             gates[:, :, 0, bass.ds(g * HPG + hh, 1)].rearrange("p i o -> p (i o)"),
                                                             ALU.mult))
                                nc.vector.tensor_tensor(Pc[:, :, 0:NC], Pc[:, :, 0:NC],
                                                        small[:, 56:60].unsqueeze(2).to_broadcast([P, NT, NC]),
                                                        ALU.mult).then_inc(S["cprob"], 1)
                            if layer == 0 and n == 0:
                                nc.vector.tensor_copy(gates_now[:, hh % 2, :], GT[:, :, :].rearrange(
                                    "p i (b h) -> p i b h", b=3)[:, :, 1:3, bass.ds(g * HPG + hh, 1)].rearrange(
                                        "p i b o -> p i (b o)"))
                            dve.wait_ge(S["score"], PRIMED + g * n_units + u + 1)
                            dve.wait_ge(S["bias_odd" if hh % 2 else "bias_even"], g * (8 * HPG) + 16 * (hh // 2 + 1))
                            if u >= 4:
                                dve.wait_ge(S["turn"], PRIMED + g * n_units + u - 3)
                            apart(dve)
                            full = WIDEST[layer]
                            if layer == 1:
                                nc.vector.tensor_copy(LP[:, u % 4, ext:ext + 1], nsink[:, bass.ds(g * HPG + hh, 1)])
                                if n == 0:
                                    nc.vector.tensor_copy(sink_now[:, hh % 2:hh % 2 + 1],
                                                          nsink[:, bass.ds(g * HPG + hh, 1)]).then_inc(S["cprob"], 1)
                                    dve.wait_ge(S["cprob"], PRIMED + g * HPG + hh + 1)
                                    apart(dve)
                            start = sink_now[:, hh % 2:hh % 2 + 1] if layer == 1 else 3.0e38
                            nc.vector.tensor_tensor_reduce(LP[:, u % 4, 0:ext], ps[4 + u % 2][:, 0:ext],
                                                           B[:, hh % 2, full - ext:full], 1.0, start, ALU.add, ALU.min,
                                                           mins[:, hh % 2, col:col + 1]).then_inc(S["logit"], 1)
                        w = u - 1
                        if layer in INVERTS and 0 <= w < n_units:
                            head, pos = divmod(w, nu)
                            c = units[layer][pos][0] * BRANCHES[layer] + units[layer][pos][1]
                            dve.wait_ge(S["expo"], PRIMED + g * n_units + w + 1)
                            nc.vector.reciprocal(inverse[:, w % 4:w % 4 + 1], sums[:, head % 2, c:c + 1]).then_inc(S["inverse"], 1)
                        v = u - LAG
                        if 0 <= v < n_units and v % 2 == 1:
                            dve.wait_ge(S["turn"], PRIMED + g * n_units + v + 1)
                            q = v // 4
                            if q >= 2:
                                dve.wait_ge(S["pv"], PRIMED + g * (HPG * BRANCHES[layer]) + q - 1)
                            copy_turned(nc.vector.tensor_copy, layer, q % 2, units[layer][v % nu][0],
                                        ps[7]).then_inc(S["pte_dve"], 1)
                        if late is not None and u < n_units:
                            late_piece(hh, n)
                steps.leave(last - first)

            def residual(n, i, b, branch, src_psum):
                x = X[:, i, b * 512:(b + 1) * 512]
                y = WORK[:, b * 512:(b + 1) * 512]
                ins = nc.vector.tensor_tensor(y, branch, G[:, n // 2, n % 2, b * 512:(b + 1) * 512], ALU.mult)
                if src_psum:
                    ins.then_inc(evac["D"], 1)
                    dve.wait_ge(evac["D"], src_psum)
                else:
                    link(ins)
                link(nc.vector.scalar_tensor_tensor(x, x, ALPHA, y, ALU.mult, ALU.add))
                link(nc.vector.bn_stats(stats[:, i, b, :], x))

            def norm_stats(n, i):
                link(nc.vector.bn_aggr(mv[:, i, 0:2], stats[:, i, :, :].rearrange("p b s -> p (b s)")))
                nc.vector.tensor_scalar(mv[:, i, 1:2], mv[:, i, 1:2], LN_EPS, None, ALU.add).then_inc(ln_var, 1)

            def norm_apply(n, i):
                dve.wait_ge(ln_in, 32 * (n + 1))
                x = X[:, i, :]
                link(nc.vector.scalar_tensor_tensor(x, x, mv[:, i, 0:1], lng, ALU.subtract, ALU.mult))
                dve.wait_ge(ln_rstd, NT * n + i + 1)
                nc.vector.scalar_tensor_tensor(x, x, mv[:, i, 2:3], lnb, ALU.mult, ALU.add).then_inc(ln_done, 1)

            def output(layer):
                wait_evacuated(dve, "rest" if layer == 0 else "next")

                def modulated_tile(i):
                    (_, j), = mine(f"hf{layer}.{i}")
                    arrived(j)
                    for k in range(4, KD):
                        last = nc.vector.tensor_scalar(HT[:, k, i * P:(i + 1) * P], bank(j)[:, (k - 4) * P:(k - 3) * P],
                                                       adaC[:, layer, 3, k:k + 1], adaC[:, layer, 2, k:k + 1],
                                                       ALU.mult, ALU.add)
                    last.then_inc(evac["D"], 1)

                for i in range(NT):
                    for b, j in enumerate(stage[f"wo{layer}.{i}"]):
                        arrived(j)
                        residual(2 * layer, i, b, bank(j)[:, :], nth[j])
                    norm_stats(2 * layer, i)
                    norm_apply(2 * layer, i)
                    if i == NT - 1 and layer == 0:
                        ada_columns("next", 1, (0, 1, 2, 3))
                    if i:
                        modulated_tile(i - 1)
                modulated_tile(NT - 1)

            def route(layer):
                wait_evacuated(dve, f"rout{layer}")
                dve.wait_ge(consts, 8)
                s, sbias, rank, tmp = (rt[:, n, :, :] for n in range(4))
                score = rt[:, 5, :, 0:NE_GRP]
                best = rt[:, 6, :, 0:1]
                inverse = rt[:, 7, :, 0:1]
                group_rank = rt[:, 7, :, 4:4 + NE_GRP]
                above, equal = (rt[:, n:n + 4, :, :].rearrange("p s i e -> p (s i e)")
                                .rearrange("p (n a b) -> p n a b", a=EPG, b=EPG) for n in (8, 12))
                tt = nc.vector.tensor_tensor

                def ranks(x, out):
                    n = x.shape[1]
                    shape = [P, n, EPG, EPG]
                    a, b = x.unsqueeze(3).to_broadcast(shape), x.unsqueeze(2).to_broadcast(shape)
                    link(tt(equal[:, 0:n], b, a, ALU.is_equal))
                    link(tt(above[:, 0:n], b, a, ALU.is_gt))
                    link(tt(equal[:, 0:n], equal[:, 0:n], earlier.unsqueeze(1).to_broadcast(shape), ALU.mult))
                    link(tt(above[:, 0:n], above[:, 0:n], equal[:, 0:n], ALU.add))
                    link(nc.vector.tensor_reduce(out, above[:, 0:n], AX.X, ALU.add))

                def in_groups(x):
                    return x.rearrange("p i (g e) -> p (i g) e", e=EPG)

                link(tt(sbias, s, routb[:, :].unsqueeze(1).to_broadcast([P, NT, N_EXP]), ALU.add))
                ranks(in_groups(sbias), in_groups(rank))
                link(nc.vector.tensor_scalar(sel, rank, 2.0, None, ALU.is_lt))
                link(tt(tmp, sel, sbias, ALU.mult))
                link(nc.vector.tensor_reduce(score, tmp.rearrange("p i (g e) -> p i g e", e=EPG), AX.X, ALU.add))
                ranks(score, group_rank)
                link(nc.vector.tensor_scalar(group_rank, group_rank, 1.0, None, ALU.is_lt))
                tt(sel.rearrange("p i (g e) -> p i g e", e=EPG), sel.rearrange("p i (g e) -> p i g e", e=EPG),
                   group_rank.unsqueeze(3).to_broadcast([P, NT, NE_GRP, EPG]), ALU.mult).then_inc(routed[layer], 1)
                dve.wait_ge(routed[layer], 1)
                link(tt(tmp, sel, s, ALU.mult))
                link(nc.vector.tensor_reduce(best.rearrange("p i o -> p (i o)"), tmp, AX.X, ALU.add))
                link(nc.vector.reciprocal(inverse, best))
                link(tt(moeg[:, :, :], tmp, inverse.to_broadcast([P, NT, N_EXP]), ALU.mult))

                j, = stage[f"place{layer}"]
                arrived(j)
                counts = bank(j)[:, NT * N_EXP:2 * NT * N_EXP].rearrange("p (i e) -> p i e", i=NT)
                base = rt[:, 8, :, :]
                total = rt[:, 9, 0:1, :]
                link(nc.vector.memset(base[:, 0:1, :], 1.0))
                for i in range(1, NT):
                    link(tt(base[:, i:i + 1, :], base[:, i - 1:i, :], counts[:, i - 1:i, :], ALU.add))
                link(tt(total, base[:, NT - 1:NT, :], counts[:, NT - 1:NT, :], ALU.add))
                tt(place[:, :, :], base, bank(j)[:, 0:NT * N_EXP].rearrange("p (i e) -> p i e", i=NT),
                   ALU.add).then_inc(evac["D"], 1)
                dve.wait_ge(evac["D"], nth[j])
                link(tt(place[:, :, :], place[:, :, :], sel, ALU.mult))
                link(nc.vector.tensor_scalar(place[:, :, :], place[:, :, :], -1.0, None, ALU.add))

                number = tcol[:, :].unsqueeze(2).to_broadcast([P, NT, N_EXP])
                link(tt(tmp, number, number, ALU.add))
                link(tt(routes[:, :, :, 1], tmp, rank, ALU.add))
                link(nc.vector.tensor_copy(routes[:, :, :, 0], number))
                link(nc.vector.memset(routes[:, :, :, 2], 1.0))
                link(nc.vector.tensor_copy(routes[:, :, :, 3], moeg[:, :, :]))
                link(tt(tmp, moeg[:, :, :], routes[:, :, :, 3], ALU.subtract))
                link(nc.vector.tensor_scalar(tmp, tmp, 2048.0, None, ALU.mult))
                link(nc.vector.tensor_copy(routes[:, :, :, 4], tmp))
                link(tt(tmp, tmp, routes[:, :, :, 4], ALU.subtract))
                link(nc.vector.tensor_scalar(routes[:, :, :, 5], tmp, 2048.0, None, ALU.mult))

                def one_hot(e):
                    return tt(onehot[:, e, :, :], row[:, :].unsqueeze(1).to_broadcast([P, NT, P]),
                              place[:, :, e].unsqueeze(2).to_broadcast([P, NT, P]), ALU.is_equal)

                def collect(q):
                    j = stage[f"slots{layer}"][q]
                    es = ROUTED_FIRST[q]
                    n = es.stop - es.start
                    arrived(j)
                    raw = rt[:, 10:12, :, :].rearrange("p s i e -> p (s i e)")[:, 0:ROUTE * n].rearrange(
                        "p (e c) -> p e c", c=ROUTE)
                    nowhere = rt[:, 9, 0, 0:n]
                    nc.vector.tensor_copy(raw, bank(j)[:, es.start * ROUTE:es.stop * ROUTE].rearrange(
                        "p (e c) -> p e c", c=ROUTE)).then_inc(evac["D"], 1)
                    dve.wait_ge(evac["D"], nth[j])
                    link(nc.vector.tensor_scalar(nowhere, raw[:, :, 2], -NOWHERE, NOWHERE, ALU.mult, ALU.add))
                    link(tt(slot_rows[:, 0, es], raw[:, :, 0], nowhere, ALU.add))
                    link(tt(slot_rows[:, 1, es], raw[:, :, 1], nowhere, ALU.add))
                    link(nc.vector.scalar_tensor_tensor(raw[:, :, 4], raw[:, :, 5], 2.0 ** -11, raw[:, :, 4],
                                                        ALU.mult, ALU.add))
                    nc.vector.scalar_tensor_tensor(by_slot[:, es, 3], raw[:, :, 4], 2.0 ** -11, raw[:, :, 3],
                                                   ALU.mult, ALU.add).then_inc(slots_ready[layer], 1)
                    dve.wait_ge(slots_ready[layer], q + 1)

                for q, es in enumerate(ROUTED_FIRST):
                    for e in range(N_EXP)[es]:
                        if e == EPG + 2:
                            collect(0)
                        last = one_hot(e)
                    last.then_inc(onehot_ready[layer], 1)
                link(nc.vector.tensor_reduce(more[:, 0:1], total.rearrange("p o e -> p (o e)"), AX.X, ALU.max))
                link(nc.vector.tensor_scalar(many[:, layer:layer + 1], more[:, 0:1], float(P + 1), None, ALU.is_gt))
                collect(1)

            def experts(layer):
                S = M[layer]

                def tokens_in(r, n):
                    dve.wait_ge(S["xturn"], PRIMED + r * SLOTS + n + 1)
                    for k in range(4, KD):
                        last = nc.vector.tensor_scalar(XgT[:, n % 2, k, :], ps[1][:, (k - 4) * P:(k - 3) * P],
                                                       adaC[:, layer, 3, k:k + 1], adaC[:, layer, 2, k:k + 1],
                                                       ALU.mult, ALU.add)
                    last.then_inc(S["xdve"], 1)

                def hidden(r, n):
                    v = r * SLOTS + n
                    dve.wait_ge(S["silu"], PRIMED + v + 1)
                    if not isinstance(v, int) or v >= 2:
                        dve.wait_ge(S["hturn"], PRIMED + v - 1)
                    nc.vector.tensor_tensor(hmid[:, n % 2, :], silu[:, n % 2, :], ps[2 + n % 2][:, D_EXP:2 * D_EXP],
                                            ALU.mult).then_inc(S["hmid"], 1)

                def step(r, n):
                    v = r * SLOTS + n
                    if not isinstance(r, int) or v + 1 < N_EXP:
                        hidden(r, n + 1)
                    if not isinstance(r, int) or v + 2 < N_EXP:
                        tokens_in(r, n + 2)
                    dve.wait_ge(S["down"], PRIMED + v + 1)
                    dve.wait_ge(S["yfree"], PRIMED + v)
                    apart(dve)
                    for h in range(2):
                        last = nc.vector.scalar_tensor_tensor(
                            Y[:, n % 2, h * 512:(h + 1) * 512], ps[6 + h][:, :],
                            by_slot[:, bass.ds(v, 1), 3:4].rearrange("p o c -> p (o c)"),
                            G[:, layer, 1, h * 512:(h + 1) * 512], ALU.mult, ALU.mult)
                    last.then_inc(S["ydve"], 1)

                tokens_in(0, 0)
                hidden(0, 0)
                tokens_in(0, 1)
                with dve.Fori(0, ROUNDS - 1) as r:
                    for n in range(SLOTS):
                        step(r, n)
                for n in range(SLOTS):
                    step(ROUNDS - 1, n)
                flag = dve.value_load(many[0:1, layer:layer + 1], min_val=0, max_val=1)
                with dve.If(flag == 1):
                    more_tokens(layer)
                n = 2 * layer + 1
                for i in range(NT):
                    dve.wait_ge(answers_in[i], 32 * (layer + 1))
                    if i:
                        dve.wait_ge(answers_sum, (NT - 1) * layer + i)
                    link(nc.vector.scalar_tensor_tensor(X[:, i, :], X[:, i, :], ALPHA, O[:, i, :], ALU.mult, ALU.add))
                    if i == 0:
                        link(nc.vector.tensor_tensor(X[:, i, :], X[:, i, :], Y1[:, i, :], ALU.add))
                    for b in range(2):
                        link(nc.vector.bn_stats(stats[:, i, b, :], X[:, i, b * 512:(b + 1) * 512]))
                    norm_stats(n, i)
                    norm_apply(n, i)

            def more_tokens(layer):
                S = FURTHER[layer]
                step = more_step[layer]
                with dve.Fori(0, N_EXP) as e:
                    for b in range(3):
                        v = PRIMED + e * 3 + b
                        m = e * 15 + 5 * b
                        dve.wait_ge(S["free"], v)
                        nc.vector.tensor_scalar(more[:, 0:NT], place[:, :, bass.ds(e, 1)].rearrange("p i o -> p (i o)"),
                                                float(-P * (b + 1)), None, ALU.add).then_inc(step, 1)
                        dve.wait_ge(step, m + 1)
                        nc.vector.tensor_tensor(onehot[:, 0, :, :], row[:, :].unsqueeze(1).to_broadcast([P, NT, P]),
                                                more[:, 0:NT].unsqueeze(2).to_broadcast([P, NT, P]),
                                                ALU.is_equal).then_inc(S["onehot"], 1)
                        dve.wait_ge(S["slots"], v + 1)
                        nc.vector.tensor_copy(more[:, 0:ROUTE], ps[5][:, 0:ROUTE]).then_inc(step, 1)
                        dve.wait_ge(step, m + 2)
                        nc.vector.tensor_scalar(more[:, 6:7], more[:, 2:3], -NOWHERE, NOWHERE, ALU.mult, ALU.add)\
                            .then_inc(step, 1)
                        dve.wait_ge(step, m + 3)
                        nc.vector.scalar_tensor_tensor(more[:, 4:5], more[:, 5:6], 2.0 ** -11, more[:, 4:5],
                                                       ALU.mult, ALU.add).then_inc(step, 1)
                        dve.wait_ge(step, m + 4)
                        nc.vector.scalar_tensor_tensor(more[:, 3:4], more[:, 4:5], 2.0 ** -11, more[:, 3:4],
                                                       ALU.mult, ALU.add).then_inc(step, 1)
                        dve.wait_ge(step, m + 5)
                        nc.vector.tensor_tensor(more_rows[:, :], more[:, 0:2], more[:, 6:7].to_broadcast([P, 2]), ALU.add)\
                            .then_inc(S["rows"], 1)
                        dve.wait_ge(S["silu"], v + 1)
                        nc.vector.tensor_tensor(hmid[:, 0, :], silu[:, 0, :], ps[2][:, D_EXP:2 * D_EXP], ALU.mult)\
                            .then_inc(S["hmid"], 1)
                        dve.wait_ge(S["down"], v + 1)
                        for h in range(2):
                            last = nc.vector.scalar_tensor_tensor(
                                Y[:, 0, h * 512:(h + 1) * 512], ps[6 + h][:, :], more[:, 3:4],
                                G[:, layer, 1, h * 512:(h + 1) * 512], ALU.mult, ALU.mult)
                        last.then_inc(S["y"], 1)
                dve.wait_ge(S["scatter"], 16 * 3 * N_EXP)

            dve.wait_ge(consts, 4)
            wait_evacuated(dve, "glT")
            dve.wait_ge(acc_bias, 32)
            attention(0, 0, NG // 2, late=0)
            dve.wait_ge(acc_bias, 48)
            attention(0, NG // 2, NG, late=1)
            ada_columns("rest", 0, (2, 3))
            output(0)
            route(0)
            experts(0)
            for i in range(NT):
                (_, j), = mine(f"xT1.{i}")
                arrived(j)
                nc.vector.tensor_copy(XTk[:, 4:8, i * P:(i + 1) * P],
                                      bank(j)[:, :].rearrange("p (k t) -> p k t", k=4)).then_inc(evac["D"], 1)
            wait_evacuated(dve, f"xT1.{NT - 1}")
            for k in range(KD):
                nc.vector.tensor_scalar(HT[:, k, :], XTk[:, k, :], adaC[:, 1, 1, k:k + 1], adaC[:, 1, 0, k:k + 1],
                                        ALU.mult, ALU.add).then_inc(hT1_ready, 1)
            keys_values("kv", 0)
            attention(1)
            output(1)
            route(1)
            experts(1)


def win_gates(t):
    return t["nsa_w_in"][0][:, QW + 6 * KVW:NSA_IN].rearrange("(k p) n -> p k n", p=P)


def split_halves(copy, dst, m, src):
    for half in range(2):
        for odd in range(2):
            last = copy(dst[odd * HD:(odd + 1) * HD, 2 * m + half, :], src[half * HD:(half + 1) * HD, odd::2])
    return last


_INS = ["x", "c", "nsa_w_in", "cmp_k_w1", "cmp_k_w2", "cmp_v_w1", "cmp_v_w2", "cmp_k_pos", "cmp_v_pos", "nsa_w_out",
        "swa_w_q", "swa_sinks", "swa_w_out", "shared_w_kv", "rel_bias", "router_w", "router_b", "moe_w_gate",
        "moe_w_up", "moe_w_down", "ada_w", "ada_b", "ln_g", "ln_b"]


def kernel(**inputs):
    import concourse.bacc as bacc
    from concourse.bass_utils import run_bass_kernel_spmd

    nc = bacc.Bacc("TRN2", target_bir_lowering=False, num_devices=1)
    arrays, tensors = {}, {}
    for name, a in [(n, np.ascontiguousarray(inputs[n])) for n in _INS] + [("buckets", bucket_rows())]:
        arrays[f"in_{name}"] = a
        tensors[name] = nc.dram_tensor(f"in_{name}", a.shape, F32, kind="ExternalInput").ap()
    tensors["out"] = nc.dram_tensor("out", (1, T, D), F32, kind="ExternalOutput").ap()
    build(nc, tensors)
    r = run_bass_kernel_spmd(nc, [arrays], core_ids=[0])
    return r.results[0]["out"]
```
